# Optimizing a Trainium2 kernel written in Bass

```python
import math
import jax
import jax.numpy as jnp
from jax import lax
import numpy as np

D_MODEL = 1024
BATCH = 1
SEQ = 256
DEPTH = 2

GRID_W = 64
CTX_LEN = 256
HEAD_DIM = 64
N_SLOTS = D_MODEL // HEAD_DIM
CONV_CH = D_MODEL // 2
CONV_W = 3
NA_HEADS = N_SLOTS // 2
NA_ROWS = 8
NA_COLS = 16
SWA_HEADS = N_SLOTS // 2
SWA_KV_HEADS = max(1, SWA_HEADS // 4)
SWA_WINDOW = 128
BLOCK = 128
DIFF_HEADS = N_SLOTS // 4
D_FF = 256 * math.ceil(8 * D_MODEL / 3 / 256)
N_EXPERTS = 8
TOP_K = 2
D_FF_EXPERT = D_FF // 2
ROPE_THETA = 10000.0
EPS = 1e-6
NEG = -1e30
N_EVEN = (DEPTH + 1) // 2
N_ODD = DEPTH // 2
NA_W = NA_HEADS * HEAD_DIM
EV_Q = 3 * CONV_CH + NA_W
EV_KV = 2 * NA_W
EV_OUT = CONV_CH + NA_W
C_Q = SWA_HEADS * HEAD_DIM
C_KV = SWA_KV_HEADS * HEAD_DIM
D_QK = DIFF_HEADS * 2 * HEAD_DIM
D_V = DIFF_HEADS * 2 * HEAD_DIM
OD_Q = C_Q + D_QK
OD_KV = 2 * C_KV + D_QK + D_V
OD_OUT = C_Q + D_V


def rms_norm(x, g):
    xf = x.astype(jnp.float32)
    y = xf * lax.rsqrt(jnp.mean(xf * xf, -1, keepdims=True) + EPS)
    return (y * g.astype(jnp.float32)).astype(x.dtype)

def split_heads(t, h):
    b, n, _ = t.shape
    return t.reshape(b, n, h, -1).transpose(0, 2, 1, 3)

def merge_heads(t):
    b, h, n, d = t.shape
    return t.transpose(0, 2, 1, 3).reshape(b, n, h * d)

def rope_tables(n):
    t = jnp.arange(n)
    pos = jnp.stack([t // GRID_W, t % GRID_W], -1).astype(jnp.float32)
    nq = HEAD_DIM // 4
    inv = ROPE_THETA ** (-jnp.arange(nq, dtype=jnp.float32) / nq)
    ang = pos[:, :, None] * inv
    return jnp.cos(ang), jnp.sin(ang)

def apply_rope(x, cos, sin):
    shp = x.shape
    xr = x.reshape(shp[:-1] + (2, 2, HEAD_DIM // 4))
    a, b = xr[..., 0, :], xr[..., 1, :]
    cos = cos.astype(x.dtype)
    sin = sin.astype(x.dtype)
    return jnp.stack([a * cos - b * sin, b * cos + a * sin], -2).reshape(shp)

def joint_softmax(parts, extra=None):
    m = parts[0].max(-1, keepdims=True)
    for p in parts[1:]:
        m = jnp.maximum(m, p.max(-1, keepdims=True))
    if extra is not None:
        m = jnp.maximum(m, extra)
    es = [jnp.exp(p - m) for p in parts]
    den = es[0].sum(-1, keepdims=True)
    for e in es[1:]:
        den = den + e.sum(-1, keepdims=True)
    if extra is not None:
        den = den + jnp.exp(extra - m)
    return [e / den for e in es]

def dense_attention(q, k, v, sink=None):
    b, hq, lq, d = q.shape
    hkv = k.shape[1]
    g = hq // hkv
    qg = q.reshape(b, hkv, g, lq, d)
    s = jnp.einsum('bkgqd,bkld->bkgql', qg, k, preferred_element_type=jnp.float32) * d ** -0.5
    extra = None if sink is None else sink.astype(jnp.float32).reshape(1, hkv, g, 1, 1)
    (p,) = joint_softmax([s], extra)
    o = jnp.einsum('bkgql,bkld->bkgqd', p.astype(v.dtype), v)
    return o.reshape(b, hq, lq, d)

def dwconv3(u, w):
    return lax.conv_general_dilated(u, w[:, None, :].astype(u.dtype), window_strides=(1,),
                                    padding=[(1, 1)], dimension_numbers=('NWC', 'WIO', 'NWC'),
                                    feature_group_count=u.shape[-1])

def neighbourhood_attention(q, k, v, k_ctx, v_ctx, rpb):
    b, h, n, d = q.shape
    rows = n // GRID_W
    kh = min(NA_ROWS, rows)
    r = jnp.arange(rows)
    col = jnp.arange(GRID_W)
    r0 = jnp.clip(r - kh // 2, 0, rows - kh)
    row_idx = r0[:, None] + jnp.arange(kh)[None, :]
    c0 = jnp.clip(col - NA_COLS // 2, 0, GRID_W - NA_COLS)
    qg = q.reshape(b, h, rows, GRID_W, d)
    kg = k.reshape(b, h, rows, GRID_W, d)[:, :, row_idx]
    vg = v.reshape(b, h, rows, GRID_W, d)[:, :, row_idx]
    dr = row_idx - r[:, None] + NA_ROWS - 1
    dc = jnp.clip(col[None, :] - col[:, None] + NA_COLS - 1, 0, 2 * NA_COLS - 2)
    col_ok = (col[None, :] >= c0[:, None]) & (col[None, :] < c0[:, None] + NA_COLS)
    bias = rpb.astype(jnp.float32)[:, dr[:, None, :, None], dc[None, :, None, :]]
    bias = jnp.where(col_ok[None, None, :, None, :], bias, NEG)
    scale = d ** -0.5
    s_loc = jnp.einsum('bhrqd,bhrjkd->bhrqjk', qg, kg, preferred_element_type=jnp.float32) * scale + bias
    s_ctx = jnp.einsum('bhrqd,bhld->bhrql', qg, k_ctx, preferred_element_type=jnp.float32) * scale
    p_loc, p_ctx = joint_softmax([s_loc.reshape(b, h, rows, GRID_W, kh * GRID_W), s_ctx])
    p_loc = p_loc.reshape(b, h, rows, GRID_W, kh, GRID_W).astype(v.dtype)
    o = (jnp.einsum('bhrqjk,bhrjkd->bhrqd', p_loc, vg)
         + jnp.einsum('bhrql,bhld->bhrqd', p_ctx.astype(v.dtype), v_ctx))
    return o.reshape(b, h, n, d)

def window_gqa(q, k, v, k_ctx, v_ctx, sink):
    b, hq, n, d = q.shape
    hkv = k.shape[1]
    g = hq // hkv
    nb = n // BLOCK
    qb = q.reshape(b, hkv, g, nb, BLOCK, d)
    pad = ((0, 0), (0, 0), (BLOCK, BLOCK), (0, 0))
    band = (jnp.arange(nb) * BLOCK)[:, None] + jnp.arange(3 * BLOCK)[None, :]
    kb = jnp.pad(k, pad)[:, :, band]
    vb = jnp.pad(v, pad)[:, :, band]
    qpos = (jnp.arange(nb) * BLOCK)[:, None, None] + jnp.arange(BLOCK)[None, :, None]
    kpos = band[:, None, :] - BLOCK
    ok = (jnp.abs(kpos - qpos) <= SWA_WINDOW) & (kpos >= 0) & (kpos < n)
    scale = d ** -0.5
    s_loc = jnp.where(ok, jnp.einsum('bkgnqd,bknmd->bkgnqm', qb, kb, preferred_element_type=jnp.float32) * scale, NEG)
    s_ctx = jnp.einsum('bkgnqd,bkld->bkgnql', qb, k_ctx, preferred_element_type=jnp.float32) * scale
    extra = sink.astype(jnp.float32).reshape(1, hkv, g, 1, 1, 1)
    p_loc, p_ctx = joint_softmax([s_loc, s_ctx], extra)
    o = (jnp.einsum('bkgnqm,bknmd->bkgnqd', p_loc.astype(v.dtype), vb)
         + jnp.einsum('bkgnql,bkld->bkgnqd', p_ctx.astype(v.dtype), v_ctx))
    return o.reshape(b, hq, n, d)

def diff_attend(q, kvs, lam):
    scale = q.shape[-1] ** -0.5
    ss = [jnp.einsum('bhiqd,bhikd->bhiqk', q, k, preferred_element_type=jnp.float32) * scale for k, _ in kvs]
    ps = joint_softmax(ss)
    out = None
    for p, (_, v) in zip(ps, kvs):
        a = (p[:, :, 0] - lam * p[:, :, 1]).astype(v.dtype)
        o = jnp.einsum('bhqk,bhkd->bhqd', a, v)
        out = o if out is None else out + o
    return out

def diff_attention_latent(q, k, v, k_ctx, v_ctx, lam):
    b, h, _, n, d = q.shape
    nb = n // BLOCK
    qb = jnp.moveaxis(q.reshape(b, h, 2, nb, BLOCK, d), 3, 0)
    o = lax.map(lambda qi: diff_attend(qi, [(k, v), (k_ctx, v_ctx)], lam), qb)
    return jnp.moveaxis(o, 0, 2).reshape(b, h, n, v.shape[-1])

def swiglu(x, w1, w3, w2):
    return (jax.nn.silu(x @ w1) * (x @ w3)) @ w2

def moe_swiglu(x, router, w1, w3, w2):
    shp = x.shape
    xt = x.reshape(-1, shp[-1])
    logits = (xt @ router).astype(jnp.float32)
    top_v, top_i = lax.top_k(logits, TOP_K)
    top_w = jax.nn.softmax(top_v, axis=-1)
    gates = jnp.sum(jax.nn.one_hot(top_i, N_EXPERTS, dtype=jnp.float32) * top_w[..., None], axis=1)
    gates = gates.astype(x.dtype)
    out = gates[:, 0:1] * swiglu(xt, w1[0], w3[0], w2[0])
    for e in range(1, N_EXPERTS):
        out = out + gates[:, e:e + 1] * swiglu(xt, w1[e], w3[e], w2[e])
    return out.reshape(shp)

def even_mixer(h_lat, h_ctx, w_in, conv_w, q_g, k_g, rpb, w_out, need_ctx):
    def query_side(p):
        gb, gc, u, q = jnp.split(p, [CONV_CH, 2 * CONV_CH, 3 * CONV_CH], -1)
        y_conv = gb * dwconv3(gc * u, conv_w)
        return y_conv, rms_norm(split_heads(q, NA_HEADS), q_g)

    def kv_side(p):
        k, v = jnp.split(p, 2, -1)
        return rms_norm(split_heads(k, NA_HEADS), k_g), split_heads(v, NA_HEADS)

    p_lat = h_lat @ w_in
    yc_lat, q_lat = query_side(p_lat[..., :EV_Q])
    k_lat, v_lat = kv_side(p_lat[..., EV_Q:])
    p_ctx = h_ctx @ (w_in if need_ctx else w_in[:, EV_Q:])
    k_ctx, v_ctx = kv_side(p_ctx[..., -EV_KV:])
    y_na = merge_heads(neighbourhood_attention(q_lat, k_lat, v_lat, k_ctx, v_ctx, rpb))
    y_lat = jnp.concatenate([yc_lat, y_na], -1) @ w_out
    y_ctx = None
    if need_ctx:
        yc_ctx, q_ctx = query_side(p_ctx[..., :EV_Q])
        y_na_ctx = merge_heads(dense_attention(q_ctx, k_ctx, v_ctx))
        y_ctx = jnp.concatenate([yc_ctx, y_na_ctx], -1) @ w_out
    return y_lat, y_ctx

def odd_mixer(h_lat, h_ctx, w_in, cq_g, ck_g, sink, dq_g, dk_g, lam_q1, lam_k1, lam_q2, lam_k2,
              subln_g, w_out, lam_init, cos, sin, need_ctx):
    def diff_split(t):
        b, n, _ = t.shape
        return t.reshape(b, n, DIFF_HEADS, 2, HEAD_DIM).transpose(0, 2, 3, 1, 4)

    def query_side(p, rope):
        cq, dq = jnp.split(p, [C_Q], -1)
        cq = rms_norm(split_heads(cq, SWA_HEADS), cq_g)
        dq = rms_norm(diff_split(dq), dq_g)
        if rope:
            cq, dq = apply_rope(cq, cos, sin), apply_rope(dq, cos, sin)
        return cq, dq

    def kv_side(p, rope):
        ck, cv, dk, dv = jnp.split(p, [C_KV, 2 * C_KV, 2 * C_KV + D_QK], -1)
        ck = rms_norm(split_heads(ck, SWA_KV_HEADS), ck_g)
        dk = rms_norm(diff_split(dk), dk_g)
        if rope:
            ck, dk = apply_rope(ck, cos, sin), apply_rope(dk, cos, sin)
        return ck, split_heads(cv, SWA_KV_HEADS), dk, split_heads(dv, DIFF_HEADS)

    f32 = jnp.float32
    lam = (jnp.exp(jnp.sum(lam_q1.astype(f32) * lam_k1.astype(f32)))
           - jnp.exp(jnp.sum(lam_q2.astype(f32) * lam_k2.astype(f32))) + lam_init)

    def merge(yc, yd):
        yd = rms_norm(yd, subln_g) * (1.0 - lam_init)
        return jnp.concatenate([merge_heads(yc), merge_heads(yd)], -1) @ w_out

    p_lat = h_lat @ w_in
    cq_l, dq_l = query_side(p_lat[..., :OD_Q], True)
    ck_l, cv_l, dk_l, dv_l = kv_side(p_lat[..., OD_Q:], True)
    p_ctx = h_ctx @ (w_in if need_ctx else w_in[:, OD_Q:])
    ck_c, cv_c, dk_c, dv_c = kv_side(p_ctx[..., -OD_KV:], False)
    y_lat = merge(window_gqa(cq_l, ck_l, cv_l, ck_c, cv_c, sink),
                  diff_attention_latent(dq_l, dk_l, dv_l, dk_c, dv_c, lam))
    y_ctx = None
    if need_ctx:
        cq_c, dq_c = query_side(p_ctx[..., :OD_Q], False)
        y_ctx = merge(dense_attention(cq_c, ck_c, cv_c, sink), diff_attend(dq_c, [(dk_c, dv_c)], lam))
    return y_lat, y_ctx

def first_inputs(seed: int = 0) -> dict:
    key = jax.random.key(seed)
    ks = iter(jax.random.split(key, 40))
    D = D_MODEL

    def nrm(shape, scale=1.0):
        return jax.random.normal(next(ks), shape, jnp.float32) * scale

    def gain(shape):
        return 1.0 + nrm(shape, 0.05)

    return {
        'x': nrm((BATCH, SEQ, D)),
        'c': nrm((BATCH, D)),
        'ctx': nrm((BATCH, CTX_LEN, D)),
        'c_ctx': nrm((D,)),
        'ada_w': nrm((DEPTH, D, 6 * D), 0.5 * D ** -0.5),
        'ada_b': nrm((DEPTH, 6 * D), 0.02),
        'norm1_g': gain((DEPTH, D)),
        'norm2_g': gain((DEPTH, D)),
        'ev_w_in': nrm((N_EVEN, D, EV_Q + EV_KV), D ** -0.5),
        'ev_conv_w': nrm((N_EVEN, CONV_W, CONV_CH), CONV_W ** -0.5),
        'ev_q_g': gain((N_EVEN, HEAD_DIM)),
        'ev_k_g': gain((N_EVEN, HEAD_DIM)),
        'ev_rpb': nrm((N_EVEN, NA_HEADS, 2 * NA_ROWS - 1, 2 * NA_COLS - 1), 0.1),
        'ev_w_out': nrm((N_EVEN, EV_OUT, D), EV_OUT ** -0.5),
        'ffn_w1': nrm((N_EVEN, D, D_FF), D ** -0.5),
        'ffn_w3': nrm((N_EVEN, D, D_FF), D ** -0.5),
        'ffn_w2': nrm((N_EVEN, D_FF, D), D_FF ** -0.5),
        'od_w_in': nrm((N_ODD, D, OD_Q + OD_KV), D ** -0.5),
        'od_cq_g': gain((N_ODD, HEAD_DIM)),
        'od_ck_g': gain((N_ODD, HEAD_DIM)),
        'od_sink': nrm((N_ODD, SWA_HEADS), 0.5),
        'od_dq_g': gain((N_ODD, HEAD_DIM)),
        'od_dk_g': gain((N_ODD, HEAD_DIM)),
        'od_lam_q1': nrm((N_ODD, HEAD_DIM), 0.1),
        'od_lam_k1': nrm((N_ODD, HEAD_DIM), 0.1),
        'od_lam_q2': nrm((N_ODD, HEAD_DIM), 0.1),
        'od_lam_k2': nrm((N_ODD, HEAD_DIM), 0.1),
        'od_subln_g': gain((N_ODD, 2 * HEAD_DIM)),
        'od_w_out': nrm((N_ODD, OD_OUT, D), OD_OUT ** -0.5),
        'moe_router': nrm((N_ODD, D, N_EXPERTS), D ** -0.5),
        'moe_w1': nrm((N_ODD, N_EXPERTS, D, D_FF_EXPERT), D ** -0.5),
        'moe_w3': nrm((N_ODD, N_EXPERTS, D, D_FF_EXPERT), D ** -0.5),
        'moe_w2': nrm((N_ODD, N_EXPERTS, D_FF_EXPERT, D), D_FF_EXPERT ** -0.5),
    }

def first_block(x, c, ctx, c_ctx, ada_w, ada_b, norm1_g, norm2_g, ev_w_in, ev_conv_w, ev_q_g, ev_k_g,
              ev_rpb, ev_w_out, ffn_w1, ffn_w3, ffn_w2, od_w_in, od_cq_g, od_ck_g, od_sink, od_dq_g,
              od_dk_g, od_lam_q1, od_lam_k1, od_lam_q2, od_lam_k2, od_subln_g, od_w_out, moe_router,
              moe_w1, moe_w3, moe_w2):
    n = x.shape[1]
    cos, sin = rope_tables(n)
    h, hc = x, ctx
    s_lat = jax.nn.silu(c)
    s_ctx = jax.nn.silu(c_ctx)
    for l in range(DEPTH):
        last = l == DEPTH - 1
        i = l // 2
        mod = (s_lat @ ada_w[l] + ada_b[l])[:, None, :]
        sh1, sc1, g1, sh2, sc2, g2 = jnp.split(mod, 6, -1)
        n_mod = 2 if last else 6
        modc = jnp.split(s_ctx @ ada_w[l][:, :n_mod * D_MODEL] + ada_b[l][:n_mod * D_MODEL], n_mod)
        a_lat = rms_norm(h, norm1_g[l]) * (1 + sc1) + sh1
        a_ctx = rms_norm(hc, norm1_g[l]) * (1 + modc[1]) + modc[0]
        if l % 2 == 0:
            y, yc = even_mixer(a_lat, a_ctx, ev_w_in[i], ev_conv_w[i], ev_q_g[i], ev_k_g[i], ev_rpb[i],
                               ev_w_out[i], not last)
            ffn = lambda t: swiglu(t, ffn_w1[i], ffn_w3[i], ffn_w2[i])
        else:
            lam_init = 0.8 - 0.6 * math.exp(-0.3 * l)
            y, yc = odd_mixer(a_lat, a_ctx, od_w_in[i], od_cq_g[i], od_ck_g[i], od_sink[i], od_dq_g[i],
                              od_dk_g[i], od_lam_q1[i], od_lam_k1[i], od_lam_q2[i], od_lam_k2[i],
                              od_subln_g[i], od_w_out[i], lam_init, cos, sin, not last)
            ffn = lambda t: moe_swiglu(t, moe_router[i], moe_w1[i], moe_w3[i], moe_w2[i])
        h = h + g1 * y
        h = h + g2 * ffn(rms_norm(h, norm2_g[l]) * (1 + sc2) + sh2)
        if not last:
            hc = hc + modc[2] * yc
            hc = hc + modc[5] * ffn(rms_norm(hc, norm2_g[l]) * (1 + modc[4]) + modc[3])
    return h


NORM_EPS = 1e-6
D_FF_2 = 2816
CONV_CH_2 = 1024
CONV_WIDTH = 31
SSM_D_INNER = 1024
SSM_HEAD_DIM = 64
SSM_HEADS = SSM_D_INNER // SSM_HEAD_DIM
SSM_GROUPS = 2
SSM_STATE = 128
SSM_CONV_WIDTH = 4
SSM_CHUNK = 128
SSM_XBC = SSM_D_INNER + 2 * SSM_GROUPS * SSM_STATE
HYB_IN_COLS = 2 * CONV_CH_2 + SSM_D_INNER + SSM_XBC + SSM_HEADS
HYB_MIX_WIDTH = CONV_CH_2 + SSM_D_INNER
ATTN_HEAD_DIM = 64
ATTN_HEADS = 8
DILATED_PATTERNS = ((128, 1), (512, 4), (2048, 16))
ATTN_GROUPS = len(DILATED_PATTERNS)
ATTN_BLOCK = 128
ATTN_QKV_COLS = 3 * ATTN_GROUPS * ATTN_HEADS * ATTN_HEAD_DIM
ATTN_OUT_WIDTH = ATTN_HEADS * ATTN_HEAD_DIM
N_EVEN_2 = (DEPTH + 1) // 2
N_ODD_2 = DEPTH // 2


def rms_norm_2(x, g):
    xf = x.astype(jnp.float32)
    y = xf * lax.rsqrt(jnp.mean(xf * xf, axis=-1, keepdims=True) + NORM_EPS)
    return (y * g.astype(jnp.float32)).astype(x.dtype)

def layer_norm(x, g, b):
    xf = x.astype(jnp.float32)
    xc = xf - jnp.mean(xf, axis=-1, keepdims=True)
    y = xc * lax.rsqrt(jnp.mean(xc * xc, axis=-1, keepdims=True) + NORM_EPS)
    return (y * g.astype(jnp.float32) + b.astype(jnp.float32)).astype(x.dtype)

def swiglu_2(u, w1, w2):
    gate, up = jnp.split(u @ w1, 2, axis=-1)
    return (jax.nn.silu(gate) * up) @ w2

def causal_depthwise_conv(x, w, b):
    k = w.shape[0]
    y = lax.conv_general_dilated(x, w[:, None, :].astype(x.dtype), window_strides=(1,), padding=[(k - 1, 0)], dimension_numbers=('NWC', 'WIO', 'NWC'), feature_group_count=x.shape[-1])
    return y + b.astype(x.dtype)

def conformer_conv(u, w_dw, b_dw, ln_g, ln_b):
    val, gate = jnp.split(u, 2, axis=-1)
    hid = causal_depthwise_conv(val * jax.nn.sigmoid(gate), w_dw, b_dw)
    return jax.nn.silu(layer_norm(hid, ln_g, ln_b))

def segsum(a):
    t = a.shape[-1]
    strict = jnp.tril(jnp.ones((t, t), dtype=bool), -1)
    incl = jnp.tril(jnp.ones((t, t), dtype=bool), 0)
    ss = jnp.cumsum(jnp.where(strict, a[..., :, None], 0.0), axis=-2)
    return jnp.where(incl, ss, -jnp.inf)

def ssd_chunked(x, a, bm, cm):
    bsz, seq, heads, hd = x.shape
    groups, nst = bm.shape[2], bm.shape[3]
    rep = heads // groups
    nc = seq // SSM_CHUNK
    x = x.reshape(bsz, nc, SSM_CHUNK, groups, rep, hd)
    a = a.reshape(bsz, nc, SSM_CHUNK, groups, rep).transpose(0, 3, 4, 1, 2)
    bm = bm.reshape(bsz, nc, SSM_CHUNK, groups, nst)
    cm = cm.reshape(bsz, nc, SSM_CHUNK, groups, nst)
    a_cum = jnp.cumsum(a, axis=-1)
    decay_in = jnp.exp(segsum(a))
    cb = jnp.einsum('bclgn,bcsgn->bgcls', cm, bm)
    y_diag = jnp.einsum('bgrcls,bcsgrp->bclgrp', cb[:, :, None] * decay_in, x)
    decay_states = jnp.exp(a_cum[..., -1:] - a_cum)
    states = jnp.einsum('bcsgn,bgrcs,bcsgrp->bcgrpn', bm, decay_states, x)
    states = jnp.concatenate([jnp.zeros_like(states[:, :1]), states], axis=1)
    chunk_tot = jnp.pad(a_cum[..., -1], ((0, 0), (0, 0), (0, 0), (1, 0)))
    decay_chunk = jnp.exp(segsum(chunk_tot))
    states = jnp.einsum('bgrzc,bcgrpn->bzgrpn', decay_chunk, states)[:, :-1]
    y_off = jnp.einsum('bclgn,bcgrpn,bgrcl->bclgrp', cm, states, jnp.exp(a_cum))
    return (y_diag + y_off).reshape(bsz, seq, heads, hd)

def mamba2_ssd(z, xbc, dt_raw, conv_w, conv_b, dt_bias, a_log, d_skip, norm_g):
    bsz, seq, _ = z.shape
    xbc = jax.nn.silu(causal_depthwise_conv(xbc, conv_w, conv_b)).astype(jnp.float32)
    xs, bm, cm = jnp.split(xbc, [SSM_D_INNER, SSM_D_INNER + SSM_GROUPS * SSM_STATE], axis=-1)
    xs = xs.reshape(bsz, seq, SSM_HEADS, SSM_HEAD_DIM)
    bm = bm.reshape(bsz, seq, SSM_GROUPS, SSM_STATE)
    cm = cm.reshape(bsz, seq, SSM_GROUPS, SSM_STATE)
    dt = jax.nn.softplus(dt_raw.astype(jnp.float32) + dt_bias.astype(jnp.float32))
    a = -jnp.exp(a_log.astype(jnp.float32))
    y = ssd_chunked(xs * dt[..., None], dt * a, bm, cm) + d_skip.astype(jnp.float32)[:, None] * xs
    y = y.reshape(bsz, seq, SSM_D_INNER) * jax.nn.silu(z.astype(jnp.float32))
    return rms_norm_2(y, norm_g).astype(z.dtype)

def conv_ssd_mixer(u, w_in, conv_dw_w, conv_dw_b, conv_ln_g, conv_ln_b, ssm_conv_w, ssm_conv_b, ssm_dt_bias, ssm_a_log, ssm_d, ssm_norm_g, w_out):
    proj = u @ w_in
    s0 = 2 * CONV_CH_2
    s1 = s0 + SSM_D_INNER
    s2 = s1 + SSM_XBC
    conv_in, z, xbc, dt_raw = jnp.split(proj, [s0, s1, s2], axis=-1)
    ya = conformer_conv(conv_in, conv_dw_w, conv_dw_b, conv_ln_g, conv_ln_b)
    yb = mamba2_ssd(z, xbc, dt_raw, ssm_conv_w, ssm_conv_b, ssm_dt_bias, ssm_a_log, ssm_d, ssm_norm_g)
    return jnp.concatenate([ya.astype(u.dtype), yb.astype(u.dtype)], axis=-1) @ w_out

def dilated_window_attention(q, k, v, slopes, window, dilation):
    bsz, seq, heads, dh = q.shape
    n = seq // dilation
    steps = window // dilation
    nb = -(-n // ATTN_BLOCK)
    pad = nb * ATTN_BLOCK - n

    def strided(t):
        t = t.reshape(bsz, n, dilation, heads, dh).transpose(0, 2, 1, 3, 4)
        t = t.reshape(bsz * dilation, n, heads, dh)
        t = jnp.pad(t, ((0, 0), (0, pad), (0, 0), (0, 0)))
        return t.reshape(bsz * dilation, nb, ATTN_BLOCK, heads, dh)

    def with_previous_block(t):
        prev = jnp.pad(t[:, :-1], ((0, 0), (1, 0), (0, 0), (0, 0), (0, 0)))
        return jnp.concatenate([prev, t], axis=2)

    qb = strided(q)
    kb = with_previous_block(strided(k))
    vb = with_previous_block(strided(v))
    scores = jnp.einsum('znqhd,znkhd->znhqk', qb.astype(jnp.float32), kb.astype(jnp.float32)) * (dh ** -0.5)
    qi = jnp.arange(ATTN_BLOCK)[:, None]
    kj = jnp.arange(2 * ATTN_BLOCK)[None, :] - ATTN_BLOCK
    rel = qi - kj
    blk0 = (jnp.arange(nb) * ATTN_BLOCK)[:, None, None]
    valid = (rel >= 0) & (rel <= steps) & (blk0 + kj >= 0)
    bias = -slopes[:, None, None] * (rel * dilation).astype(jnp.float32)
    scores = jnp.where(valid[None, :, None], scores + bias[None, None], -jnp.inf)
    lse = jax.nn.logsumexp(scores, axis=-1)
    probs = jnp.exp(scores - lse[..., None]).astype(v.dtype)
    out = jnp.einsum('znhqk,znkhd->znqhd', probs, vb)
    out = out.reshape(bsz, dilation, nb * ATTN_BLOCK, heads, dh)[:, :, :n]
    out = out.transpose(0, 2, 1, 3, 4).reshape(bsz, seq, heads, dh)
    lse = lse.transpose(0, 1, 3, 2).reshape(bsz, dilation, nb * ATTN_BLOCK, heads)[:, :, :n]
    lse = lse.transpose(0, 2, 1, 3).reshape(bsz, seq, heads)
    return out, lse

def dilated_attention_mixer(u, w_qkv, w_o):
    bsz, seq, _ = u.shape
    qkv = (u @ w_qkv).reshape(bsz, seq, 3, ATTN_GROUPS, ATTN_HEADS, ATTN_HEAD_DIM)
    slopes = jnp.exp2(-8.0 * jnp.arange(1, ATTN_HEADS + 1, dtype=jnp.float32) / ATTN_HEADS)
    outs = []
    lses = []
    for g, (window, dilation) in enumerate(DILATED_PATTERNS):
        o, l = dilated_window_attention(qkv[:, :, 0, g], qkv[:, :, 1, g], qkv[:, :, 2, g], slopes, window, dilation)
        outs.append(o)
        lses.append(l)
    weights = jax.nn.softmax(jnp.stack(lses, axis=0), axis=0)
    merged = jnp.einsum('gblh,gblhd->blhd', weights, jnp.stack(outs, axis=0).astype(jnp.float32))
    return merged.reshape(bsz, seq, ATTN_OUT_WIDTH).astype(u.dtype) @ w_o

def second_inputs(seed: int = 0) -> dict:
    key = jax.random.key(seed)
    ks = jax.random.split(key, 20)

    def normal(k, shape, scale):
        return jax.random.normal(k, shape, jnp.float32) * scale

    x = normal(ks[0], (BATCH, SEQ, D_MODEL), 1.0)
    norm_g = 1.0 + normal(ks[1], (DEPTH, 6, D_MODEL), 0.05)
    ffn_w1 = normal(ks[2], (DEPTH, 2, D_MODEL, 2 * D_FF_2), D_MODEL ** -0.5)
    ffn_w2 = normal(ks[3], (DEPTH, 2, D_FF_2, D_MODEL), D_FF_2 ** -0.5)
    hyb_w_in = normal(ks[4], (N_EVEN_2, D_MODEL, HYB_IN_COLS), D_MODEL ** -0.5)
    conv_dw_w = normal(ks[5], (N_EVEN_2, CONV_WIDTH, CONV_CH_2), CONV_WIDTH ** -0.5)
    conv_dw_b = normal(ks[6], (N_EVEN_2, CONV_CH_2), 0.02)
    conv_ln_g = 1.0 + normal(ks[7], (N_EVEN_2, CONV_CH_2), 0.05)
    conv_ln_b = normal(ks[8], (N_EVEN_2, CONV_CH_2), 0.02)
    ssm_conv_w = normal(ks[9], (N_EVEN_2, SSM_CONV_WIDTH, SSM_XBC), SSM_CONV_WIDTH ** -0.5)
    ssm_conv_b = normal(ks[10], (N_EVEN_2, SSM_XBC), 0.02)
    dt0 = jnp.exp(jax.random.uniform(ks[11], (N_EVEN_2, SSM_HEADS), jnp.float32, math.log(1e-3), math.log(1e-1)))
    ssm_dt_bias = dt0 + jnp.log(-jnp.expm1(-dt0))
    ssm_a_log = jnp.log(jax.random.uniform(ks[12], (N_EVEN_2, SSM_HEADS), jnp.float32, 1.0, 16.0))
    ssm_d = 1.0 + normal(ks[13], (N_EVEN_2, SSM_HEADS), 0.1)
    ssm_norm_g = 1.0 + normal(ks[14], (N_EVEN_2, SSM_D_INNER), 0.05)
    hyb_w_out = normal(ks[15], (N_EVEN_2, HYB_MIX_WIDTH, D_MODEL), HYB_MIX_WIDTH ** -0.5)
    attn_w_qkv = normal(ks[16], (N_ODD_2, D_MODEL, ATTN_QKV_COLS), D_MODEL ** -0.5)
    attn_w_o = normal(ks[17], (N_ODD_2, ATTN_OUT_WIDTH, D_MODEL), ATTN_OUT_WIDTH ** -0.5)
    return {'x': x, 'norm_g': norm_g, 'ffn_w1': ffn_w1, 'ffn_w2': ffn_w2, 'hyb_w_in': hyb_w_in, 'conv_dw_w': conv_dw_w, 'conv_dw_b': conv_dw_b, 'conv_ln_g': conv_ln_g, 'conv_ln_b': conv_ln_b, 'ssm_conv_w': ssm_conv_w, 'ssm_conv_b': ssm_conv_b, 'ssm_dt_bias': ssm_dt_bias, 'ssm_a_log': ssm_a_log, 'ssm_d': ssm_d, 'ssm_norm_g': ssm_norm_g, 'hyb_w_out': hyb_w_out, 'attn_w_qkv': attn_w_qkv, 'attn_w_o': attn_w_o}

def second_block(x, norm_g, ffn_w1, ffn_w2, hyb_w_in, conv_dw_w, conv_dw_b, conv_ln_g, conv_ln_b, ssm_conv_w, ssm_conv_b, ssm_dt_bias, ssm_a_log, ssm_d, ssm_norm_g, hyb_w_out, attn_w_qkv, attn_w_o):
    h = x
    for i in range(DEPTH):
        g = norm_g[i]
        h = h + 0.5 * rms_norm_2(swiglu_2(rms_norm_2(h, g[0]), ffn_w1[i, 0], ffn_w2[i, 0]), g[1])
        u = rms_norm_2(h, g[2])
        j = i // 2
        if i % 2 == 0:
            m = conv_ssd_mixer(u, hyb_w_in[j], conv_dw_w[j], conv_dw_b[j], conv_ln_g[j], conv_ln_b[j], ssm_conv_w[j], ssm_conv_b[j], ssm_dt_bias[j], ssm_a_log[j], ssm_d[j], ssm_norm_g[j], hyb_w_out[j])
        else:
            m = dilated_attention_mixer(u, attn_w_qkv[j], attn_w_o[j])
        h = h + rms_norm_2(m, g[3])
        h = h + 0.5 * rms_norm_2(swiglu_2(rms_norm_2(h, g[4]), ffn_w1[i, 1], ffn_w2[i, 1]), g[5])
    return h


def setup_inputs(seed=0):
    out = dict(first_inputs(seed))
    for name, value in second_inputs(seed + 1).items():
        if name != "x":
            out[name + "_2"] = value
    return out


def reference(
    x, c, ctx, c_ctx, ada_w, ada_b, norm1_g, norm2_g, ev_w_in, ev_conv_w, ev_q_g, ev_k_g,
    ev_rpb, ev_w_out, ffn_w1, ffn_w3, ffn_w2, od_w_in, od_cq_g, od_ck_g, od_sink, od_dq_g,
    od_dk_g, od_lam_q1, od_lam_k1, od_lam_q2, od_lam_k2, od_subln_g, od_w_out, moe_router,
    moe_w1, moe_w3, moe_w2, norm_g_2, ffn_w1_2, ffn_w2_2, hyb_w_in_2, conv_dw_w_2, conv_dw_b_2,
    conv_ln_g_2, conv_ln_b_2, ssm_conv_w_2, ssm_conv_b_2, ssm_dt_bias_2, ssm_a_log_2, ssm_d_2,
    ssm_norm_g_2, hyb_w_out_2, attn_w_qkv_2, attn_w_o_2,
):
    x = first_block(
        x, c, ctx, c_ctx, ada_w, ada_b, norm1_g, norm2_g, ev_w_in, ev_conv_w, ev_q_g, ev_k_g,
        ev_rpb, ev_w_out, ffn_w1, ffn_w3, ffn_w2, od_w_in, od_cq_g, od_ck_g, od_sink, od_dq_g,
        od_dk_g, od_lam_q1, od_lam_k1, od_lam_q2, od_lam_k2, od_subln_g, od_w_out, moe_router,
        moe_w1, moe_w3, moe_w2,
    )
    return second_block(
        x, norm_g_2, ffn_w1_2, ffn_w2_2, hyb_w_in_2, conv_dw_w_2, conv_dw_b_2, conv_ln_g_2,
        conv_ln_b_2, ssm_conv_w_2, ssm_conv_b_2, ssm_dt_bias_2, ssm_a_log_2, ssm_d_2,
        ssm_norm_g_2, hyb_w_out_2, attn_w_qkv_2, attn_w_o_2,
    )


_drawn_inputs = setup_inputs


def setup_inputs(seed=0):
    import zlib

    import numpy as np

    out = dict(_drawn_inputs(seed))
    spreads = {}
    factors = {'ev_q_g': 8.0,
     'ev_k_g': 8.0,
     'ev_rpb': 8.0,
     'od_cq_g': 8.0,
     'od_ck_g': 8.0,
     'od_sink': 8.0,
     'od_dq_g': 6.592,
     'od_dk_g': 3.808,
     'od_lam_q1': 2.892,
     'od_lam_k2': 4.086,
     'od_subln_g': 3.364,
     'conv_dw_b_2': 2.708,
     'conv_ln_b_2': 5.211,
     'ssm_conv_b_2': 3.173}
    for name, (base, spread) in spreads.items():
        noise = np.random.default_rng([zlib.crc32(name.encode()), seed]).standard_normal(out[name].shape)
        drawn = base * np.exp(spread * noise) if base else spread * noise
        out[name] = jnp.asarray(drawn.astype(out[name].dtype))
    for name, factor in factors.items():
        out[name] = (out[name] * factor).astype(out[name].dtype)
    return out
```

```python
from contextlib import ExitStack

import concourse.bass as bass
from concourse import mybir
import numpy as np

F32 = mybir.dt.float32
F32R = mybir.dt.float32r
ACT = mybir.ActivationFunctionType
ALU = mybir.AluOpType
AX = mybir.AxisListType

P = 128
TOK = 256
NT = TOK // P
D = 1024
KD = D // P
N = 512
HD = 64
RAWS = 4
EPS = 1e-6
LAM_INIT = 0.8 - 0.6 * float(np.exp(-0.3))
FF = 2816
FE = 1408
EXPERTS = 8
HYB = 4624
TAPS = 31
SSM_H = 16
STOP = 99


class Count:

    def __init__(self, n=0):
        self.n = n
        self.turn = None
        self.per = 0

    def at(self, ahead=0):
        if self.turn is None:
            return self.n + ahead
        return self.turn * self.per + (self.n + ahead)


def twice(count, ahead):
    if count.turn is None:
        return 2 * count.n + ahead
    return count.turn * (2 * count.per) + (2 * count.n + ahead)


class Turns:

    def __init__(self, turn, times, counts):
        self.times = times
        self.start = [(c, c.n, per) for c, per in counts]
        for c, per in counts:
            c.turn, c.per = turn, per

    def end(self):
        for c, n, per in self.start:
            assert c.n == n + per, (c.n, n, per)
            c.turn, c.n = None, n + per * self.times


class Chain:

    def __init__(self, eng, sem, plan, key):
        self.eng, self.sem, self.plan, self.key, self.n = eng, sem, plan, key, 0

    def put(self, ins, name=None):
        ins.then_inc(self.sem, 1)
        self.n += 1
        if name:
            self.plan["new"][name] = (self.key, self.n)
        return ins

    def link(self, ins, name=None):
        self.put(ins, name)
        self.eng.wait_ge(self.sem, self.n)


def constants():
    i = np.arange(P)
    ident = np.eye(P)
    upto = (i[:, None] <= i[None, :]) * 1.0
    after = (i[:, None] > i[None, :]) * 1.0
    pick = np.zeros((P, 2))
    pick[[0, 2, 4], 0] = 1
    pick[[1, 3, 4], 1] = 1
    lat = np.repeat(pick[:, 0:1], P, 1)
    ctx = np.repeat(pick[:, 1:2], P, 1)
    e = np.arange(EXPERTS)
    before = np.broadcast_to((e[None, :] < e[:, None]).reshape(1, -1) * 1.0, (P, EXPERTS * EXPERTS))
    base = np.concatenate([ident, upto, after, lat, ctx, before, pick], 1)
    tok = np.arange(TOK).reshape(NT, P).T
    key = np.arange(TOK)
    col, kcol = tok % 64, key % 64
    c0 = np.clip(col - 8, 0, 64 - 16)
    near = np.where((kcol >= c0[..., None]) & (kcol < c0[..., None] + 16), 0.0, -1e30)
    band = np.where(np.abs(key - tok[..., None]) <= 128, 0.0, -1e30)
    inv = np.float32(10000.0) ** (-np.arange(16, dtype=np.float32) / np.float32(16))
    pos = np.stack([tok // 64, tok % 64], -1).astype(np.float32)
    ang = pos[..., None] * inv.astype(np.float32)
    cos, sin = np.cos(ang), np.sin(ang)
    ropec = np.stack([cos, cos], -2).reshape(P, NT * HD)
    ropes = np.stack([-sin, sin], -2).reshape(P, NT * HD)
    rel = tok[..., None] - key
    dist = -np.maximum(rel, 0)
    dil = [np.where((rel >= 0) & (rel % d == 0) & (rel // d <= 128), 0.0, -1e30) for d in (1, 4, 16)]
    flat = lambda a: np.ascontiguousarray(np.asarray(a, np.float32).reshape(P, -1))
    return {
        "k_base": flat(base), "k_near": flat(near), "k_band": flat(band),
        "k_rope": flat(np.concatenate([ropec, ropes], 1)), "k_dist": flat(dist),
        "k_dil": flat(np.stack(dil, 1)),
    }


def program(nc, a, out, plan):
    plan["new"] = {}
    old = plan["old"]
    ctx = ExitStack()
    sems = {}

    def sem(name):
        if name not in sems:
            sems[name] = ctx.enter_context(nc.semaphore(name))
        return sems[name]

    def sb(name, shape, dt=F32):
        return ctx.enter_context(nc.sbuf_tensor(name, shape, dt))

    h = sb("h", [P, NT, D])
    hc = sb("hc", [P, NT, D])
    y = sb("y", [P, NT, D])
    raw = [sb(f"raw{i}", [P, 4, N]) for i in range(RAWS)]
    whi = [sb(f"whi{i}", [P, 2, N], F32R) for i in range(4)]
    wlo = [sb(f"wlo{i}", [P, 2, N], F32R) for i in range(4)]
    xhi = sb("xhi", [P, KD, TOK], F32R)
    xlo = sb("xlo", [P, KD, TOK], F32R)
    tmp = sb("tmp", [P, NT, D])
    gates = sb("gates", [P, 2, D])
    spad = sb("spad", [P, KD, P], F32R)
    kb = sb("kb", [P, 5 * P + 64 + 2])
    ident, upto, after = kb[:, 0:P], kb[:, P:2 * P], kb[:, 2 * P:3 * P]
    pick_lat, pick_ctx = kb[:, 3 * P:4 * P], kb[:, 4 * P:5 * P]
    before = kb[:, 5 * P:5 * P + 64]
    pick = kb[:, 5 * P + 64:5 * P + 66]
    cols = sb("cols", [P, 5, P])
    mod = sb("mod", [P, 4, KD, 2])
    scal = sb("scal", [P, 2, KD, 2])
    ss = sb("ss", [P, 96])
    negm = sb("negm", [P, 64])
    den = sb("den", [P, 64])
    mhalf = sb("mhalf", [P, 96])
    seed = sb("seed", [P, 2])
    logits = sb("logits", [P, NT, EXPERTS])
    rank = sb("rank", [P, NT, EXPERTS])
    gate = sb("gate", [P, NT, EXPERTS])
    dtraw = sb("dtraw", [P, NT, SSM_H])
    ones = sb("ones", [P, P])
    epsc = sb("epsc", [P, 1])
    onec = sb("onec", [P, 1])
    top = sb("top", [P, NT, 8])
    cmp = sb("cmp", [P, EXPERTS * EXPERTS])
    cmp2 = sb("cmp2", [P, EXPERTS * EXPERTS])
    small = {n: sb(n, [P, w]) for n, w in (("lamv", 4 * HD), ("lame", 4), ("sink", 8), ("nsink", 8),
                                           ("sinke", 16), ("sublng", 1), ("router", KD * EXPERTS), ("vtop", 8))}
    layouts = []

    def region(prefix, **parts):
        inner = ExitStack()
        got = {}
        for name, (shape, dt) in parts.items():
            got[name] = inner.enter_context(nc.sbuf_tensor(f"{prefix}_{name}", shape, dt))
        inner.close()
        layouts.append(got)
        return got

    R_S = region("s", mr=([P, 6 * D], F32), prm=([P, 5, P], F32), srow=([P, P], F32),
                 ssig=([P, 2 * KD], F32))
    R_F = region("f", hhi=([P, FF // P, TOK], F32R), hlo=([P, FF // P, TOK], F32R))
    R_E = region("e", p=([P, 2, NT, 6 * N], F32), qT=([P, 4, 2 * TOK], F32), kT=([P, 4, 2 * TOK], F32),
                 cT=([P, 4, TOK + 2], F32), bias=([P, 2, NT, TOK], F32), gqk=([P, 2 * HD], F32))
    OW = 2304
    OQ, QK = 1024, 1792
    R_O = region("o", pl=([P, NT, OW], F32), pc=([P, NT, OW - OQ], F32), sq=([P, NT, QK], F32),
                 gain=([P, QK], F32), qT=([P, 8, TOK], F32), kT=([P, 6, 2 * TOK], F32),
                 band=([P, NT, TOK], F32), rope=([P, 2, NT, HD], F32))
    R_H = region("h", p=([P, NT, HYB], F32), pad=([P, KD, TOK + TAPS - 1], F32), hid=([P, KD, TOK], F32),
                 xhead=([P, KD, SSM_H], F32), mu=([P, TOK], F32), rstd=([P, TOK], F32))
    R_G = region("g", p=([P, NT, HYB], F32), pad=([P, 12, TOK + 3], F32), xc=([P, 12, TOK], F32),
                 a1=([P, 2, 4, P], F32), dt=([P, 6, NT, SSM_H], F32), row=([P, 3, SSM_H], F32),
                 dec=([P, 2, SSM_H], F32))
    R_G2 = region("g2", p=([P, NT, HYB], F32), x2hi=([P, KD, TOK], F32R), x2lo=([P, KD, TOK], F32R))
    QKV = 4608
    R_A = region("a", p=([P, NT, QKV], F32), qT=([P, 12, TOK], F32), kT=([P, 12, TOK], F32),
                 dist=([P, NT, TOK], F32R), dil=([P, 3, NT, TOK], F32R), slope=([P, 8, P], F32R),
                 one=([P, P], F32R))
    psum = [ctx.enter_context(nc.psum_tensor(f"bank{i}", [P, N], F32)) for i in range(8)]
    G, U, O, T = psum[0:2], psum[2:4], psum[4:6], psum[6:8]

    params = R_S["prm"]
    vec = lambda ap: ap.rearrange("(r c) -> r c", c=P)
    prm_src = [
        (0, 0, a["norm1_g"].rearrange("l (r c) -> (l r) c", c=P)),
        (0, 16, a["norm2_g"].rearrange("l (r c) -> (l r) c", c=P)),
        (0, 32, a["norm_g_2"].rearrange("l s (r c) -> (l s r) c", c=P)),
        (1, 0, a["ev_conv_w"][0].rearrange("j (r c) -> (j r) c", c=P)),
        (1, 12, vec(a["conv_dw_b_2"][0])),
        (1, 20, vec(a["conv_ln_g_2"][0])),
        (1, 28, vec(a["conv_ln_b_2"][0])),
        (1, 36, a["ssm_conv_w_2"][0].rearrange("j (r c) -> (j r) c", c=P)),
        (1, 84, vec(a["ssm_conv_b_2"][0])),
        (1, 96, vec(a["ssm_norm_g_2"][0])),
        (1, 104, a["od_subln_g"]),
        (2, 0, a["conv_dw_w_2"][0, 0:16].rearrange("j (r c) -> (j r) c", c=P)),
        (3, 0, a["conv_dw_w_2"][0, 16:TAPS].rearrange("j (r c) -> (j r) c", c=P)),
    ]
    prm_rows = [128, 105, 128, 120]
    gain1 = lambda l: cols[:, 0, 8 * l:8 * l + 8]
    gain2 = lambda l: cols[:, 0, 16 + 8 * l:24 + 8 * l]
    gain_b2 = lambda l, s: cols[:, 0, 32 + 48 * l + 8 * s:40 + 48 * l + 8 * s]

    def tiles(w, k0, kt, c0, n):
        return w[k0 * P:(k0 + kt) * P, c0:c0 + n].rearrange("(k p) n -> p k n", p=P)

    class Load:

        def __init__(self, eng):
            self.eng, self.r = eng, Count()

        def unit(self, src, kt, n):
            slot = self.r.n % RAWS
            if self.r.n >= RAWS:
                self.eng.wait_ge(sem("w_lo"), twice(self.r, 2 - 2 * RAWS))
            to = raw[slot][:, 0:3:2, 0:n] if kt == 2 else raw[slot][:, 0:kt, 0:n]
            self.eng.dma_start(to, src).then_inc(sem(f"raw_in{slot}"), 16)
            self.r.n += 1

        def columns(self, w, k, c0, n):
            for k0 in range(0, k // P, 4):
                self.unit(tiles(w, k0, 4, c0, n), 4, n)

    class Split:

        def __init__(self, eng, high):
            self.eng, self.high = eng, high
            self.r = Count()
            self.used = Count()
            self.total = old.get("units", (0, 10 ** 6))[1]

        def half(self, j):
            if self.r.turn is None and self.r.n >= self.total:
                return
            slot, s = self.r.n % RAWS, (2 * self.r.n + j) % 4
            if self.high:
                if j == 0:
                    v = 16 * (self.r.n // RAWS + 1)
                    if self.r.turn is not None:
                        v = self.r.turn * (16 * self.r.per // RAWS) + v
                    self.eng.wait_ge(sem(f"raw_in{slot}"), v)
                if 2 * self.r.n + j >= 4:
                    self.eng.wait_ge(sem("w_used"), twice(self.r, j - 3))
                nc.scalar.activation(whi[s][:, :, :], raw[slot][:, 2 * j:2 * j + 2, :], ACT.Copy)\
                    .then_inc(sem("w_hi"), 1)
            else:
                self.eng.wait_ge(sem("w_hi"), twice(self.r, j + 1))
                nc.vector.tensor_tensor(wlo[s][:, :, :], raw[slot][:, 2 * j:2 * j + 2, :],
                                        whi[s][:, :, :].bitcast(F32), ALU.subtract)\
                    .then_inc(sem("w_lo"), 1)

        def step(self, between=None):
            self.half(0)
            self.used.n += 1
            if between:
                self.eng.wait_ge(sem("w_used"), twice(self.used, 0))
                between()
            self.half(1)
            self.r.n += 1

        def first(self):
            for _ in range(2):
                self.half(0)
                self.half(1)
                self.r.n += 1

    class Use:

        def __init__(self, eng):
            self.eng, self.r = eng, Count()

        def unit(self, xh, xl, k0, kt, n, banks, start, stop):
            cut = 1 if kt == 2 else 2
            for j, (b0, b1) in enumerate(((0, cut), (cut, kt))):
                s = (2 * self.r.n + j) % 4
                self.eng.wait_ge(sem("w_lo"), twice(self.r, j + 1))
                for t, bank in enumerate(banks):
                    for k in range(b0, b1):
                        tok = slice(t * P, t * P + P)
                        xk_h, xk_l = xh[:, k0 + k, tok], xl[:, k0 + k, tok] if xl is not None else None
                        wk = k - b0
                        first = start and k == 0
                        last = stop and k == kt - 1
                        nc.tensor.matmul(bank[:, 0:n], xk_h, whi[s][:, wk, 0:n], start=first, stop=False)
                        ins = nc.tensor.matmul(bank[:, 0:n], xk_h, wlo[s][:, wk, 0:n], start=False,
                                               stop=last and xl is None)
                        if xl is not None:
                            ins = nc.tensor.matmul(bank[:, 0:n], xk_l, whi[s][:, wk, 0:n], start=False,
                                                   stop=last)
                ins.then_inc(sem("w_used"), 1)
            self.r.n += 1

    FFN_SEMS = ("silu_done", "product_ready", "turned", "turned_hi", "turned_lo", "y_done")

    def widths(f):
        return [N] * (f // N) + ([f % N] if f % N else [])

    def spans(k):
        step = 3 if k == FE // P else 4
        return [(k0, min(step, k - k0)) for k0 in range(0, k, step)]

    PER_PAIR, PER_EXPERT = 4, 4 * len(widths(FE)) + 2 * len(spans(FE // P))
    assert PER_EXPERT % RAWS == 0 and PER_PAIR % RAWS == 0
    hs = tmp[:, :, N:2 * N]
    sg = tmp[:, :, 0:N]
    hhi, hlo = R_F["hhi"], R_F["hlo"]

    def load_ffn(ld, w1, w3, w2, f):
        ws = widths(f)

        def pair(c0, n):
            for w in (w1, w3):
                ld.columns(w, D, c0, n)

        full = f // N
        pair(0, N)
        if f == FF:
            with ld.eng.Fori(1, full) as i:
                turns = Turns(i - 1, full - 1, [(ld.r, PER_PAIR)])
                for w in (w1, w3):
                    for k0 in (0, 4):
                        src = w[k0 * P:(k0 + 4) * P, bass.ds(i * N, N)].rearrange("(k p) n -> p k n", p=P)
                        ld.unit(src, 4, N)
                turns.end()
            pair(full * N, f % N)
        else:
            for j, n in enumerate(ws[1:]):
                pair((j + 1) * N, n)
        for c in range(2):
            for k0, kt in spans(f // P):
                ld.unit(tiles(w2, k0, kt, c * N, N), kt, N)

    class Ffn:

        def __init__(self, eng, stream):
            self.eng, self.s = eng, stream
            self.pairs, self.ys = Count(1), Count(1)

        def counts(self, per, pairs, ys):
            c = [(self.s.r, per), (self.pairs, pairs), (self.ys, ys)]
            if isinstance(self.s, Split):
                c.append((self.s.used, per))
            return c

    class FfnPe(Ffn):
        def turn_over(self, n):
            self.eng.wait_ge(sem("product_ready"), self.pairs.at(0))
            self.eng.wait_ge(sem("turned_lo"), self.pairs.at(-1))
            for f in range(n // P):
                for t in range(NT):
                    c = (f % 2) * TOK + t * P
                    ins = nc.tensor.transpose(T[f // 2][:, c:c + P], hs[:, t, f * P:f * P + P], ident)
            ins.then_inc(sem("turned"), 1)

        def pair(self, n, former):
            self.eng.wait_ge(sem("silu_done"), self.pairs.at(0))
            self.s.unit(xhi, xlo, 0, 4, n, G, True, False)
            if former:
                self.turn_over(former)
            self.s.unit(xhi, xlo, 4, 4, n, G, False, True)
            self.eng.wait_ge(sem("product_ready"), self.pairs.at(0))
            self.eng.wait_ge(sem("y_done"), self.ys.at(0))
            self.s.unit(xhi, xlo, 0, 4, n, U, True, False)
            self.s.unit(xhi, xlo, 4, 4, n, U, False, True)
            self.pairs.n += 1

        def down(self, f):
            ws = widths(f)
            last_tile = (len(ws) - 1) * 4
            for c, banks in enumerate((O, U)):
                self.eng.wait_ge(sem("y_done"), self.ys.at(0))
                if c == 1:
                    self.eng.wait_ge(sem("product_ready"), self.pairs.at(0))
                for n, (k0, kt) in enumerate(spans(f // P)):
                    if c == 0:
                        self.eng.wait_ge(sem("turned_lo"), self.pairs.at(0 if k0 + kt > last_tile else -1))
                    self.s.unit(hhi, hlo, k0, kt, N, banks, n == 0, k0 + kt == f // P)
                    if c == 0 and n == 0:
                        self.turn_over(ws[-1])
            self.ys.n += 2

    class FfnAct(Ffn):
        def turned_hi(self, n, tile):
            def work():
                self.eng.wait_ge(sem("turned"), self.pairs.at(0))
                if not isinstance(tile, int):
                    self.eng.wait_ge(sem("turned"), 1)
                for b in range(0, n, TOK):
                    k = min(2, (n - b) // P)
                    at = slice(tile + b // P, tile + b // P + k) if isinstance(tile, int) \
                        else bass.ds(tile + b // P, k)
                    ins = nc.scalar.activation(hhi[:, at, :].rearrange("p k t -> p (k t)"),
                                               T[b // TOK][:, 0:k * TOK], ACT.Copy)
                ins.then_inc(sem("turned_hi"), 1)
            return work

        def pair(self, n, former, tile):
            def silu():
                self.eng.wait_ge(sem("product_ready"), self.pairs.at(0))
                for t in range(NT):
                    ins = nc.scalar.activation(sg[:, t, 0:n], G[t][:, 0:n], ACT.Silu)
                ins.then_inc(sem("silu_done"), 1)

            self.s.step(self.turned_hi(former, tile) if former else None)
            self.s.step(silu)
            self.s.step()
            self.s.step()
            self.pairs.n += 1

        def down(self, f):
            ws = widths(f)
            for c in range(2):
                for n, _ in enumerate(spans(f // P)):
                    self.s.step(self.turned_hi(ws[-1], (len(ws) - 1) * 4) if c == n == 0 else None)
            self.ys.n += 2

    class FfnDve(Ffn):
        def turned_lo(self, n, tile):
            def work():
                self.eng.wait_ge(sem("turned_hi"), self.pairs.at(0))
                for b in range(0, n, TOK):
                    k = min(2, (n - b) // P)
                    at = slice(tile + b // P, tile + b // P + k) if isinstance(tile, int) \
                        else bass.ds(tile + b // P, k)
                    flat = "p k t -> p (k t)"
                    ins = nc.vector.tensor_tensor(hlo[:, at, :].rearrange(flat), T[b // TOK][:, 0:k * TOK],
                                                  hhi[:, at, :].bitcast(F32).rearrange(flat), ALU.subtract)
                ins.then_inc(sem("turned_lo"), 1)
            return work

        def pair(self, n, former, tile, gate_of=None):
            def product():
                self.eng.wait_ge(sem("silu_done"), self.pairs.at(1))
                for t in range(NT):
                    if gate_of is None:
                        ins = nc.vector.tensor_tensor(hs[:, t, 0:n], sg[:, t, 0:n], U[t][:, 0:n], ALU.mult)
                    else:
                        ins = nc.vector.scalar_tensor_tensor(
                            out=hs[:, t, 0:n], in0=sg[:, t, 0:n], scalar=gate[:, t, bass.ds(gate_of, 1)],
                            in1=U[t][:, 0:n], op0=ALU.mult, op1=ALU.mult)
                ins.then_inc(sem("product_ready"), 1)

            self.s.step(self.turned_lo(former, tile) if former else None)
            self.s.step()
            self.s.step()
            self.s.step(product)
            self.pairs.n += 1

        def down(self, f, add):
            ws = widths(f)
            last = len(spans(f // P)) - 1
            for c, banks in enumerate((O, U)):
                def half_of_y():
                    for t in range(NT):
                        part = y[:, t, c * N:c * N + N]
                        if add:
                            ins = nc.vector.tensor_tensor(part, part, banks[t][:, :], ALU.add)
                        else:
                            ins = nc.vector.tensor_copy(part, banks[t][:, :])
                    ins.then_inc(sem("y_done"), 1)
                for n, _ in enumerate(spans(f // P)):
                    self.s.step(self.turned_lo(ws[-1], (len(ws) - 1) * 4) if c == n == 0
                                else half_of_y if n == last else None)
            self.ys.n += 2

    def dense(side):
        pe = isinstance(side, FfnPe)
        full = FF // N
        side.pair(*((N, None) if pe else (N, None, 0)))
        with side.eng.Fori(1, full) as i:
            turns = Turns(i - 1, full - 1, side.counts(PER_PAIR, 1, 0))
            side.pair(*((N, N) if pe else (N, N, (i - 1) * 4)))
            turns.end()
        side.pair(*((FF % N, N) if pe else (FF % N, N, (full - 1) * 4)))
        side.down(*((FF, False) if isinstance(side, FfnDve) else (FF,)))

    def experts(side):
        pe, dve = isinstance(side, FfnPe), isinstance(side, FfnDve)
        with side.eng.Fori(0, EXPERTS) as e:
            turns = Turns(e, EXPERTS, side.counts(PER_EXPERT, len(widths(FE)), 2))
            former = None
            for j, n in enumerate(widths(FE)):
                side.pair(*((n, former) if pe else (n, former, 4 * (j - 1)) + ((e,) if dve else ())))
                former = n
            side.down(*((FE, True) if dve else (FE,)))
            turns.end()

    class Engine:
        def __init__(self, eng, key):
            self.eng, self.key = eng, key
            self.chain = Chain(eng, sem(f"{key}_done"), plan, key)
            self.put, self.link = self.chain.put, self.chain.link
            self.outs = Count()

        def after(self, *names):
            for name in names:
                if plan["dry"]:
                    continue
                key, n = old[name]
                self.eng.wait_ge(sem(f"{key}_done"), n)

    def project_load(ld, w, k, cols_, first=0):
        for c0 in range(0, cols_, N):
            ld.columns(w, k, first + c0, min(N, cols_ - c0))

    def project_pe(e, s, xs, cols_, tag):
        for c in range(0, cols_, N):
            n = min(N, cols_ - c)
            if e.outs.n >= 3:
                e.eng.wait_ge(sem("out_done"), e.outs.n - 2)
            total = sum(k for _, _, k in xs)
            done = 0
            for xh, xl, k in xs:
                for k0 in range(0, k, 4):
                    s.unit(xh, xl, k0, 4, n, (G, U, O)[e.outs.n % 3], done == 0, done + 4 == total)
                    done += 4
            e.outs.n += 1

    def project_act(e, s, k, cols_, to):
        for c in range(0, cols_, N):
            n = min(N, cols_ - c)
            banks = (G, U, O)[e.outs.n % 3]

            def take():
                for t in range(NT):
                    ins = nc.scalar.activation(to(t, c, n), banks[t][:, 0:n], ACT.Copy)
                ins.then_inc(sem("out_done"), 1)
            for u in range(k // P // 4):
                s.step(take if u == k // P // 4 - 1 else None)
            e.outs.n += 1

    def project_dve(e, s, k, cols_):
        for c in range(0, cols_, N):
            for u in range(k // P // 4):
                s.step()
            e.outs.n += 1

    def rms_act(e, src, tag, *deps):
        e.after(*deps)
        for t in range(NT):
            e.link(nc.scalar.activation(tmp[:, t, :], src[:, t, :], ACT.Square, accum_out=ss[:, t:t + 1]),
                   tag + ":ss")

    def root_pool(e, tag, n, width, dep):
        e.after(dep)
        e.link(nc.gpsimd.tensor_scalar(ss[:, 0:n], ss[:, 0:n], 1.0 / width, EPS, ALU.mult, ALU.add))
        e.link(nc.gpsimd.tensor_tensor(ss[:, 0:n], ss[:, 0:n], mhalf[:, 0:n], ALU.pow), tag + ":root")

    xf = y[:, :, :].rearrange("p t d -> p (t d)").rearrange("p (k c) -> p k c", k=KD)

    def norm_act(e, src, tag, scale, shift, *deps):
        rms_act(e, src, tag, *deps)
        for k in range(KD):
            if k % 2 == 0:
                e.after(f"{tag}:xT{k // 2}")
            bank = psum[k // 2][:, (k % 2) * TOK:(k % 2) * TOK + TOK]
            bias = shift(k) if shift else 0.0
            e.put(nc.scalar.activation(xf[:, k, :], bank, ACT.Identity, bias=bias, scale=scale(k)),
                  f"{tag}:xf{k}")

    def norm_pool(e, tag):
        root_pool(e, tag, NT, D, tag + ":ss")

    def norm_dve(e, src, tag, to=None):
        hi, lo = to or (xhi, xlo)
        e.after(tag + ":root")
        for t in range(NT):
            e.put(nc.vector.tensor_scalar(tmp[:, t, :], src[:, t, :], ss[:, t:t + 1], None, ALU.mult),
                  f"{tag}:xn{t}")
        for half in range(2):
            e.after(f"{tag}:xf{half * 4 + 3}")
            sl = slice(half * 4, half * 4 + 4)
            flat = "p k t -> p (k t)"
            e.link(nc.vector.tensor_copy(hi[:, sl, :].rearrange(flat), xf[:, sl, :].rearrange(flat)))
            e.put(nc.vector.tensor_tensor(lo[:, sl, :].rearrange(flat), xf[:, sl, :].rearrange(flat),
                                          hi[:, sl, :].bitcast(F32).rearrange(flat), ALU.subtract),
                  tag + ":x")

    def norm_pe(e, tag, *deps):
        e.after(f"{tag}:xn{NT - 1}", *deps)
        for b in range(4):
            for k in range(2):
                for t in range(NT):
                    c = k * TOK + t * P
                    kk = 2 * b + k
                    ins = nc.tensor.transpose(psum[b][:, c:c + P], tmp[:, t, kk * P:kk * P + P], ident)
            e.put(ins, f"{tag}:xT{b}")

    def resid_pe(e, tag, pick_, g, *deps):
        e.after(*deps)
        for c in range(2):
            ins = nc.tensor.matmul(psum[6 + c][:, :], pick_[0:5, :], gates[0:5, g, c * N:c * N + N],
                                   start=True, stop=True)
        e.put(ins, tag + ":gate")

    def resid_dve(e, hh, tag, outs=None):
        e.after(tag + ":gate")
        if outs is not None:
            e.eng.wait_ge(sem("out_done"), outs)
        else:
            e.link(nc.vector.tensor_copy(seed[:, 1:2], seed[:, 0:1]))
        for t in range(NT):
            for c in range(2):
                part = y[:, t, c * N:c * N + N]
                e.put(nc.vector.tensor_tensor(part, part, psum[6 + c][:, :], ALU.mult))
        e.eng.wait_ge(e.chain.sem, e.chain.n)
        e.link(nc.vector.tensor_tensor(hh[:, :, :], hh[:, :, :], y[:, :, :], ALU.add), tag + ":h")

    srow, ssig, mr = (R_S[n] for n in ("srow", "ssig", "mr"))

    def side_load(e, dst, src, name):
        e.eng.dma_start(dst, src).then_inc(sem("in_" + name), 16)

    def loaded(e, name, n=1):
        e.eng.wait_ge(sem("in_" + name), 16 * n)

    def setup_pool(e):
        side_load(e, kb[:, :], a["k_base"], "base")
        side_load(e, srow[0:8, :], a["c"].rearrange("o (r c) -> (o r) c", c=P), "c")
        side_load(e, srow[8:16, :], a["c_ctx"].rearrange("(r c) -> r c", c=P), "c")
        for tile, row, src in prm_src:
            side_load(e, params[row:row + src.shape[0], tile, :], src, "params")
        for n, t in (("x", h), ("ctx", hc)):
            side_load(e, t[:, :, :], a[n][0].rearrange("(t p) d -> p t d", p=P), n)
        e.link(nc.gpsimd.memset(mhalf[:, :], -0.5), "mhalf")

    def setup_pe(e):
        loaded(e, "base")
        loaded(e, "c", 2)
        e.put(nc.tensor.transpose(psum[4][:, 0:16], srow[0:16, :], ident[0:16, 0:16]), "scol")
        loaded(e, "params", len(prm_src))
        for i, r in enumerate(prm_rows):
            ins = nc.tensor.transpose(psum[5][:, i * P:i * P + r], params[0:r, i, :], ident[0:r, 0:r])
        e.put(ins, "cols")

    def setup_act(e):
        e.after("scol")
        e.link(nc.scalar.activation(ssig[:, :], psum[4][:, 0:16], ACT.Silu), "silu c")
        e.after("spad zero")
        sv = ssig[:, :].rearrange("p (s k) -> p k s", s=2)
        e.link(nc.scalar.activation(spad[:, :, 0:2], sv, ACT.Copy), "spad hi")

    def setup_dve(e):
        e.link(nc.vector.memset(seed[:, :], 0.0))
        e.link(nc.vector.memset(epsc[:, :], EPS))
        e.link(nc.vector.memset(onec[:, :], 1.0))
        e.link(nc.vector.memset(spad[:, :, :].rearrange("p k c -> p (k c)").bitcast(F32), 0.0), "spad zero")
        e.after("spad hi")
        sv = ssig[:, :].rearrange("p (s k) -> p k s", s=2)
        e.link(nc.vector.tensor_tensor(spad[:, :, 2:4], sv, spad[:, :, 0:2].bitcast(F32), ALU.subtract), "spad")
        e.after("cols")
        for i, r in enumerate(prm_rows):
            e.link(nc.vector.tensor_copy(cols[:, i, 0:r], psum[5][:, i * P:i * P + r]), "params")

    def mod_load(ld, l):
        for c in range(12):
            ld.columns(a["ada_w"][l], D, c * N, N)

    def mod_pool(e, l, *deps):
        e.after(*deps)
        side_load(e, mr[4:5, :], a["ada_b"][l:l + 1, :], f"bias{l}")
        for g, part in enumerate((2, 5)):
            side_load(e, gates[4:5, g, :], a["ada_b"][l:l + 1, part * D:part * D + D], f"bias{l}")

    def mod_pe(e, s, l, ffn):
        e.after("spad")
        e.eng.wait_ge(sem("y_done"), ffn.ys.n)
        for c in range(12):
            if e.outs.n >= 3:
                e.eng.wait_ge(sem("out_done"), e.outs.n - 2)
            bank = (G, U, O)[e.outs.n % 3][0]
            for k0 in (0, 4):
                s.unit(spad, None, k0, 4, N, [bank], k0 == 0, k0 == 4)
            e.outs.n += 1
        e.eng.wait_ge(sem("out_done"), e.outs.n)
        loaded(e, f"bias{l}", 3)
        if l:
            e.after("res_f1:h")
        for i, part in enumerate((0, 1, 3, 4)):
            for k in range(KD):
                c = (i * KD + k) * 2
                ins = nc.tensor.matmul(psum[7][:, c:c + 2], mr[0:5, part * D + k * P:part * D + k * P + P],
                                       pick[0:5, :], start=True, stop=True)
        e.put(ins, f"mod{l}:cols")

    def mod_act(e, s, l):
        if l:
            e.after("res_f1:gate")
        for c in range(12):
            bank = (G, U, O)[e.outs.n % 3][0]

            def take():
                part, c0 = c // 2, (c % 2) * N
                if part in (2, 5):
                    nc.scalar.activation(gates[0:4, part // 3, c0:c0 + N], bank[0:4, :], ACT.Copy)\
                        .then_inc(sem("out_done"), 1)
                else:
                    nc.scalar.activation(mr[0:4, c * N:c * N + N], bank[0:4, :], ACT.Copy)\
                        .then_inc(sem("out_done"), 1)
            s.step()
            s.step(take)
            e.outs.n += 1

    def mod_dve(e, s, l):
        for c in range(12):
            s.step()
            s.step()
            e.outs.n += 1
        e.after(f"mod{l}:cols")
        e.link(nc.vector.tensor_copy(mod[:, :, :, :].rearrange("p a k s -> p (a k s)"), psum[7][:, 0:64]))
        for i, g in enumerate((gain1(l), gain2(l))):
            for st in range(2):
                e.link(nc.vector.scalar_tensor_tensor(out=scal[:, i, :, st], in0=mod[:, 2 * i + 1, :, st],
                                                      scalar=1.0, in1=g, op0=ALU.add, op1=ALU.mult),
                       f"mod{l}")

    def cut_x(e, name, *deps, tiles_=KD):
        e.after(*deps)
        flat = lambda ap: ap[:, 0:tiles_, :].rearrange("p k t -> p (k t)")
        e.link(nc.vector.tensor_copy(flat(xhi), flat(xf)))
        e.link(nc.vector.tensor_tensor(flat(xlo), flat(xf), flat(xhi).bitcast(F32), ALU.subtract), name)

    prob = [tmp[:, i, 0:N] for i in range(2)]
    probT = [tmp[:, i, N:2 * N] for i in range(2)]
    SC, PT = psum[0:2], psum[2:4]
    ITEM = Count()

    def attn_pe(e, base, items, ready, *deps):
        e.after(*deps)
        last = len(items)

        def scores(i):
            it = items[i]
            if ready:
                ready(e, i)
            if i >= 2:
                e.eng.wait_ge(sem("exp_done"), base + i - 1)
            bank = SC[i % 2]
            n = it["n"]
            adds = it["adds"]
            nc_last = nc.tensor.matmul(bank[:, 0:n], it["q"], it["k"], start=True, stop=not adds)
            for j, (l_, r_) in enumerate(adds):
                nc_last = nc.tensor.matmul(bank[:, 0:r_.shape[-1]], l_, r_, start=False, stop=j == len(adds) - 1)
            nc_last.then_inc(sem("scores"), 1)

        def outputs(i):
            it = items[i]
            e.eng.wait_ge(sem("probT_done"), base + i + 1)
            if it.get("o_free"):
                it["o_free"](e)
            kt = it["n"] // P
            for k in range(kt):
                ins = nc.tensor.matmul(it["o"], probT[i % 2][:, k * P:k * P + P], it["v"][k],
                                       start=k == 0, stop=k == kt - 1)
            ins.then_inc(sem("out_ready"), 1)

        scores(0)
        for i in range(last):
            if i + 1 < last:
                scores(i + 1)
            e.eng.wait_ge(sem("exp_done"), base + i + 1)
            if i >= 2:
                e.eng.wait_ge(sem("probT_done"), base + i - 1)
            for k in range(items[i]["n"] // P):
                ins = nc.tensor.transpose(PT[i % 2][:, k * P:k * P + P], prob[i % 2][:, k * P:k * P + P], ident)
            ins.then_inc(sem("prob_turned"), 1)
            if i >= 1:
                outputs(i - 1)
        outputs(last - 1)

    def attn_dve(e, base, items, floor, *deps, every=None):
        e.after(*deps)

        def take(i):
            e.eng.wait_ge(sem("prob_turned"), base + i + 1)
            if i >= 2:
                e.eng.wait_ge(sem("out_ready"), base + i - 1)
            n = items[i]["n"]
            nc.vector.tensor_copy(probT[i % 2][:, 0:n], PT[i % 2][:, 0:n]).then_inc(sem("probT_done"), 1)

        for i, it in enumerate(items):
            e.eng.wait_ge(sem("scores"), base + i + 1)
            col = negm[:, i:i + 1]
            if floor:
                e.link(nc.vector.tensor_reduce(col, SC[i % 2][:, 0:it["n"]], AX.X, ALU.max, negate=True))
                nc.vector.tensor_tensor(col, col, floor(i), ALU.min).then_inc(sem("max_done"), 1)
            else:
                nc.vector.tensor_reduce(col, SC[i % 2][:, 0:it["n"]], AX.X, ALU.max, negate=True)\
                    .then_inc(sem("max_done"), 1)
            if i >= 1:
                take(i - 1)
            if every:
                every(i)
        take(len(items) - 1)

    def attn_act(e, base, items, *deps):
        e.after(*deps)
        for i, it in enumerate(items):
            e.eng.wait_ge(sem("max_done"), base + i + 1)
            if i >= 2:
                e.eng.wait_ge(sem("prob_turned"), base + i - 1)
            nc.scalar.activation(prob[i % 2][:, 0:it["n"]], SC[i % 2][:, 0:it["n"]], ACT.Exp,
                                 bias=negm[:, i:i + 1], accum_out=den[:, i:i + 1]).then_inc(sem("exp_done"), 1)

    def over(col_ap, heads, width):
        return col_ap.rearrange("p (h o) -> p h o", o=1).broadcast_to([P, heads, width])

    p_e, qT, kT, cT = R_E["p"], R_E["qT"], R_E["kT"], R_E["cT"]
    NA_H = 8

    def even_items(st):
        items = []
        for hd in range(NA_H):
            for t in range(NT):
                half = slice((hd % 2) * HD, (hd % 2) * HD + HD)
                q0 = st * TOK + t * P
                keys = slice(0, 2 * TOK) if st == 0 else slice(TOK, 2 * TOK)
                vs = [p_e[:, s_, t_, 2560 + hd * HD:2560 + hd * HD + HD]
                      for s_ in ((0, 1) if st == 0 else (1,)) for t_ in range(NT)]
                items.append(dict(
                    n=2 * TOK if st == 0 else TOK, q=qT[half, hd // 2, q0:q0 + P], k=kT[half, hd // 2, keys],
                    adds=[(ident, R_E["bias"][:, hd % 2, t, :])] if st == 0 else [], v=vs,
                    o=psum[4 + t][:, hd * HD:hd * HD + HD]))
        return items

    def even_pool(e):
        e.after("in_e1:x")
        near = xf[:, 4:6, :].rearrange("p t k -> p (t k)")
        side_load(e, near, a["k_near"], "near")
        for i, name in enumerate(("ev_q_g", "ev_k_g")):
            side_load(e, R_E["gqk"][:, i * HD:i * HD + HD], a[name].broadcast_to([P, HD]), "gqk")
        loaded(e, "gqk", 2)
        e.link(nc.gpsimd.tensor_scalar(R_E["gqk"][:, 0:HD], R_E["gqk"][:, 0:HD], HD ** -0.5, None, ALU.mult), "gqk")
        root_pool(e, "qk_e", 64, HD, "qk_e:ss")
        loaded(e, "near")
        for hd in range(NA_H):
            if hd >= 2:
                e.eng.wait_ge(sem("scores"), 2 * (hd - 1))
            b = R_E["bias"][:, hd % 2, :, :].rearrange("p t k -> p (t k)")
            e.eng.dma_start(b, a["k_rpb"][hd]).then_inc(sem(f"in_rpb{hd % 2}"), 16)
            e.eng.wait_ge(sem(f"in_rpb{hd % 2}"), 16 * (hd // 2 + 1))
            e.link(nc.gpsimd.tensor_tensor(b, b, near, ALU.add),
                   f"bias{hd}")

    def even_qk_act(e):
        for st in range(2):
            for t in range(NT):
                if st:
                    e.after("qk_e:ss0")
                e.put(nc.scalar.activation(tmp[:, t, :], p_e[:, st, t, 1536:2560], ACT.Square), f"qk_e:sq{st}")

    def even_qk_dve(e):
        for st in range(2):
            e.after(f"qk_e:sq{st}")
            for t in range(NT):
                c = st * 32 + t * 16
                e.put(nc.vector.tensor_reduce(ss[:, c:c + 16], tmp[:, t, :].rearrange("p (h d) -> p h d", d=HD),
                                              AX.X, ALU.add), f"qk_e:ss{st}" if st == 0 else "qk_e:ss")
        e.after("qk_e:root", "gqk")
        for st in range(2):
            for t in range(NT):
                c = st * 32 + t * 16
                qk = p_e[:, st, t, 1536:2560].rearrange("p (h d) -> p h d", d=HD)
                e.link(nc.vector.tensor_tensor(qk, qk, over(ss[:, c:c + 16], 16, HD), ALU.mult))
                both = p_e[:, st, t, 1536:2560].rearrange("p (a h d) -> p a h d", a=2, d=HD)
                g = R_E["gqk"][:, :].rearrange("p (a o d) -> p a o d", a=2, o=1).broadcast_to([P, 2, 8, HD])
                e.link(nc.vector.tensor_tensor(both, both, g, ALU.mult), f"qk_e:{st}")

    def even_qk_pe(e):
        for st in range(2):
            e.after(f"qk_e:{st}")
            if st:
                e.after("qkT0")
            for b in range(8):
                for t in range(NT):
                    c = (b % 2) * TOK + t * P
                    ins = nc.tensor.transpose(psum[b // 2][:, c:c + P],
                                              p_e[:, st, t, 1536 + b * P:1536 + b * P + P], ident)
            e.put(ins, f"qkT_ps{st}")

    def even_qk_out(e):
        for st in range(2):
            e.after(f"qkT_ps{st}")
            for b in range(4):
                to = (qT, kT)[b // 2][:, (b % 2) * 2:(b % 2) * 2 + 2, st * TOK:st * TOK + TOK]
                e.link(nc.scalar.activation(to, psum[b][:, :].rearrange("p (k t) -> p k t", k=2), ACT.Copy),
                       f"qkT{st}")

    def conv_pe(e, st, *deps):
        e.after(f"gcu{st}", *deps)
        for b in range(4):
            for t in range(NT):
                c = (b % 2) * TOK + t * P
                nc.tensor.transpose(psum[4 + b // 2][:, c:c + P], tmp[:, t, b * P:b * P + P], ident)
                ins = nc.tensor.transpose(psum[6 + b // 2][:, c:c + P], p_e[:, st, t, b * P:b * P + P], ident)
        e.put(ins, f"conv_ps{st}")

    def conv_act(e, st):
        e.after(f"conv_ps{st}", "pads")
        for b in range(2):
            two = lambda x: x.rearrange("p (k t) -> p k t", k=2)
            e.put(nc.scalar.activation(cT[:, 2 * b:2 * b + 2, 1:TOK + 1], two(psum[4 + b][:, :]), ACT.Copy))
            e.link(nc.scalar.activation(tmp[:, b, N:2 * N], psum[6 + b][:, :], ACT.Copy), f"convT{st}")

    def conv_dve(e, st, *deps):
        e.after(*deps)
        for t in range(NT):
            e.link(nc.vector.tensor_tensor(tmp[:, t, 0:N], p_e[:, st, t, N:2 * N], p_e[:, st, t, 2 * N:3 * N],
                                           ALU.mult), f"gcu{st}")
        if st == 0:
            e.put(nc.vector.memset(cT[:, :, 0:1], 0.0))
            e.link(nc.vector.memset(cT[:, :, TOK + 1:TOK + 2], 0.0), "pads")
        e.after(f"convT{st}")
        for b in range(4):
            for j in range(3):
                tap = cols[:, 1, j * 4 + b:j * 4 + b + 1]
                if j == 0:
                    ins = nc.vector.tensor_scalar(xf[:, b, :], cT[:, b, 0:TOK], tap, None, ALU.mult)
                else:
                    ins = nc.vector.scalar_tensor_tensor(out=xf[:, b, :], in0=cT[:, b, j:j + TOK], scalar=tap,
                                                         in1=xf[:, b, :], op0=ALU.mult, op1=ALU.add)
                e.link(ins)
            e.link(nc.vector.tensor_tensor(xf[:, b, :], xf[:, b, :],
                                           tmp[:, b // 2, N + (b % 2) * TOK:N + (b % 2) * TOK + TOK], ALU.mult),
                   f"conv{st}")

    def heads_out_dve(e, tag, n_items, base, width=HD, heads=8):
        e.eng.wait_ge(sem("out_ready"), base + n_items)
        e.eng.wait_ge(sem("exp_done"), base + n_items)
        e.link(nc.vector.reciprocal(den[:, 0:n_items], den[:, 0:n_items]))
        for t in range(NT):
            r = den[:, 0:n_items].rearrange("p (h t) -> p h t", t=NT)[:, :, t:t + 1].broadcast_to([P, heads, width])
            e.link(nc.vector.tensor_tensor(tmp[:, t, 0:N].rearrange("p (h d) -> p h d", d=width),
                                           psum[4 + t][:, :].rearrange("p (h d) -> p h d", d=width), r, ALU.mult),
                   tag + ":o")

    def heads_out_pe(e, tag):
        e.after(tag + ":o")
        for b in range(4):
            for t in range(NT):
                c = (b % 2) * TOK + t * P
                ins = nc.tensor.transpose(psum[6 + b // 2][:, c:c + P], tmp[:, t, b * P:b * P + P], ident)
        e.put(ins, tag + ":oT_ps")

    def heads_out_act(e, tag, first=4, scale=1.0):
        e.after(tag + ":oT_ps")
        for b in range(2):
            e.link(nc.scalar.activation(xf[:, first + 2 * b:first + 2 * b + 2, :].rearrange("p k t -> p (k t)"),
                                        psum[6 + b][:, :], ACT.Identity, scale=scale), tag + ":oT")

    pl, pc, sq, gain, qTo, kTo, band, rope = (R_O[n] for n in
                                              ("pl", "pc", "sq", "gain", "qT", "kT", "band", "rope"))
    lamv, lame, sink, nsink, sinke, sublng, router, vtop = small.values()
    NORMED = [(pl, 0, 18), (pl, 20, 8), (pc, 0, 2), (pc, 4, 8)]
    root_at = lambda src, t, hd: (t * 28 if src is pl else 56 + t * 12) + hd

    def gain_at(src, hd):
        return (hd if src is pl else hd + 16) * HD

    def window_items():
        items = []
        for hd in range(8):
            for t in range(NT):
                half = slice((hd % 2) * HD, (hd % 2) * HD + HD)
                kv = hd // 4
                v = [pl[:, t_, 1152 + kv * HD:1152 + kv * HD + HD] for t_ in range(NT)] + \
                    [pc[:, t_, 128 + kv * HD:128 + kv * HD + HD] for t_ in range(NT)]
                items.append(dict(n=2 * TOK, q=qTo[half, hd // 2, t * P:t * P + P], k=kTo[half, kv, :],
                                  adds=[(ident, band[:, t, :])], v=v, o=psum[4 + t][:, hd * HD:hd * HD + HD]))
        return items

    def diff_items():
        items = []
        for hd in range(4):
            for i in range(2):
                for t in range(NT):
                    half = slice(i * HD, i * HD + HD)
                    v = [pl[:, t_, 1792 + hd * P:1792 + hd * P + P] for t_ in range(NT)] + \
                        [pc[:, t_, 768 + hd * P:768 + hd * P + P] for t_ in range(NT)]
                    items.append(dict(n=2 * TOK, q=qTo[half, 4 + hd, t * P:t * P + P], k=kTo[half, 2 + hd, :],
                                      adds=[], v=v, o=psum[4 + 2 * i + t][:, hd * P:hd * P + P]))
        return items

    def odd_pool(e):
        e.after("in_o1:x")
        side_load(e, band[:, :, :].rearrange("p t k -> p (t k)"), a["k_band"], "odd")
        side_load(e, rope[:, :, :, :].rearrange("p a t d -> p (a t d)"), a["k_rope"], "odd")
        for name, hd, n in (("od_cq_g", 0, 8), ("od_dq_g", 8, 8), ("od_ck_g", 16, 2), ("od_dk_g", 20, 8)):
            side_load(e, gain[:, hd * HD:(hd + n) * HD].rearrange("p (h d) -> p h d", h=n),
                      a[name].rearrange("o (h d) -> o h d", h=1).broadcast_to([P, n, HD]), "odd")
        for i, name in enumerate(("od_lam_q1", "od_lam_k1", "od_lam_q2", "od_lam_k2")):
            side_load(e, lamv[:, i * HD:i * HD + HD], a[name].broadcast_to([P, HD]), "odd")
        side_load(e, sink[:, :], a["od_sink"].broadcast_to([P, 8]), "odd")
        side_load(e, router[:, :].rearrange("p (k e) -> p k e", e=EXPERTS),
                  a["moe_router"][0].rearrange("(k p) e -> p k e", p=P), "odd")
        loaded(e, "odd", 12)
        e.link(nc.gpsimd.tensor_scalar(gain[:, 0:OQ], gain[:, 0:OQ], HD ** -0.5, None, ALU.mult))
        e.link(nc.gpsimd.tensor_scalar(nsink[:, :], sink[:, :], -1.0, None, ALU.mult), "odd loads")
        root_pool(e, "qk_o", 80, HD, "qk_o:ss")

    def odd_qk_act(e):
        e.eng.wait_ge(sem("out_done"), e.outs.n)
        for t in range(NT):
            e.put(nc.scalar.activation(sq[:, t, :], pl[:, t, 0:QK], ACT.Square), "qk_o:sq0")
        e.after("qk_o:ss0")
        for t in range(NT):
            e.put(nc.scalar.activation(sq[:, t, 0:768], pc[:, t, 0:768], ACT.Square), "qk_o:sq1")

    def odd_qk_dve(e):
        heads = lambda ap: ap.rearrange("p (h d) -> p h d", d=HD)
        for st, (n, c0) in enumerate(((28, 0), (12, 56))):
            e.after(f"qk_o:sq{st}")
            for t in range(NT):
                c = c0 + t * n
                e.link(nc.vector.tensor_reduce(ss[:, c:c + n], heads(sq[:, t, 0:n * HD]), AX.X, ALU.add),
                       "qk_o:ss0" if st == 0 else "qk_o:ss")
        e.after("odd loads")
        for i in range(2):
            pr = lamv[:, 2 * i * HD:2 * i * HD + HD]
            e.link(nc.vector.tensor_tensor(pr, pr, lamv[:, (2 * i + 1) * HD:(2 * i + 2) * HD], ALU.mult))
            e.link(nc.vector.tensor_reduce(lame[:, i:i + 1], pr, AX.X, ALU.add), "lam dots")
        e.link(nc.vector.tensor_scalar(sublng[:, :], cols[:, 1, 104:105], 1.0 - LAM_INIT, None, ALU.mult), "sublng")
        e.after("qk_o:root")
        for src, hd, n in NORMED:
            for t in range(NT):
                part = src[:, t, hd * HD:(hd + n) * HD]
                c = root_at(src, t, hd)
                e.link(nc.vector.tensor_tensor(heads(part), heads(part), over(ss[:, c:c + n], n, HD), ALU.mult))
                g0 = gain_at(src, hd)
                e.link(nc.vector.tensor_tensor(part, part, gain[:, g0:g0 + n * HD], ALU.mult), "k_ctx")
        rot = y[:, :, :].rearrange("p t d -> p (t d)")
        for src, hd, n in NORMED[:2]:
            for t in range(NT):
                part = src[:, t, hd * HD:(hd + n) * HD]
                first = sq[:, t, 0:n * HD]
                table = lambda i: rope[:, i, t, :].rearrange("p (o d) -> p o d", o=1).broadcast_to([P, n, HD])
                e.link(nc.vector.tensor_tensor(heads(first), heads(part), table(0), ALU.mult))
                quad = lambda ap: ap.rearrange("p (h a b c) -> p h a b c", a=2, b=2, c=16)
                s5 = rope[:, 1, t, :].rearrange("p (o a b c) -> p o a b c", o=1, a=2, b=2, c=16)
                for b in range(2):
                    e.link(nc.vector.tensor_tensor(quad(rot[:, 0:n * HD])[:, :, :, b, :],
                                                   quad(part)[:, :, :, 1 - b, :],
                                                   s5[:, :, :, b, :].broadcast_to([P, n, 2, 16]), ALU.mult))
                e.link(nc.vector.tensor_tensor(part, first, rot[:, 0:n * HD], ALU.add), "qk_o")

    def odd_qk_pe(e):
        e.after("qk_o")
        for b in range(8):
            for t in range(NT):
                c = (b % 2) * TOK + t * P
                ins = nc.tensor.transpose(psum[b // 2][:, c:c + P], pl[:, t, b * P:b * P + P], ident)
        e.put(ins, "qoT_ps")
        for b in range(4):
            for t in range(2 * NT):
                src, c = (pl, 1280) if t < NT else (pc, 256)
                ins = nc.tensor.transpose(psum[4 + b][:, t * P:t * P + P],
                                          src[:, t % NT, c + b * P:c + b * P + P], ident)
        e.put(ins, "dkT_ps")
        e.after("qoT")
        for b in range(2):
            for t in range(2 * NT):
                src, c = (pl, 1024) if t < NT else (pc, 0)
                for half in range(2):
                    ins = nc.tensor.transpose(psum[b][half * 0:HD, t * P:t * P + P] if half == 0 else
                                              psum[2 + b][0:HD, t * P:t * P + P],
                                              src[:, t % NT, c + b * HD:c + b * HD + HD], ident)
        e.put(ins, "ckT_ps")

    def odd_qk_out(e):
        e.after("qoT_ps")
        for b in range(4):
            e.link(nc.scalar.activation(qTo[:, 2 * b:2 * b + 2, :].rearrange("p k t -> p (k t)"), psum[b][:, :],
                                        ACT.Copy), "qoT")
        e.after("dkT_ps")
        for b in range(4):
            e.link(nc.scalar.activation(kTo[:, 2 + b, :], psum[4 + b][:, :], ACT.Copy), "dkT")
        e.after("ckT_ps")
        for b in range(2):
            for half in range(2):
                e.link(nc.scalar.activation(kTo[half * HD:half * HD + HD, b, :], psum[2 * half + b][0:HD, :],
                                            ACT.Copy), "ckT")
        e.after("lam dots")
        e.link(nc.scalar.activation(lame[:, 2:4], lame[:, 0:2], ACT.Exp), "lam exp")

    def window_sinks_dve(e, base):
        e.eng.wait_ge(sem("exp_done"), base + 16)
        e.eng.wait_ge(sem("max_done"), base + 16)
        two = lambda ap: ap.rearrange("p (h t) -> p h t", t=NT)
        e.link(nc.vector.tensor_tensor(two(sinke[:, :]), two(negm[:, 0:16]), over(sink[:, :], 8, NT), ALU.add),
               "sink args")
        e.after("sink exps")
        e.link(nc.vector.tensor_tensor(den[:, 0:16], den[:, 0:16], sinke[:, :], ALU.add))

    def window_sinks_act(e):
        e.after("sink args")
        e.link(nc.scalar.activation(sinke[:, :], sinke[:, :], ACT.Exp), "sink exps")

    def diff_out_dve(e, base):
        e.eng.wait_ge(sem("out_ready"), base + 16)
        e.eng.wait_ge(sem("exp_done"), base + 16)
        e.after("lam exp")
        e.link(nc.vector.tensor_tensor(lame[:, 0:1], lame[:, 2:3], lame[:, 3:4], ALU.subtract))
        e.link(nc.vector.tensor_scalar(lame[:, 0:1], lame[:, 0:1], -1.0, -LAM_INIT, ALU.mult, ALU.add))
        e.link(nc.vector.reciprocal(den[:, 0:16], den[:, 0:16]))
        r = den[:, 0:16].rearrange("p (h i t) -> p h i t", i=2, t=NT)
        e.link(nc.vector.tensor_scalar(r[:, :, 1, :], r[:, :, 1, :], lame[:, 0:1], None, ALU.mult))
        heads = lambda ap: ap.rearrange("p (h d) -> p h d", d=P)
        for t in range(NT):
            for i in range(2):
                e.link(nc.vector.tensor_tensor(heads(tmp[:, t, i * N:i * N + N]), heads(psum[4 + 2 * i + t][:, :]),
                                               r[:, :, i, t:t + 1].broadcast_to([P, 4, P]), ALU.mult))
            e.link(nc.vector.tensor_tensor(tmp[:, t, 0:N], tmp[:, t, 0:N], tmp[:, t, N:2 * N], ALU.add), "diff")
        for t in range(NT):
            e.link(nc.vector.tensor_tensor(tmp[:, t, N:2 * N], tmp[:, t, 0:N], tmp[:, t, 0:N], ALU.mult))
            e.link(nc.vector.tensor_reduce(ss[:, t * 4:t * 4 + 4], heads(tmp[:, t, N:2 * N]), AX.X, ALU.add),
                   "subln:ss")
        e.after("subln:root")
        for t in range(NT):
            e.link(nc.vector.tensor_tensor(heads(tmp[:, t, 0:N]), heads(tmp[:, t, 0:N]),
                                           over(ss[:, t * 4:t * 4 + 4], 4, P), ALU.mult), "att_d:o")

    def router_pe(e):
        for t in range(NT):
            for k in range(KD):
                ins = nc.tensor.matmul(psum[4 + t][:, 0:EXPERTS], xf[:, k, t * P:t * P + P],
                                       router[:, k * EXPERTS:(k + 1) * EXPERTS], start=k == 0, stop=k == KD - 1)
        e.put(ins, "logits")

    def router_dve(e):
        e.after("logits")
        for t in range(NT):
            e.link(nc.vector.tensor_copy(logits[:, t, :], psum[4 + t][:, 0:EXPERTS]))
        e.link(nc.vector.memset(y[:, :, :], 0.0))
        pairs = lambda ap: ap.rearrange("p (e j) -> p e j", j=EXPERTS)
        for t in range(NT):
            e.link(nc.vector.max(top[:, t, :], logits[:, t, :]))
            e.link(nc.vector.tensor_tensor(vtop[:, t:t + 1], top[:, t, 1:2], top[:, t, 0:1], ALU.subtract), "gap")
            lj = logits[:, t:t + 1, :].broadcast_to([P, EXPERTS, EXPERTS])
            le = over(logits[:, t, :], EXPERTS, EXPERTS)
            e.link(nc.vector.tensor_tensor(pairs(cmp[:, :]), lj, le, ALU.is_gt))
            e.link(nc.vector.tensor_tensor(pairs(cmp2[:, :]), lj, le, ALU.is_equal))
            e.link(nc.vector.tensor_tensor(cmp2[:, :], cmp2[:, :], before, ALU.mult))
            e.link(nc.vector.tensor_tensor(cmp[:, :], cmp[:, :], cmp2[:, :], ALU.add))
            e.link(nc.vector.tensor_reduce(rank[:, t, :], pairs(cmp[:, :]), AX.X, ALU.add))
        e.after("gap exp")
        e.link(nc.vector.tensor_scalar(vtop[:, 4:6], vtop[:, 2:4], 1.0, None, ALU.add))
        e.link(nc.vector.reciprocal(vtop[:, 4:6], vtop[:, 4:6]))
        e.link(nc.vector.tensor_tensor(vtop[:, 6:8], vtop[:, 4:6], vtop[:, 2:4], ALU.mult))
        for t in range(NT):
            e.link(nc.vector.tensor_scalar(gate[:, t, :], rank[:, t, :], 0.0, vtop[:, 4 + t:5 + t], ALU.is_equal,
                                           ALU.mult))
            e.link(nc.vector.tensor_scalar(cmp[:, 0:EXPERTS], rank[:, t, :], 1.0, vtop[:, 6 + t:7 + t],
                                           ALU.is_equal, ALU.mult))
            e.link(nc.vector.tensor_tensor(gate[:, t, :], gate[:, t, :], cmp[:, 0:EXPERTS], ALU.add))

    def router_act(e):
        e.after("gap")
        e.link(nc.scalar.activation(vtop[:, 2:4], vtop[:, 0:2], ACT.Exp), "gap exp")

    def resid2_pool(e, tag, i, l, s_, dep):
        if dep:
            e.after(dep)
        side_load(e, gates[:, i % 2, :], a["norm_g_2"][l, s_:s_ + 1, :].broadcast_to([P, D]), f"post{i % 2}")
        root_pool(e, tag, NT, D, tag + ":ss")

    def resid2_dve(e, tag, i, factor):
        e.after(tag + ":root")
        loaded(e, f"post{i % 2}", i // 2 + 1)
        for t in range(NT):
            e.put(nc.vector.scalar_tensor_tensor(out=y[:, t, :], in0=y[:, t, :], scalar=ss[:, t:t + 1],
                                                 in1=gates[:, i % 2, :], op0=ALU.mult, op1=ALU.mult))
        e.eng.wait_ge(e.chain.sem, e.chain.n)
        for t in range(NT):
            e.link(nc.vector.scalar_tensor_tensor(out=h[:, t, :], in0=y[:, t, :], scalar=factor, in1=h[:, t, :],
                                                  op0=ALU.mult, op1=ALU.add), tag + ":h")

    def ffn2_weights(l, f):
        w = a["ffn_w1_2"][l, f]
        return w[:, 0:FF], w[:, FF:2 * FF], a["ffn_w2_2"][l, f]

    p_h, hpad, hid, xhead, mu, rstd = (R_H[n] for n in ("p", "pad", "hid", "xhead", "mu", "rstd"))
    flat3 = lambda ap: ap.rearrange("p k t -> p (k t)")

    def conf_pool(e, dep):
        e.after(dep)
        side_load(e, xhead[:, :, :], a["hyb_w_in_2"][0, :, HYB - SSM_H:HYB].rearrange("(k p) e -> p k e", p=P), "xhead")
        e.link(nc.gpsimd.memset(hpad[:, :, 0:TAPS - 1], 0.0), "hpad zero")
        e.link(nc.gpsimd.memset(ones[:, :], 1.0), "ones")

    def head_pe(e):
        loaded(e, "xhead")
        for t in range(NT):
            for k in range(KD):
                ins = nc.tensor.matmul(psum[6 + t][:, 0:SSM_H], xf[:, k, t * P:t * P + P], xhead[:, k, :],
                                       start=k == 0, stop=k == KD - 1)
        e.put(ins, "head")

    def conf_act(e):
        e.after("head taken")
        for t in range(NT):
            e.link(nc.scalar.activation(p_h[:, t, D:2 * D], p_h[:, t, D:2 * D], ACT.Sigmoid), f"sigmoid{t}")
        e.after("hpad zero")
        for b in range(4):
            e.after(f"gluT{b}")
            e.link(nc.scalar.activation(hpad[:, 2 * b:2 * b + 2, TAPS - 1:TAPS - 1 + TOK],
                                        psum[b][:, :].rearrange("p (k t) -> p k t", k=2), ACT.Copy), f"hpad{b}")
        e.after("centred")
        e.link(nc.scalar.activation(hpad[:, :, 0:TOK], hid[:, :, :], ACT.Square), "squares")
        e.after("var_ps")
        e.link(nc.scalar.activation(rstd[:, :], psum[5][:, 0:TOK], ACT.Sqrt, scale=1.0 / D, bias=epsc[:, 0:1]), "std")
        e.after("hid normed")
        for k in range(KD):
            e.put(nc.scalar.activation(xf[:, k, :], hid[:, k, :], ACT.Silu, scale=cols[:, 1, 20 + k:21 + k],
                                       bias=cols[:, 1, 28 + k:29 + k]), "conformer")

    def conf_pe(e):
        e.after("glu")
        for b in range(4):
            for k in range(2):
                for t in range(NT):
                    c, kk = k * TOK + t * P, 2 * b + k
                    ins = nc.tensor.transpose(psum[b][:, c:c + P], p_h[:, t, kk * P:kk * P + P], ident)
            e.put(ins, f"gluT{b}")
        e.after("hid", "ones")
        for k in range(KD):
            ins = nc.tensor.matmul(psum[4][:, 0:TOK], ones[:, :], hid[:, k, :], start=k == 0, stop=k == KD - 1)
        e.put(ins, "mean_ps")
        e.after("squares")
        for k in range(KD):
            ins = nc.tensor.matmul(psum[5][:, 0:TOK], ones[:, :], hpad[:, k, 0:TOK], start=k == 0, stop=k == KD - 1)
        e.put(ins, "var_ps")

    def conf_dve(e):
        for t in range(NT):
            e.after(f"sigmoid{t}")
            e.link(nc.vector.tensor_tensor(p_h[:, t, 0:D], p_h[:, t, 0:D], p_h[:, t, D:2 * D], ALU.mult), "glu")
        e.after("hpad3")
        for j in range(TAPS):
            for k in range(KD):
                tile, c = (2, j * KD + k) if j < 16 else (3, (j - 16) * KD + k)
                tap = cols[:, tile, c:c + 1]
                if j == 0:
                    ins = nc.vector.tensor_scalar(hid[:, k, :], hpad[:, k, 0:TOK], tap, cols[:, 1, 12 + k:13 + k],
                                                  ALU.mult, ALU.add)
                else:
                    e.eng.wait_ge(e.chain.sem, e.chain.n - KD + 1)
                    ins = nc.vector.scalar_tensor_tensor(out=hid[:, k, :], in0=hpad[:, k, j:j + TOK], scalar=tap,
                                                         in1=hid[:, k, :], op0=ALU.mult, op1=ALU.add)
                e.put(ins, "hid")
        e.after("mean_ps")
        e.link(nc.vector.tensor_scalar(mu[:, :], psum[4][:, 0:TOK], 1.0 / D, None, ALU.mult))
        rows_ = lambda ap: ap.rearrange("p (o t) -> p o t", o=1).broadcast_to([P, KD, TOK])
        e.link(nc.vector.tensor_tensor(hid[:, :, :], hid[:, :, :], rows_(mu[:, :]), ALU.subtract), "centred")
        e.after("std")
        e.link(nc.vector.reciprocal(rstd[:, :], rstd[:, :]))
        e.link(nc.vector.tensor_tensor(hid[:, :, :], hid[:, :, :], rows_(rstd[:, :]), ALU.mult), "hid normed")
        cut_x(e, "cat_h1", "conformer")

    gpad, xc, a1, dts, srow2, dec = (R_G[n] for n in ("pad", "xc", "a1", "dt", "row", "dec"))
    gflat = flat3(gpad[:, :, :])
    cbm = gflat[:, 0:4 * P].rearrange("p (i l) -> p i l", i=4)
    bmt = gflat[:, 4 * P:6 * P]
    xw = gflat[:, 6 * P:6 * P + D]
    s0 = gflat[:, 6 * P + D:6 * P + 2 * D].rearrange("p (g c) -> p g c", g=2)
    xs = [p_h[:, t, 0:D] for t in range(NT)]
    xdt = [p_h[:, t, D:2 * D] for t in range(NT)]
    ex = [tmp[:, i, 0:N] for i in range(2)]
    mt = [tmp[:, i, N:2 * N].rearrange("p (i l) -> p i l", i=4) for i in range(2)]
    DT, ADT, NEG, ABS = dts[:, 0], dts[:, 1], dts[:, 2], dts[:, 3]
    heads = lambda ap: ap.rearrange("p (h d) -> p h d", d=HD)

    def ssm_pool(e):
        e.after("cat_h1")
        for i, name in enumerate(("ssm_dt_bias_2", "ssm_a_log_2", "ssm_d_2")):
            side_load(e, srow2[:, i, :], a[name].broadcast_to([P, SSM_H]), "ssm_rows")
        e.link(nc.gpsimd.memset(gpad[:, :, 0:3], 0.0), "gpad zero")

    def ssm_act(e):
        e.after("gpad zero")
        for b in range(6):
            e.after(f"xbcT{b}")
            e.link(nc.scalar.activation(gpad[:, 2 * b:2 * b + 2, 3:3 + TOK],
                                        psum[b][:, :].rearrange("p (k t) -> p k t", k=2), ACT.Copy), "gpad")
        e.after("dt abs")
        e.link(nc.scalar.activation(ABS, ABS, ACT.Exp, scale=-1.0))
        e.link(nc.scalar.activation(ABS, ABS, ACT.Ln, bias=onec[:, 0:1]))
        e.link(nc.scalar.activation(srow2[:, 1, :], srow2[:, 1, :], ACT.Exp), "a exp")
        e.after("conv4")
        e.link(nc.scalar.activation(flat3(xc[:, :, :]), flat3(xc[:, :, :]), ACT.Silu), "xc")
        e.after("xsT")
        for t in range(NT):
            for half in range(2):
                e.link(nc.scalar.activation(xs[t][:, half * N:half * N + N], psum[2 * t + half][:, :], ACT.Copy), "xs")
        e.after("bmT")
        e.link(nc.scalar.activation(bmt, psum[4][:, 0:2 * P], ACT.Copy), "bmt")
        e.after("decays_ps")
        e.link(nc.scalar.activation(dec[:, :, :].rearrange("p a h -> p (a h)"), psum[6][:, 0:2 * SSM_H], ACT.Exp),
               "decays")
        for i in range(8):
            e.after(f"seg{i}")
            if i >= 2:
                e.after(f"mt{i - 2}")
            e.link(nc.scalar.activation(ex[i % 2], psum[i % 2][:, :], ACT.Exp), f"ex{i}")
        for g in range(2):
            e.after("s0_ps")
            e.link(nc.scalar.activation(s0[:, g, :], psum[g][:, :], ACT.Copy), "s0")
        e.after("gated z")
        for t in range(NT):
            e.link(nc.scalar.activation(p_h[:, t, 2 * D:3 * D], p_h[:, t, 2 * D:3 * D], ACT.Silu), "z")

    def ssm_pe(e):
        e.after("cat_h1")
        for b in range(6):
            for k in range(2):
                for t in range(NT):
                    c, kk = k * TOK + t * P, 3 * D + (2 * b + k) * P
                    ins = nc.tensor.transpose(psum[b][:, c:c + P], p_h[:, t, kk:kk + P], ident)
            e.put(ins, f"xbcT{b}")
        e.after("xc", "gpad")
        for t in range(NT):
            for b in range(8):
                ins = nc.tensor.transpose(psum[2 * t + b // 4][:, (b % 4) * P:(b % 4) * P + P],
                                          xc[:, b, t * P:t * P + P], ident)
        e.put(ins, "xsT")
        for g in range(2):
            ins = nc.tensor.transpose(psum[4][:, g * P:g * P + P], xc[:, 8 + g, 0:P], ident)
        e.put(ins, "bmT")
        for c in range(NT):
            for g in range(2):
                tok = slice(c * P, c * P + P)
                i = c * 2 + g
                ins = nc.tensor.matmul(psum[5][:, i * P:i * P + P], xc[:, 8 + g, tok], xc[:, 10 + g, tok],
                                       start=True, stop=True)
        e.put(ins, "cb_ps")
        e.after("adt")
        nc.tensor.matmul(psum[6][:, 0:SSM_H], after, ADT[:, 0, :], start=True, stop=True)
        e.put(nc.tensor.matmul(psum[6][:, SSM_H:2 * SSM_H], upto, ADT[:, 1, :], start=True, stop=True), "decays_ps")

        def diagonal(i):
            c, quad_ = i // 4, i % 4
            bank = psum[4 + 2 * c + quad_ // 2]
            for j in range(4):
                hd = quad_ * 4 + j
                ins = nc.tensor.matmul(bank[:, (hd % 8) * HD:(hd % 8) * HD + HD], mt[i % 2][:, j, :],
                                       xdt[c][:, hd * HD:hd * HD + HD], start=True, stop=True)
            e.put(ins, f"diag{i}")

        for i in range(8):
            e.after(f"a1_{i}")
            if i == 0:
                e.after("xdt", "xs")
            if i >= 2:
                e.after(f"ex{i - 2}")
            for j in range(4):
                ins = nc.tensor.matmul(psum[i % 2][:, j * P:j * P + P], a1[:, i % 2, j, :], upto, start=True, stop=True)
            e.put(ins, f"seg{i}")
            if i >= 1:
                if i == 1:
                    e.after("cbm", "decays", "bmt")
                e.after(f"mt{i - 1}")
                diagonal(i - 1)
        e.after("mt7", "ex7")
        diagonal(7)
        e.after("xw", "bmt")
        for g in range(2):
            ins = nc.tensor.matmul(psum[g][:, :], bmt[:, g * P:g * P + P], xw[:, g * N:g * N + N],
                                   start=True, stop=True)
        e.put(ins, "s0_ps")
        e.after("s0")
        for g in range(2):
            ins = nc.tensor.matmul(psum[2 + g][:, :], xc[:, 10 + g, P:2 * P], s0[:, g, :], start=True, stop=True)
        e.put(ins, "yoff_ps")

    def dt_dve(e):
        e.after("head")
        for t in range(NT):
            e.link(nc.vector.tensor_copy(dtraw[:, t, :], psum[6 + t][:, 0:SSM_H]), "head taken")

    def ssm_dve(e):
        loaded(e, "ssm_rows", 3)
        step = lambda ap: ap.rearrange("p (o h) -> p o h", o=1).broadcast_to([P, NT, SSM_H])
        e.link(nc.vector.tensor_tensor(DT, dtraw[:, :, :], step(srow2[:, 0, :]), ALU.add))
        e.link(nc.vector.tensor_scalar(NEG, DT, -1.0, None, ALU.mult))
        e.link(nc.vector.tensor_tensor(ABS, DT, NEG, ALU.max), "dt abs")
        e.after("a exp")
        e.link(nc.vector.scalar_tensor_tensor(out=DT.rearrange("p t h -> p (t h)"), in0=DT.rearrange("p t h -> p (t h)"),
                                              scalar=0.0, in1=ABS.rearrange("p t h -> p (t h)"),
                                              op0=ALU.max, op1=ALU.add))
        e.link(nc.vector.tensor_scalar(srow2[:, 1, :], srow2[:, 1, :], -1.0, None, ALU.mult))
        e.link(nc.vector.tensor_tensor(ADT, DT, step(srow2[:, 1, :]), ALU.mult), "adt")
        e.after("gpad")
        for j in range(4):
            for b in range(12):
                tap = cols[:, 1, 36 + j * 12 + b:37 + j * 12 + b]
                if j == 0:
                    ins = nc.vector.tensor_scalar(xc[:, b, :], gpad[:, b, 0:TOK], tap, cols[:, 1, 84 + b:85 + b],
                                                  ALU.mult, ALU.add)
                else:
                    e.eng.wait_ge(e.chain.sem, e.chain.n - 11)
                    ins = nc.vector.scalar_tensor_tensor(out=xc[:, b, :], in0=gpad[:, b, j:j + TOK], scalar=tap,
                                                         in1=xc[:, b, :], op0=ALU.mult, op1=ALU.add)
                e.put(ins, "conv4")
        e.after("xs")
        for t in range(NT):
            e.link(nc.vector.tensor_tensor(heads(xdt[t]), heads(xs[t]), over(DT[:, t, :], SSM_H, HD), ALU.mult), "xdt")
        e.after("cb_ps")
        e.link(nc.vector.tensor_tensor(cbm, psum[5][:, :].rearrange("p (i l) -> p i l", i=4),
                                       upto.rearrange("p (o l) -> p o l", o=1).broadcast_to([P, 4, P]), ALU.mult),
               "cbm")

        def masked_steps(i):
            c, q4 = i // 4, (i % 4) * 4
            if i >= 2:
                e.after(f"seg{i - 2}")
            e.link(nc.vector.tensor_tensor(a1[:, i % 2, :, :],
                                           after.rearrange("p (o l) -> p o l", o=1).broadcast_to([P, 4, P]),
                                           over(ADT[:, c, q4:q4 + 4], 4, P), ALU.mult), f"a1_{i}")

        masked_steps(0)
        e.after("decays")
        e.link(nc.vector.tensor_tensor(heads(xw), heads(xdt[0]), over(dec[:, 0, :], SSM_H, HD), ALU.mult), "xw")
        for i in range(8):
            c, g = i // 4, (i % 4) // 2
            if i < 7:
                masked_steps(i + 1)
            e.after(f"ex{i}")
            if i >= 2:
                e.after(f"diag{i - 2}")
            e.link(nc.vector.tensor_tensor(mt[i % 2], ex[i % 2].rearrange("p (i l) -> p i l", i=4),
                                           cbm[:, c * 2 + g:c * 2 + g + 1, :].broadcast_to([P, 4, P]), ALU.mult),
                   f"mt{i}")
        e.after("yoff_ps")
        e.link(nc.vector.tensor_copy(y[:, 0, 0:1], seed[:, 0:1]), "gated z")
        for t in range(NT):
            for half in range(2):
                part = y[:, t, half * N:half * N + N]
                rng = slice(half * N, half * N + N)
                hh = slice(half * 8, half * 8 + 8)
                e.link(nc.vector.tensor_tensor(heads(part), heads(xs[t][:, rng]), over(srow2[:, 2, hh], 8, HD), ALU.mult))
                e.link(nc.vector.tensor_tensor(part, part, psum[4 + 2 * t + half][:, :], ALU.add))
                if t == 1:
                    e.link(nc.vector.tensor_tensor(heads(xw[:, rng]), heads(psum[2 + half][:, :]),
                                                   over(dec[:, 1, hh], 8, HD), ALU.mult))
                    e.link(nc.vector.tensor_tensor(part, part, xw[:, rng], ALU.add))
        e.after("z")
        for t in range(NT):
            e.link(nc.vector.tensor_tensor(y[:, t, :], y[:, t, :], p_h[:, t, 2 * D:3 * D], ALU.mult), "ssm y")

    p_a, qTa, kTa, dist, dil, slope, one = (R_A[n] for n in ("p", "qT", "kT", "dist", "dil", "slope", "one"))
    stage_d = flat3(y[:, :, :])

    def dilated_items():
        items = []
        for t in range(NT):
            for g in range(3):
                for hd in range(8):
                    half = slice((hd % 2) * HD, (hd % 2) * HD + HD)
                    n = (t + 1) * P
                    b = g * 4 + hd // 2
                    items.append(dict(
                        n=n, q=qTa[half, b, t * P:t * P + P], k=kTa[half, b, 0:n],
                        adds=[(slope[:, hd, :], dist[:, t, 0:n]), (one[:, :], dil[:, g, t, 0:n])],
                        v=[p_a[:, t_, 3072 + g * N + hd * HD:3072 + g * N + hd * HD + HD] for t_ in range(t + 1)],
                        o=psum[4 + (t * 3 + g) % 2][:, hd * HD:hd * HD + HD]))
        return items

    def raw_out(gi):
        return (y if gi < 4 else hc)[:, (gi % 4) // 2, (gi % 2) * N:(gi % 2) * N + N]

    def dil_pool(e):
        e.after("in_at:x")
        side_load(e, stage_d[:, 0:N], a["k_dist"], "dil0")
        side_load(e, stage_d[:, N:4 * N], a["k_dil"], "dil0")

    def dil_act(e):
        loaded(e, "dil0", 2)
        e.put(nc.scalar.activation(flat3(dist[:, :, :]), stage_d[:, 0:N], ACT.Copy))
        e.put(nc.scalar.activation(dil[:, :, :, :].rearrange("p g t k -> p (g t k)"), stage_d[:, N:4 * N], ACT.Copy))
        e.put(nc.scalar.activation(one[:, :], ident, ACT.Copy))
        for hd in range(8):
            e.put(nc.scalar.activation(slope[:, hd, :], ident, ACT.Copy, scale=2.0 ** -(hd + 1)), "masks")
        for r in range(3):
            e.after(f"dilT{r}")
            for b in range(4):
                to = (qTa, kTa)[(4 * r + b) // 6]
                at = 2 * ((4 * r + b) % 6)
                e.link(nc.scalar.activation(flat3(to[:, at:at + 2, :]), psum[(4 * r + b) % 8][:, :], ACT.Copy,
                                            scale=HD ** -0.5 if to is qTa else 1.0), f"dilqk{r}")

    def dil_pe(e):
        e.eng.wait_ge(sem("out_done"), e.outs.n)
        for r in range(3):
            if r == 2:
                e.after("dilqk0")
            for b in range(4):
                for k in range(2):
                    for t in range(NT):
                        blk = 2 * (4 * r + b) + k
                        c = k * TOK + t * P
                        ins = nc.tensor.transpose(psum[(4 * r + b) % 8][:, c:c + P],
                                                  p_a[:, t, blk * P:blk * P + P], ident)
            e.put(ins, f"dilT{r}")

    def dil_every(e, base):
        def every(i):
            if i >= 9 and (i - 9) % 8 == 0:
                raw_take((i - 9) // 8)

        def raw_take(gi):
            e.eng.wait_ge(sem("out_ready"), base + 8 * gi + 8)
            e.link(nc.vector.tensor_copy(raw_out(gi), psum[4 + gi % 2][:, :]), f"raw{gi}")
        return every, raw_take

    def merge_dve(e, base):
        e.eng.wait_ge(sem("exp_done"), base + 48)
        e.eng.wait_ge(sem("max_done"), base + 48)
        grp = lambda ap, t, g: ap[:, (t * 3 + g) * 8:(t * 3 + g) * 8 + 8]
        for t in range(NT):
            low = ss[:, t * 8:t * 8 + 8]
            e.link(nc.vector.tensor_tensor(low, grp(negm, t, 0), grp(negm, t, 1), ALU.min))
            e.link(nc.vector.tensor_tensor(low, low, grp(negm, t, 2), ALU.min))
            for g in range(3):
                e.link(nc.vector.tensor_tensor(grp(negm, t, g), low, grp(negm, t, g), ALU.subtract), "weights")
        e.after("weight exps")
        for t in range(NT):
            z = ss[:, t * 8:t * 8 + 8]
            for g in range(3):
                e.link(nc.vector.tensor_tensor(grp(den, t, g), grp(den, t, g), grp(negm, t, g), ALU.mult))
            e.link(nc.vector.tensor_tensor(z, grp(den, t, 0), grp(den, t, 1), ALU.add))
            e.link(nc.vector.tensor_tensor(z, z, grp(den, t, 2), ALU.add))
            e.link(nc.vector.reciprocal(z, z))
            for g in range(3):
                e.link(nc.vector.tensor_tensor(grp(negm, t, g), grp(negm, t, g), z, ALU.mult))
                part = raw_out(t * 3 + g)
                e.link(nc.vector.tensor_tensor(heads(part), heads(part), over(grp(negm, t, g), 8, HD), ALU.mult))
            e.link(nc.vector.tensor_tensor(tmp[:, t, 0:N], raw_out(t * 3), raw_out(t * 3 + 1), ALU.add))
            e.link(nc.vector.tensor_tensor(tmp[:, t, 0:N], tmp[:, t, 0:N], raw_out(t * 3 + 2), ALU.add), "att_a:o")

    def merge_act(e):
        e.after("weights")
        e.link(nc.scalar.activation(negm[:, 0:48], negm[:, 0:48], ACT.Exp), "weight exps")

    E_ITEMS = [even_items(0), even_items(1)]
    W_ITEMS, D_ITEMS, A_ITEMS = window_items(), diff_items(), dilated_items()
    ATT0 = [0, 16, 32, 48, 64]

    STAGES = plan["stop"]

    def on(n):
        return STAGES >= n

    with ctx:
        block = ctx.enter_context(nc.Block())

        @block.sync
        def _(sp):
            ld = Load(sp)
            mod_load(ld, 0)
            for _ in range(2):
                project_load(ld, a["ev_w_in"][0], D, 6 * N)
            for _ in range(2):
                project_load(ld, a["ev_w_out"][0], D, D)
            if on(2):
                for _ in range(2):
                    load_ffn(ld, a["ffn_w1"][0], a["ffn_w3"][0], a["ffn_w2"][0], FF)
            if on(3):
                mod_load(ld, 1)
                project_load(ld, a["od_w_in"][0], D, OW)
                project_load(ld, a["od_w_in"][0], D, OW - OQ, OQ)
                project_load(ld, a["od_w_out"][0], D, D)
            if on(4):
                with sp.Fori(0, EXPERTS) as x:
                    turns = Turns(x, EXPERTS, [(ld.r, PER_EXPERT)])
                    load_ffn(ld, a["moe_w1"][0, bass.ds(x, 1)].rearrange("o k n -> (o k) n"),
                             a["moe_w3"][0, bass.ds(x, 1)].rearrange("o k n -> (o k) n"),
                             a["moe_w2"][0, bass.ds(x, 1)].rearrange("o k n -> (o k) n"), FE)
                    turns.end()
            if on(5):
                load_ffn(ld, *ffn2_weights(0, 0), FF)
                project_load(ld, a["hyb_w_in_2"][0], D, HYB - SSM_H)
                project_load(ld, a["hyb_w_out_2"][0], 2 * D, D)
            if on(6):
                load_ffn(ld, *ffn2_weights(0, 1), FF)
                load_ffn(ld, *ffn2_weights(1, 0), FF)
                project_load(ld, a["attn_w_qkv_2"][0], D, QKV)
                project_load(ld, a["attn_w_o_2"][0], D // 2, D)
                load_ffn(ld, *ffn2_weights(1, 1), FF)
            if STAGES == 4:
                for _ in range(2):
                    ld.unit(tiles(a["ada_w"][0], 0, 4, 0, N), 4, N)
            plan["new"]["units"] = ("units", ld.r.n)
            if not plan["dry"]:
                key, n = old["final"]
                sp.wait_ge(sem("dve_done"), n)
            sp.dma_start(out[0].rearrange("(t p) d -> p t d", p=P), h[:, :, :]).then_inc(sem("stored"), 16)
            sp.wait_ge(sem("stored"), 16)

        @block.gpsimd
        def _(g):
            e = Engine(g, "pool")
            setup_pool(e)
            mod_pool(e, 0)
            norm_pool(e, "in_e0")
            norm_pool(e, "in_e1")
            even_pool(e)
            if on(2):
                norm_pool(e, "ff0")
                norm_pool(e, "ff1")
            if on(3):
                mod_pool(e, 1, "res_f1:h")
                norm_pool(e, "in_o0")
                norm_pool(e, "in_o1")
                odd_pool(e)
                root_pool(e, "subln", 8, P, "subln:ss")
            if on(4):
                norm_pool(e, "moe")
            if on(5):
                norm_pool(e, "a0")
                resid2_pool(e, "ra0", 0, 0, 1, "res_m:h")
                conf_pool(e, "ra0:h")
                norm_pool(e, "in_h")
                ssm_pool(e)
                norm_pool(e, "ssm")
                resid2_pool(e, "rh", 1, 0, 3, "ra0:h")
            if on(6):
                for i, (tag, l, g_) in enumerate((("a1", 0, 5), ("b0", 1, 1))):
                    norm_pool(e, tag)
                    resid2_pool(e, "r" + tag, 2 + i, l, g_, ("ra0:h", "rh:h")[i])
                norm_pool(e, "in_at")
                dil_pool(e)
                resid2_pool(e, "rat", 4, 1, 3, "ra1:h")
                norm_pool(e, "b1")
                resid2_pool(e, "rb1", 5, 1, 5, "rb0:h")

        @block.scalar
        def _(act):
            e = Engine(act, "act")
            s = Split(act, True)
            f = FfnAct(act, s)
            setup_act(e)
            for name in ("silu_done", "turned_hi"):
                act.sem_inc(sem(name), 1)
            s.first()
            mod_act(e, s, 0)
            for st, src in enumerate((h, hc)):
                loaded(e, ("x", "ctx")[st])
                norm_act(e, src, f"in_e{st}", lambda k: scal[:, 0, k, st:st + 1],
                         lambda k: mod[:, 0, k, st:st + 1], "mod0")
                project_act(e, s, D, 6 * N, lambda t, c, n: p_e[:, st, t, c:c + n])
            even_qk_act(e)
            conv_act(e, 0)
            even_qk_out(e)
            for st in range(2):
                if st:
                    conv_act(e, 1)
                attn_act(e, ATT0[st], E_ITEMS[st])
                heads_out_act(e, f"att_e{st}")
                project_act(e, s, D, D, lambda t, c, n: y[:, t, c:c + n])
            if on(2):
                for st, src in enumerate((h, hc)):
                    norm_act(e, src, f"ff{st}", lambda k: scal[:, 1, k, st:st + 1],
                             lambda k: mod[:, 2, k, st:st + 1], f"res_e{st}:h")
                    dense(f)
            if on(3):
                mod_act(e, s, 1)
                for st, (src, dst, n) in enumerate(((h, pl, OW), (hc, pc, OW - OQ))):
                    norm_act(e, src, f"in_o{st}", lambda k: scal[:, 0, k, st:st + 1],
                             lambda k: mod[:, 0, k, st:st + 1], "mod1")
                    project_act(e, s, D, n, lambda t, c, w: dst[:, t, c:c + w])
                odd_qk_act(e)
                odd_qk_out(e)
                attn_act(e, ATT0[2], W_ITEMS)
                window_sinks_act(e)
                heads_out_act(e, "att_w", 0)
                attn_act(e, ATT0[3], D_ITEMS)
                e.after("sublng")
                heads_out_act(e, "att_d", 4, sublng[:, 0:1])
                project_act(e, s, D, D, lambda t, c, n: y[:, t, c:c + n])
            if on(4):
                norm_act(e, h, "moe", lambda k: scal[:, 1, k, 0:1], lambda k: mod[:, 2, k, 0:1], "res_o:h")
                router_act(e)
                experts(f)
            if on(5):
                norm_act(e, h, "a0", lambda k: gain_b2(0, 0)[:, k:k + 1], None, "res_m:h")
                dense(f)
                e.eng.wait_ge(sem("y_done"), f.ys.n)
                rms_act(e, y, "ra0")
                norm_act(e, h, "in_h", lambda k: gain_b2(0, 2)[:, k:k + 1], None, "ra0:h")
                project_act(e, s, D, HYB - SSM_H, lambda t, c, n: p_h[:, t, c:c + n])
                conf_act(e)
                ssm_act(e)
                norm_act(e, y, "ssm", lambda k: cols[:, 1, 96 + k:97 + k], None, "ssm y")
                project_act(e, s, 2 * D, D, lambda t, c, n: y[:, t, c:c + n])
                e.eng.wait_ge(sem("out_done"), e.outs.n)
                rms_act(e, y, "rh")
            if on(6):
                for tag, l, g_, dep in (("a1", 0, 4, "rh:h"), ("b0", 1, 0, "ra1:h")):
                    norm_act(e, h, tag, lambda k: gain_b2(l, g_)[:, k:k + 1], None, dep)
                    dense(f)
                    e.eng.wait_ge(sem("y_done"), f.ys.n)
                    rms_act(e, y, "r" + tag)
                norm_act(e, h, "in_at", lambda k: gain_b2(1, 2)[:, k:k + 1], None, "rb0:h")
                project_act(e, s, D, QKV, lambda t, c, n: p_a[:, t, c:c + n])
                dil_act(e)
                attn_act(e, ATT0[4], A_ITEMS)
                merge_act(e)
                heads_out_act(e, "att_a", 0)
                project_act(e, s, D // 2, D, lambda t, c, n: y[:, t, c:c + n])
                e.eng.wait_ge(sem("out_done"), e.outs.n)
                rms_act(e, y, "rat")
                norm_act(e, h, "b1", lambda k: gain_b2(1, 4)[:, k:k + 1], None, "rat:h")
                dense(f)
                e.eng.wait_ge(sem("y_done"), f.ys.n)
                rms_act(e, y, "rb1")

        @block.vector
        def _(dve):
            e = Engine(dve, "dve")
            s = Split(dve, False)
            f = FfnDve(dve, s)
            setup_dve(e)
            for name in ("product_ready", "turned_lo", "y_done"):
                dve.sem_inc(sem(name), 1)
            s.first()
            mod_dve(e, s, 0)
            for st, src in enumerate((h, hc)):
                norm_dve(e, src, f"in_e{st}")
                project_dve(e, s, D, 6 * N)
            e.eng.wait_ge(sem("out_done"), e.outs.n)
            even_qk_dve(e)
            conv_dve(e, 0)
            for st, src in enumerate((h, hc)):
                if st:
                    conv_dve(e, 1, )
                attn_dve(e, ATT0[st], E_ITEMS[st], None)
                heads_out_dve(e, f"att_e{st}", 16, ATT0[st])
                cut_x(e, f"cat_e{st}", f"att_e{st}:oT")
                project_dve(e, s, D, D)
                resid_dve(e, src, f"res_e{st}", e.outs.n)
            if on(2):
                for st, src in enumerate((h, hc)):
                    norm_dve(e, src, f"ff{st}")
                    dense(f)
                    resid_dve(e, src, f"res_f{st}")
            if on(3):
                mod_dve(e, s, 1)
                for st, (src, n) in enumerate(((h, OW), (hc, OW - OQ))):
                    norm_dve(e, src, f"in_o{st}")
                    project_dve(e, s, D, n)
                e.eng.wait_ge(sem("out_done"), e.outs.n)
                odd_qk_dve(e)
                attn_dve(e, ATT0[2], W_ITEMS, lambda i: nsink[:, i // NT:i // NT + 1])
                window_sinks_dve(e, ATT0[2])
                heads_out_dve(e, "att_w", 16, ATT0[2])
                attn_dve(e, ATT0[3], D_ITEMS, None)
                diff_out_dve(e, ATT0[3])
                cut_x(e, "cat_o", "att_w:oT", "att_d:oT")
                project_dve(e, s, D, D)
                resid_dve(e, h, "res_o", e.outs.n)
            if on(4):
                norm_dve(e, h, "moe")
                router_dve(e)
                experts(f)
                resid_dve(e, h, "res_m")
            if on(5):
                norm_dve(e, h, "a0")
                dense(f)
                resid2_dve(e, "ra0", 0, 0.5)
                norm_dve(e, h, "in_h")
                dt_dve(e)
                project_dve(e, s, D, HYB - SSM_H)
                e.eng.wait_ge(sem("out_done"), e.outs.n)
                conf_dve(e)
                ssm_dve(e)
                norm_dve(e, y, "ssm", (R_G2["x2hi"], R_G2["x2lo"]))
                project_dve(e, s, 2 * D, D)
                resid2_dve(e, "rh", 1, 1.0)
            if on(6):
                for i, tag in enumerate(("a1", "b0")):
                    norm_dve(e, h, tag)
                    dense(f)
                    resid2_dve(e, "r" + tag, 2 + i, 0.5)
                norm_dve(e, h, "in_at")
                project_dve(e, s, D, QKV)
                every, raw_take = dil_every(e, ATT0[4])
                attn_dve(e, ATT0[4], A_ITEMS, None, every=every)
                raw_take(5)
                merge_dve(e, ATT0[4])
                cut_x(e, "cat_a", "att_a:oT", tiles_=4)
                project_dve(e, s, D // 2, D)
                resid2_dve(e, "rat", 4, 1.0)
                norm_dve(e, h, "b1")
                dense(f)
                resid2_dve(e, "rb1", 5, 0.5)
            e.link(nc.vector.tensor_copy(seed[:, 1:2], seed[:, 0:1]), "final")

        @block.tensor
        def _(pe):
            e = Engine(pe, "pe")
            s = Use(pe)
            f = FfnPe(pe, s)
            pe.sem_inc(sem("turned"), 1)
            setup_pe(e)
            mod_pe(e, s, 0, f)
            for st in range(2):
                norm_pe(e, f"in_e{st}")
                e.after(f"in_e{st}:x")
                project_pe(e, s, [(xhi, xlo, KD)], 6 * N, f"in_e{st}")
            e.eng.wait_ge(sem("out_done"), e.outs.n)
            conv_pe(e, 0)
            even_qk_pe(e)
            for st in range(2):
                if st:
                    conv_pe(e, 1)

                def ready(e, i):
                    if st == 0 and i % NT == 0:
                        e.after(f"bias{i // NT}")
                attn_pe(e, ATT0[st], E_ITEMS[st], ready, "qkT1", f"convT{st}")
                heads_out_pe(e, f"att_e{st}")
                e.after(f"cat_e{st}")
                project_pe(e, s, [(xhi, xlo, KD)], D, f"out_e{st}")
                resid_pe(e, f"res_e{st}", (pick_lat, pick_ctx)[st], 0)
            if on(2):
                for st in range(2):
                    norm_pe(e, f"ff{st}")
                    e.after(f"ff{st}:x")
                    dense(f)
                    resid_pe(e, f"res_f{st}", (pick_lat, pick_ctx)[st], 1)
            if on(3):
                mod_pe(e, s, 1, f)
                for st, n in enumerate((OW, OW - OQ)):
                    norm_pe(e, f"in_o{st}")
                    e.after(f"in_o{st}:x")
                    project_pe(e, s, [(xhi, xlo, KD)], n, f"in_o{st}")
                odd_qk_pe(e)
                attn_pe(e, ATT0[2], W_ITEMS, None, "ckT", "dkT")
                heads_out_pe(e, "att_w")
                attn_pe(e, ATT0[3], D_ITEMS, None, "att_w:oT")
                heads_out_pe(e, "att_d")
                e.after("cat_o")
                project_pe(e, s, [(xhi, xlo, KD)], D, "out_o")
                resid_pe(e, "res_o", pick_lat, 0)
            if on(4):
                norm_pe(e, "moe")
                e.after("moe:x")
                router_pe(e)
                experts(f)
                resid_pe(e, "res_m", pick_lat, 1)
            if on(5):
                norm_pe(e, "a0", "res_m:h")
                e.after("a0:x")
                dense(f)
                norm_pe(e, "in_h")
                e.after("in_h:x")
                head_pe(e)
                project_pe(e, s, [(xhi, xlo, KD)], HYB - SSM_H, "in_h")
                e.eng.wait_ge(sem("out_done"), e.outs.n)
                conf_pe(e)
                ssm_pe(e)
                norm_pe(e, "ssm")
                e.after("ssm:x")
                project_pe(e, s, [(xhi, xlo, KD), (R_G2["x2hi"], R_G2["x2lo"], KD)], D, "out_h")
            if on(6):
                for tag in ("a1", "b0"):
                    norm_pe(e, tag)
                    e.after(tag + ":x")
                    dense(f)
                norm_pe(e, "in_at")
                e.after("in_at:x")
                project_pe(e, s, [(xhi, xlo, KD)], QKV, "in_at")
                dil_pe(e)
                attn_pe(e, ATT0[4], A_ITEMS, lambda e, i: e.after(f"raw{i // 8 - 2}") if i % 8 == 0 and i >= 16
                        else None, "dilqk2", "masks")
                heads_out_pe(e, "att_a")
                e.after("cat_a")
                project_pe(e, s, [(xhi, xlo, KD // 2)], D, "out_a")
                norm_pe(e, "b1")
                e.after("b1:x")
                dense(f)


def kernel(**inputs):
    import concourse.bacc as bacc
    from concourse.bass_utils import run_bass_kernel_spmd as run

    arrays = {k: np.ascontiguousarray(v) for k, v in inputs.items()}
    arrays.update(constants())
    rows, width = TOK // 64, 64
    r, c = np.arange(rows), np.arange(width)
    dr = np.clip(np.arange(rows)[None, :] - r[:, None] + 7, 0, 14)
    dc = np.clip(c[None, :] - c[:, None] + 15, 0, 30)
    laid = arrays["ev_rpb"][0][:, dr[:, None, :, None], dc[None, :, None, :]]
    laid = laid.reshape(8, NT, P, TOK).transpose(0, 2, 1, 3)
    arrays["k_rpb"] = np.ascontiguousarray(laid.reshape(8, P, NT * TOK))

    def build(plan):
        nc = bacc.Bacc("TRN2", target_bir_lowering=False, num_devices=1)
        aps = {k: nc.dram_tensor(f"in_{k}", v.shape, mybir.dt.from_np(v.dtype), kind="ExternalInput").ap()
               for k, v in arrays.items()}
        o = nc.dram_tensor("out_0", (1, TOK, D), F32, kind="ExternalOutput").ap()
        program(nc, aps, o, plan)
        return nc

    plan = {"old": {}, "dry": True, "stop": STOP}
    build(plan)
    plan = {"old": plan["new"], "dry": False, "stop": STOP}
    nc = build(plan)
    res = run(nc, [{f"in_{k}": v for k, v in arrays.items()}], core_ids=[0])
    return res.results[0]["out_0"]
```

```python
from contextlib import ExitStack

import concourse.bass as bass
from concourse import mybir
import numpy as np

F32 = mybir.dt.float32
F32R = mybir.dt.float32r
ACT = mybir.ActivationFunctionType
ALU = mybir.AluOpType
AX = mybir.AxisListType

P = 128
TOK = 256
NT = TOK // P
D = 1024
KD = D // P
N = 512
HD = 64
RAWS = 4
EPS = 1e-6
LAM_INIT = 0.8 - 0.6 * float(np.exp(-0.3))
FF = 2816
FE = 1408
EXPERTS = 8
HYB = 4624
TAPS = 31
SSM_H = 16
STOP = 99


class Count:

    def __init__(self, n=0):
        self.n = n
        self.turn = None
        self.per = 0

    def at(self, ahead=0):
        if self.turn is None:
            return self.n + ahead
        return self.turn * self.per + (self.n + ahead)


def twice(count, ahead):
    if count.turn is None:
        return 2 * count.n + ahead
    return count.turn * (2 * count.per) + (2 * count.n + ahead)


class Turns:

    def __init__(self, turn, times, counts):
        self.times = times
        self.start = [(c, c.n, per) for c, per in counts]
        for c, per in counts:
            c.turn, c.per = turn, per

    def end(self):
        for c, n, per in self.start:
            assert c.n == n + per, (c.n, n, per)
            c.turn, c.n = None, n + per * self.times


class Chain:

    def __init__(self, eng, sem, plan, key):
        self.eng, self.sem, self.plan, self.key, self.n = eng, sem, plan, key, 0

    def put(self, ins, name=None):
        ins.then_inc(self.sem, 1)
        self.n += 1
        for each in name if isinstance(name, tuple) else (name,):
            if each:
                self.plan["new"][each] = (self.key, self.n)
        return ins

    def link(self, ins, name=None):
        self.put(ins, name)
        self.eng.wait_ge(self.sem, self.n)


def constants():
    i = np.arange(P)
    ident = np.eye(P)
    upto = (i[:, None] <= i[None, :]) * 1.0
    after = (i[:, None] > i[None, :]) * 1.0
    pick = np.zeros((P, 2))
    pick[[0, 2, 4], 0] = 1
    pick[[1, 3, 4], 1] = 1
    lat = np.repeat(pick[:, 0:1], P, 1)
    ctx = np.repeat(pick[:, 1:2], P, 1)
    e = np.arange(EXPERTS)
    before = np.broadcast_to((e[None, :] < e[:, None]).reshape(1, -1) * 1.0, (P, EXPERTS * EXPERTS))
    base = np.concatenate([ident, upto, after, lat, ctx, before, pick], 1)
    tok = np.arange(TOK).reshape(NT, P).T
    key = np.arange(TOK)
    col, kcol = tok % 64, key % 64
    c0 = np.clip(col - 8, 0, 64 - 16)
    near = np.where((kcol >= c0[..., None]) & (kcol < c0[..., None] + 16), 0.0, -1e30)
    band = np.where(np.abs(key - tok[..., None]) <= 128, 0.0, -1e30)
    inv = np.float32(10000.0) ** (-np.arange(16, dtype=np.float32) / np.float32(16))
    pos = np.stack([tok // 64, tok % 64], -1).astype(np.float32)
    ang = pos[..., None] * inv.astype(np.float32)
    cos, sin = np.cos(ang), np.sin(ang)
    ropec = np.stack([cos, cos], -2).reshape(P, NT * HD)
    ropes = np.stack([-sin, sin], -2).reshape(P, NT * HD)
    rel = tok[..., None] - key
    dist = -np.maximum(rel, 0)
    dil = [np.where((rel >= 0) & (rel % d == 0) & (rel // d <= 128), 0.0, -1e30) for d in (1, 4, 16)]
    flat = lambda a: np.ascontiguousarray(np.asarray(a, np.float32).reshape(P, -1))
    return {
        "k_base": flat(base), "k_near": flat(near), "k_band": flat(band),
        "k_rope": flat(np.concatenate([ropec, ropes], 1)), "k_dist": flat(dist),
        "k_dil": flat(np.stack(dil, 1)),
    }


def program(nc, a, out, plan):
    plan["new"] = {}
    old = plan["old"]
    ctx = ExitStack()
    sems = {}

    def sem(name):
        if name not in sems:
            sems[name] = ctx.enter_context(nc.semaphore(name))
        return sems[name]

    def sb(name, shape, dt=F32):
        return ctx.enter_context(nc.sbuf_tensor(name, shape, dt))

    h = sb("h", [P, NT, D])
    hc = sb("hc", [P, NT, D])
    y = sb("y", [P, NT, D])
    raw = [sb(f"raw{i}", [P, 4, N]) for i in range(RAWS)]
    whi = [sb(f"whi{i}", [P, 2, N], F32R) for i in range(4)]
    wlo = [sb(f"wlo{i}", [P, 2, N], F32R) for i in range(4)]
    xhi = sb("xhi", [P, KD, TOK], F32R)
    xlo = sb("xlo", [P, KD, TOK], F32R)
    tmp = sb("tmp", [P, NT, D])
    gates = sb("gates", [P, 2, D])
    spad = sb("spad", [P, KD, P], F32R)
    kb = sb("kb", [P, 5 * P + 64 + 2])
    ident, upto, after = kb[:, 0:P], kb[:, P:2 * P], kb[:, 2 * P:3 * P]
    pick_lat, pick_ctx = kb[:, 3 * P:4 * P], kb[:, 4 * P:5 * P]
    before = kb[:, 5 * P:5 * P + 64]
    pick = kb[:, 5 * P + 64:5 * P + 66]
    cols = sb("cols", [P, 5, P])
    mod = sb("mod", [P, 4, KD, 2])
    scal = sb("scal", [P, 2, KD, 2])
    ss = sb("ss", [P, 96])
    negm = sb("negm", [P, 64])
    den = sb("den", [P, 64])
    mhalf = sb("mhalf", [P, 96])
    seed = sb("seed", [P, 2])
    logits = sb("logits", [P, NT, EXPERTS])
    rank = sb("rank", [P, NT, EXPERTS])
    gate = sb("gate", [P, NT, EXPERTS])
    dtraw = sb("dtraw", [P, NT, SSM_H])
    ones = sb("ones", [P, P])
    epsc = sb("epsc", [P, 1])
    onec = sb("onec", [P, 1])
    top = sb("top", [P, NT, 8])
    cmp = sb("cmp", [P, EXPERTS * EXPERTS])
    cmp2 = sb("cmp2", [P, EXPERTS * EXPERTS])
    small = {n: sb(n, [P, w]) for n, w in (("lamv", 4 * HD), ("lame", 4), ("sink", 8), ("nsink", 8),
                                           ("sinke", 16), ("sublng", 1), ("router", KD * EXPERTS), ("vtop", 8))}
    layouts = []

    def region(prefix, **parts):
        inner = ExitStack()
        got = {}
        for name, (shape, dt) in parts.items():
            got[name] = inner.enter_context(nc.sbuf_tensor(f"{prefix}_{name}", shape, dt))
        inner.close()
        layouts.append(got)
        return got

    R_S = region("s", mr=([P, 2 * D], F32), prm=([P, 5, P], F32), srow=([P, P], F32),
                 ssig=([P, 2 * KD], F32))
    R_F = region("f", hhi=([P, FF // P, TOK], F32R), hlo=([P, FF // P, TOK], F32R))
    R_E = region("e", p=([P, 2, NT, 6 * N], F32), qT=([P, 4, 2 * TOK], F32), kT=([P, 4, 2 * TOK], F32),
                 cT=([P, 4, TOK + 2], F32), bias=([P, 2, NT, TOK], F32), gqk=([P, 2 * HD], F32))
    OW = 2304
    OQ, QK = 1024, 1792
    R_O = region("o", pl=([P, NT, OW], F32), pc=([P, NT, OW - OQ], F32), sq=([P, NT, QK], F32),
                 gain=([P, QK], F32), qT=([P, 8, TOK], F32), kT=([P, 6, 2 * TOK], F32),
                 band=([P, NT, TOK], F32), rope=([P, 2, NT, HD], F32))
    R_H = region("h", p=([P, NT, HYB], F32), pad=([P, KD, TOK + TAPS - 1], F32), hid=([P, KD, TOK], F32),
                 xhead=([P, KD, SSM_H], F32), mu=([P, TOK], F32), rstd=([P, TOK], F32))
    R_G = region("g", p=([P, NT, HYB], F32), pad=([P, 12, TOK + 3], F32), xc=([P, 12, TOK], F32),
                 a1=([P, 2, 4, P], F32), dt=([P, 6, NT, SSM_H], F32), row=([P, 3, SSM_H], F32),
                 dec=([P, 2, SSM_H], F32))
    R_G2 = region("g2", p=([P, NT, HYB], F32), x2hi=([P, KD, TOK], F32R), x2lo=([P, KD, TOK], F32R))
    QKV = 4608
    R_A = region("a", p=([P, NT, QKV], F32), qT=([P, 12, TOK], F32), kT=([P, 12, TOK], F32),
                 dist=([P, NT, TOK], F32R), dil=([P, 3, NT, TOK], F32R), slope=([P, 8, P], F32R),
                 one=([P, P], F32R))
    psum = [ctx.enter_context(nc.psum_tensor(f"bank{i}", [P, N], F32)) for i in range(8)]
    G, U, O, T = psum[0:2], psum[2:4], psum[4:6], psum[6:8]

    params = R_S["prm"]
    vec = lambda ap: ap.rearrange("(r c) -> r c", c=P)
    prm_src = [
        (0, 0, a["norm1_g"].rearrange("l (r c) -> (l r) c", c=P)),
        (0, 16, a["norm2_g"].rearrange("l (r c) -> (l r) c", c=P)),
        (0, 32, a["norm_g_2"].rearrange("l s (r c) -> (l s r) c", c=P)),
        (1, 0, a["ev_conv_w"][0].rearrange("j (r c) -> (j r) c", c=P)),
        (1, 12, vec(a["conv_dw_b_2"][0])),
        (1, 20, vec(a["conv_ln_g_2"][0])),
        (1, 28, vec(a["conv_ln_b_2"][0])),
        (1, 36, a["ssm_conv_w_2"][0].rearrange("j (r c) -> (j r) c", c=P)),
        (1, 84, vec(a["ssm_conv_b_2"][0])),
        (1, 96, vec(a["ssm_norm_g_2"][0])),
        (1, 104, a["od_subln_g"]),
        (2, 0, a["conv_dw_w_2"][0, 0:16].rearrange("j (r c) -> (j r) c", c=P)),
        (3, 0, a["conv_dw_w_2"][0, 16:TAPS].rearrange("j (r c) -> (j r) c", c=P)),
    ]
    prm_rows = [128, 105, 128, 120]
    gain1 = lambda l: cols[:, 0, 8 * l:8 * l + 8]
    gain2 = lambda l: cols[:, 0, 16 + 8 * l:24 + 8 * l]
    gain_b2 = lambda l, s: cols[:, 0, 32 + 48 * l + 8 * s:40 + 48 * l + 8 * s]

    def tiles(w, k0, kt, c0, n):
        return w[k0 * P:(k0 + kt) * P, c0:c0 + n].rearrange("(k p) n -> p k n", p=P)

    class Load:

        def __init__(self, eng):
            self.eng, self.r = eng, Count()

        def unit(self, src, kt, n):
            slot = self.r.n % RAWS
            if self.r.n >= RAWS:
                self.eng.wait_ge(sem("w_lo"), twice(self.r, 2 - 2 * RAWS))
            to = raw[slot][:, 0:3:2, 0:n] if kt == 2 else raw[slot][:, 0:kt, 0:n]
            self.eng.dma_start(to, src).then_inc(sem(f"raw_in{slot}"), 16)
            self.r.n += 1

        def columns(self, w, k, c0, n):
            for k0 in range(0, k // P, 4):
                self.unit(tiles(w, k0, 4, c0, n), 4, n)

    class Split:

        def __init__(self, eng, high):
            self.eng, self.high = eng, high
            self.r = Count()
            self.used = Count()
            self.total = old.get("units", (0, 10 ** 6))[1]
            self.beside, self.steps = None, 0

        def with_(self, beside):
            self.beside, self.steps = beside, 0

        def half(self, j):
            if self.r.turn is None and self.r.n >= self.total:
                return
            slot, s = self.r.n % RAWS, (2 * self.r.n + j) % 4
            if self.high:
                if j == 0:
                    v = 16 * (self.r.n // RAWS + 1)
                    if self.r.turn is not None:
                        v = self.r.turn * (16 * self.r.per // RAWS) + v
                    self.eng.wait_ge(sem(f"raw_in{slot}"), v)
                if 2 * self.r.n + j >= 4:
                    self.eng.wait_ge(sem("w_used"), twice(self.r, j - 3))
                nc.scalar.activation(whi[s][:, :, :], raw[slot][:, 2 * j:2 * j + 2, :], ACT.Copy)\
                    .then_inc(sem("w_hi"), 1)
            else:
                self.eng.wait_ge(sem("w_hi"), twice(self.r, j + 1))
                nc.vector.tensor_tensor(wlo[s][:, :, :], raw[slot][:, 2 * j:2 * j + 2, :],
                                        whi[s][:, :, :].bitcast(F32), ALU.subtract)\
                    .then_inc(sem("w_lo"), 1)

        def step(self, between=None):
            self.half(0)
            self.used.n += 1
            if between:
                self.eng.wait_ge(sem("w_used"), twice(self.used, 0))
                between()
            self.half(1)
            self.r.n += 1
            if self.beside:
                self.beside(self.steps)
                self.steps += 1

        def first(self):
            for _ in range(2):
                self.half(0)
                self.half(1)
                self.r.n += 1

    class Use:

        def __init__(self, eng):
            self.eng, self.r = eng, Count()
            self.needs = {}

        def unit(self, xh, xl, k0, kt, n, banks, start, stop):
            cut = 1 if kt == 2 else 2
            for j, (b0, b1) in enumerate(((0, cut), (cut, kt))):
                s = (2 * self.r.n + j) % 4
                self.eng.wait_ge(sem("w_lo"), twice(self.r, j + 1))
                need = self.needs.pop(k0 + b0, None)
                if need:
                    need()
                for t, bank in enumerate(banks):
                    for k in range(b0, b1):
                        tok = slice(t * P, t * P + P)
                        xk_h, xk_l = xh[:, k0 + k, tok], xl[:, k0 + k, tok] if xl is not None else None
                        wk = k - b0
                        first = start and k == 0
                        last = stop and k == kt - 1
                        nc.tensor.matmul(bank[:, 0:n], xk_h, whi[s][:, wk, 0:n], start=first, stop=False)
                        ins = nc.tensor.matmul(bank[:, 0:n], xk_h, wlo[s][:, wk, 0:n], start=False,
                                               stop=last and xl is None)
                        if xl is not None:
                            ins = nc.tensor.matmul(bank[:, 0:n], xk_l, whi[s][:, wk, 0:n], start=False,
                                                   stop=last)
                ins.then_inc(sem("w_used"), 1)
            self.r.n += 1

    FFN_SEMS = ("silu_done", "product_ready", "turned", "turned_hi", "turned_lo", "y_done")

    def widths(f):
        return [N] * (f // N) + ([f % N] if f % N else [])

    def spans(k):
        step = 3 if k == FE // P else 4
        return [(k0, min(step, k - k0)) for k0 in range(0, k, step)]

    PER_PAIR, PER_EXPERT = 4, 4 * len(widths(FE)) + 2 * len(spans(FE // P))
    assert PER_EXPERT % RAWS == 0 and PER_PAIR % RAWS == 0
    hs = tmp[:, :, N:2 * N]
    sg = tmp[:, :, 0:N]
    hhi, hlo = R_F["hhi"], R_F["hlo"]

    def load_ffn(ld, w1, w3, w2, f):
        ws = widths(f)

        def pair(c0, n):
            for w in (w1, w3):
                ld.columns(w, D, c0, n)

        full = f // N
        pair(0, N)
        if f == FF:
            with ld.eng.Fori(1, full) as i:
                turns = Turns(i - 1, full - 1, [(ld.r, PER_PAIR)])
                for w in (w1, w3):
                    for k0 in (0, 4):
                        src = w[k0 * P:(k0 + 4) * P, bass.ds(i * N, N)].rearrange("(k p) n -> p k n", p=P)
                        ld.unit(src, 4, N)
                turns.end()
            pair(full * N, f % N)
        else:
            for j, n in enumerate(ws[1:]):
                pair((j + 1) * N, n)
        for c in range(2):
            for k0, kt in spans(f // P):
                ld.unit(tiles(w2, k0, kt, c * N, N), kt, N)

    class Ffn:

        def __init__(self, eng, stream):
            self.eng, self.s = eng, stream
            self.pairs, self.ys = Count(1), Count(1)

        def counts(self, per, pairs, ys):
            c = [(self.s.r, per), (self.pairs, pairs), (self.ys, ys)]
            if isinstance(self.s, Split):
                c.append((self.s.used, per))
            return c

    class FfnPe(Ffn):
        def turn_over(self, n):
            self.eng.wait_ge(sem("product_ready"), self.pairs.at(0))
            self.eng.wait_ge(sem("turned_lo"), self.pairs.at(-1))
            for f in range(n // P):
                for t in range(NT):
                    c = (f % 2) * TOK + t * P
                    ins = nc.tensor.transpose(T[f // 2][:, c:c + P], hs[:, t, f * P:f * P + P], ident)
            ins.then_inc(sem("turned"), 1)

        def pair(self, n, former):
            self.eng.wait_ge(sem("silu_done"), self.pairs.at(0))
            self.s.unit(xhi, xlo, 0, 4, n, G, True, False)
            if former:
                self.turn_over(former)
            self.s.unit(xhi, xlo, 4, 4, n, G, False, True)
            self.eng.wait_ge(sem("product_ready"), self.pairs.at(0))
            self.eng.wait_ge(sem("y_done"), self.ys.at(0))
            self.s.unit(xhi, xlo, 0, 4, n, U, True, False)
            self.s.unit(xhi, xlo, 4, 4, n, U, False, True)
            self.pairs.n += 1

        def down(self, f):
            ws = widths(f)
            last_tile = (len(ws) - 1) * 4
            for c, banks in enumerate((O, U)):
                self.eng.wait_ge(sem("y_done"), self.ys.at(0))
                if c == 1:
                    self.eng.wait_ge(sem("product_ready"), self.pairs.at(0))
                for n, (k0, kt) in enumerate(spans(f // P)):
                    if c == 0:
                        self.eng.wait_ge(sem("turned_lo"), self.pairs.at(0 if k0 + kt > last_tile else -1))
                    self.s.unit(hhi, hlo, k0, kt, N, banks, n == 0, k0 + kt == f // P)
                    if c == 0 and n == 0:
                        self.turn_over(ws[-1])
            self.ys.n += 2

    class FfnAct(Ffn):
        def turned_hi(self, n, tile):
            def work():
                self.eng.wait_ge(sem("turned"), self.pairs.at(0))
                if not isinstance(tile, int):
                    self.eng.wait_ge(sem("turned"), 1)
                for b in range(0, n, TOK):
                    k = min(2, (n - b) // P)
                    at = slice(tile + b // P, tile + b // P + k) if isinstance(tile, int) \
                        else bass.ds(tile + b // P, k)
                    ins = nc.scalar.activation(hhi[:, at, :].rearrange("p k t -> p (k t)"),
                                               T[b // TOK][:, 0:k * TOK], ACT.Copy)
                ins.then_inc(sem("turned_hi"), 1)
            return work

        def pair(self, n, former, tile):
            def silu():
                self.eng.wait_ge(sem("product_ready"), self.pairs.at(0))
                for t in range(NT):
                    ins = nc.scalar.activation(sg[:, t, 0:n], G[t][:, 0:n], ACT.Silu)
                ins.then_inc(sem("silu_done"), 1)

            self.s.step(self.turned_hi(former, tile) if former else None)
            self.s.step(silu)
            self.s.step()
            self.s.step()
            self.pairs.n += 1

        def down(self, f):
            ws = widths(f)
            for c in range(2):
                for n, _ in enumerate(spans(f // P)):
                    self.s.step(self.turned_hi(ws[-1], (len(ws) - 1) * 4) if c == n == 0 else None)
            self.ys.n += 2

    class FfnDve(Ffn):
        def turned_lo(self, n, tile):
            def work():
                self.eng.wait_ge(sem("turned_hi"), self.pairs.at(0))
                for b in range(0, n, TOK):
                    k = min(2, (n - b) // P)
                    at = slice(tile + b // P, tile + b // P + k) if isinstance(tile, int) \
                        else bass.ds(tile + b // P, k)
                    flat = "p k t -> p (k t)"
                    ins = nc.vector.tensor_tensor(hlo[:, at, :].rearrange(flat), T[b // TOK][:, 0:k * TOK],
                                                  hhi[:, at, :].bitcast(F32).rearrange(flat), ALU.subtract)
                ins.then_inc(sem("turned_lo"), 1)
            return work

        def pair(self, n, former, tile, gate_of=None):
            def product():
                self.eng.wait_ge(sem("silu_done"), self.pairs.at(1))
                for t in range(NT):
                    if gate_of is None:
                        ins = nc.vector.tensor_tensor(hs[:, t, 0:n], sg[:, t, 0:n], U[t][:, 0:n], ALU.mult)
                    else:
                        ins = nc.vector.scalar_tensor_tensor(
                            out=hs[:, t, 0:n], in0=sg[:, t, 0:n], scalar=gate[:, t, bass.ds(gate_of, 1)],
                            in1=U[t][:, 0:n], op0=ALU.mult, op1=ALU.mult)
                ins.then_inc(sem("product_ready"), 1)

            self.s.step(self.turned_lo(former, tile) if former else None)
            self.s.step()
            self.s.step()
            self.s.step(product)
            self.pairs.n += 1

        def down(self, f, add):
            ws = widths(f)
            last = len(spans(f // P)) - 1
            for c, banks in enumerate((O, U)):
                def half_of_y():
                    for t in range(NT):
                        part = y[:, t, c * N:c * N + N]
                        if add:
                            ins = nc.vector.tensor_tensor(part, part, banks[t][:, :], ALU.add)
                        else:
                            ins = nc.vector.tensor_copy(part, banks[t][:, :])
                    ins.then_inc(sem("y_done"), 1)
                for n, _ in enumerate(spans(f // P)):
                    self.s.step(self.turned_lo(ws[-1], (len(ws) - 1) * 4) if c == n == 0
                                else half_of_y if n == last else None)
            self.ys.n += 2

    def dense(side):
        pe = isinstance(side, FfnPe)
        full = FF // N
        side.pair(*((N, None) if pe else (N, None, 0)))
        with side.eng.Fori(1, full) as i:
            turns = Turns(i - 1, full - 1, side.counts(PER_PAIR, 1, 0))
            side.pair(*((N, N) if pe else (N, N, (i - 1) * 4)))
            turns.end()
        side.pair(*((FF % N, N) if pe else (FF % N, N, (full - 1) * 4)))
        side.down(*((FF, False) if isinstance(side, FfnDve) else (FF,)))

    def experts(side):
        pe, dve = isinstance(side, FfnPe), isinstance(side, FfnDve)
        with side.eng.Fori(0, EXPERTS) as e:
            turns = Turns(e, EXPERTS, side.counts(PER_EXPERT, len(widths(FE)), 2))
            former = None
            for j, n in enumerate(widths(FE)):
                side.pair(*((n, former) if pe else (n, former, 4 * (j - 1)) + ((e,) if dve else ())))
                former = n
            side.down(*((FE, True) if dve else (FE,)))
            turns.end()

    class Engine:
        def __init__(self, eng, key):
            self.eng, self.key = eng, key
            self.chain = Chain(eng, sem(f"{key}_done"), plan, key)
            self.put, self.link = self.chain.put, self.chain.link
            self.outs = Count()

        def after(self, *names):
            for name in names:
                if plan["dry"]:
                    continue
                key, n = old[name]
                self.eng.wait_ge(sem(f"{key}_done"), n)

    def project_load(ld, w, k, cols_, first=0, extra=None):
        for i, c0 in enumerate(range(0, cols_, N)):
            ld.columns(w, k, first + c0, min(N, cols_ - c0))
            if extra:
                extra(i)

    def project_pe(e, s, xs, cols_, tag, extra=None):
        for c in range(0, cols_, N):
            n = min(N, cols_ - c)
            if e.outs.n >= 3:
                e.eng.wait_ge(sem("out_done"), e.outs.n - 2)
            total = sum(k for _, _, k in xs)
            done = 0
            for xh, xl, k in xs:
                for k0 in range(0, k, 4):
                    s.unit(xh, xl, k0, 4, n, (G, U, O)[e.outs.n % 3], done == 0, done + 4 == total)
                    done += 4
            e.outs.n += 1
            if extra:
                extra(c // N)

    def project_act(e, s, k, cols_, to, extra=None):
        for c in range(0, cols_, N):
            n = min(N, cols_ - c)
            banks = (G, U, O)[e.outs.n % 3]

            def take():
                for t in range(NT):
                    ins = nc.scalar.activation(to(t, c, n), banks[t][:, 0:n], ACT.Copy)
                ins.then_inc(sem("out_done"), 1)
            for u in range(k // P // 4):
                s.step(take if u == k // P // 4 - 1 else None)
            e.outs.n += 1
            if extra:
                extra(c // N)

    def project_dve(e, s, k, cols_, extra=None):
        for c in range(0, cols_, N):
            for u in range(k // P // 4):
                s.step()
            e.outs.n += 1
            if extra:
                extra(c // N)

    def tiled(dep, t):
        return dep + str(t) if dep.endswith(":h") else dep

    def rms_act(e, src, tag, *deps):
        for t in range(NT):
            e.after(*(tiled(dep, t) for dep in deps))
            e.put(nc.scalar.activation(tmp[:, t, :], src[:, t, :], ACT.Square, accum_out=ss[:, t:t + 1]),
                  f"{tag}:ss{t}")

    def root_pool(e, tag, c0, c1, width, dep):
        e.after(dep)
        s_ = ss[:, c0:c1]
        e.link(nc.gpsimd.tensor_scalar(s_, s_, 1.0 / width, EPS, ALU.mult, ALU.add))
        e.link(nc.gpsimd.tensor_tensor(s_, s_, mhalf[:, c0:c1], ALU.pow), tag + ":root")

    def roots_pool(e, tag):
        for t in range(NT):
            e.after(f"{tag}:ss{t}")
            s_ = ss[:, t:t + 1]
            e.link(nc.gpsimd.tensor_scalar(s_, s_, 1.0 / D, EPS, ALU.mult, ALU.add))
            e.link(nc.gpsimd.tensor_tensor(s_, s_, mhalf[:, t:t + 1], ALU.pow), f"{tag}:root{t}")

    xf = y[:, :, :].rearrange("p t d -> p (t d)").rearrange("p (k c) -> p k c", k=KD)

    def norm_banks(e, projection):
        if not projection:
            return U + O
        pairs = [G, U, O]
        pairs.pop(e.outs.n % 3)
        return pairs[0] + pairs[1]

    def norm_act(e, src, tag, scale, shift, *deps):
        banks = norm_banks(e, tag[:3] == "in_")
        rms_act(e, src, tag, *deps)
        for k in range(KD):
            if k % 2 == 0:
                e.after(f"{tag}:xT{k // 2}")
            bank = banks[k // 2][:, (k % 2) * TOK:(k % 2) * TOK + TOK]
            bias = shift(k) if shift else 0.0
            e.put(nc.scalar.activation(xf[:, k, :], bank, ACT.Identity, bias=bias, scale=scale(k)),
                  f"{tag}:xf{k}")

    def norm_pool(e, tag):
        roots_pool(e, tag)

    def norm_dve(e, src, tag, to=None):
        hi, lo = to or (xhi, xlo)
        for t in range(NT):
            e.after(f"{tag}:root{t}")
            e.put(nc.vector.tensor_scalar(tmp[:, t, :], src[:, t, :], ss[:, t:t + 1], None, ALU.mult),
                  f"{tag}:xn{t}")
        for b in range(4):
            e.after(f"{tag}:xf{b * 2 + 1}")
            sl = slice(b * 2, b * 2 + 2)
            flat = "p k t -> p (k t)"
            e.link(nc.vector.tensor_copy(hi[:, sl, :].rearrange(flat), xf[:, sl, :].rearrange(flat)))
            e.put(nc.vector.tensor_tensor(lo[:, sl, :].rearrange(flat), xf[:, sl, :].rearrange(flat),
                                          hi[:, sl, :].bitcast(F32).rearrange(flat), ALU.subtract),
                  (f"{tag}:x{b}", tag + ":x"))

    def norm_pe(e, tag, *deps):
        banks = norm_banks(e, tag[:3] == "in_")
        e.after(*deps)
        for t in range(NT):
            e.after(f"{tag}:xn{t}")
            for b in range(4):
                for k in range(2):
                    c = k * TOK + t * P
                    kk = 2 * b + k
                    ins = nc.tensor.transpose(banks[b][:, c:c + P], tmp[:, t, kk * P:kk * P + P], ident)
                if t == NT - 1:
                    e.put(ins, f"{tag}:xT{b}")

    def follow(e, s, tag, pairs=4):
        for b in range(pairs):
            s.needs[2 * b] = lambda b=b: e.after(f"{tag}:x{b}")

    def resid_pe(e, tag, pick_, g, *deps):
        e.after(*deps)
        for c in range(2):
            ins = nc.tensor.matmul(psum[6 + c][:, :], pick_[0:5, :], gates[0:5, g, c * N:c * N + N],
                                   start=True, stop=True)
        e.put(ins, tag + ":gate")

    def resid_dve(e, hh, tag, outs=None):
        e.after(tag + ":gate")
        if outs is not None:
            e.eng.wait_ge(sem("out_done"), outs)
        else:
            e.link(nc.vector.tensor_copy(seed[:, 1:2], seed[:, 0:1]))
        for t in range(NT):
            for c in range(2):
                part = y[:, t, c * N:c * N + N]
                e.put(nc.vector.tensor_tensor(part, part, psum[6 + c][:, :], ALU.mult))
            e.eng.wait_ge(e.chain.sem, e.chain.n)
            e.link(nc.vector.tensor_tensor(hh[:, t, :], hh[:, t, :], y[:, t, :], ALU.add),
                   (f"{tag}:h{t}", tag + ":h"))

    srow, ssig, mr = (R_S[n] for n in ("srow", "ssig", "mr"))

    def side_load(e, dst, src, name):
        e.eng.dma_start(dst, src).then_inc(sem("in_" + name), 16)

    def loaded(e, name, n=1):
        e.eng.wait_ge(sem("in_" + name), 16 * n)

    def setup_pool(e):
        side_load(e, kb[:, :], a["k_base"], "base")
        side_load(e, srow[0:8, :], a["c"].rearrange("o (r c) -> (o r) c", c=P), "c")
        side_load(e, srow[8:16, :], a["c_ctx"].rearrange("(r c) -> r c", c=P), "c")
        for tile, row, src in prm_src:
            side_load(e, params[row:row + src.shape[0], tile, :], src, "params")
        for n, t in (("x", h), ("ctx", hc)):
            side_load(e, t[:, :, :], a[n][0].rearrange("(t p) d -> p t d", p=P), n)
        e.link(nc.gpsimd.memset(mhalf[:, :], -0.5), "mhalf")

    def setup_pe(e):
        loaded(e, "base")
        loaded(e, "c", 2)
        e.put(nc.tensor.transpose(psum[4][:, 0:16], srow[0:16, :], ident[0:16, 0:16]), "scol")
        loaded(e, "params", len(prm_src))
        for i, r in enumerate(prm_rows):
            ins = nc.tensor.transpose(psum[5][:, i * P:i * P + r], params[0:r, i, :], ident[0:r, 0:r])
        e.put(ins, "cols")

    def setup_act(e):
        e.after("scol")
        e.link(nc.scalar.activation(ssig[:, :], psum[4][:, 0:16], ACT.Silu), "silu c")
        e.after("spad zero")
        sv = ssig[:, :].rearrange("p (s k) -> p k s", s=2)
        e.link(nc.scalar.activation(spad[:, :, 0:2], sv, ACT.Copy), "spad hi")

    def setup_dve(e):
        e.link(nc.vector.memset(seed[:, :], 0.0))
        e.link(nc.vector.memset(epsc[:, :], EPS))
        e.link(nc.vector.memset(onec[:, :], 1.0))
        e.link(nc.vector.memset(spad[:, :, :].rearrange("p k c -> p (k c)").bitcast(F32), 0.0), "spad zero")
        e.after("spad hi")
        sv = ssig[:, :].rearrange("p (s k) -> p k s", s=2)
        e.link(nc.vector.tensor_tensor(spad[:, :, 2:4], sv, spad[:, :, 0:2].bitcast(F32), ALU.subtract), "spad")
        e.after("cols")
        for i, r in enumerate(prm_rows):
            e.link(nc.vector.tensor_copy(cols[:, i, 0:r], psum[5][:, i * P:i * P + r]), "params")

    EARLY = range(4)
    LATE = {(0, 0): ({0: [6], 1: [7], 2: [8], 3: [9]}, 4), (0, 1): ({0: [4], 1: [5], 2: [10], 3: [11]}, None),
            (1, 0): ({0: [6, 7], 1: [8], 2: [9], 3: [4]}, 3), (1, 1): ({0: [5], 1: [10], 2: [11]}, None)}
    late_rows = tmp[:, :, :].rearrange("p t d -> p (t d)")

    def late(l, st, chunk_, turn_=None):
        chunks, turn_at = LATE[l, st]

        def extra(i):
            for c in chunks.get(i, ()):
                chunk_(c)
            if turn_ and i == turn_at:
                turn_()
        return extra

    def mod_load(ld, l, chunks):
        for c in chunks:
            ld.columns(a["ada_w"][l], D, c * N, N)

    def mod_pool(e, l, *deps):
        e.after(*deps)
        side_load(e, mr[4:5, :], a["ada_b"][l:l + 1, 0:2 * D], f"bias{l}")

    def late_pool(e, l, tag):
        e.after(f"{tag}:xT3")
        if l:
            e.after("res_f1:h")
        side_load(e, late_rows[4:5, :], a["ada_b"][l:l + 1, 3 * D:5 * D], f"late{l}")
        for g, part in enumerate((2, 5)):
            side_load(e, gates[4:5, g, :], a["ada_b"][l:l + 1, part * D:part * D + D], f"late{l}")

    def mod_chunk_pe(e, s):
        if e.outs.n >= 3:
            e.eng.wait_ge(sem("out_done"), e.outs.n - 2)
        bank = (G, U, O)[e.outs.n % 3][0]
        for k0 in (0, 4):
            s.unit(spad, None, k0, 4, N, [bank], k0 == 0, k0 == 4)
        e.outs.n += 1

    def mod_columns_pe(e, rows, name):
        for i in range(2 * KD):
            ins = nc.tensor.matmul(psum[7][:, 2 * i:2 * i + 2], rows[0:5, i * P:i * P + P], pick[0:5, :],
                                   start=True, stop=True)
        e.put(ins, name)

    def mod_pe(e, s, l, ffn):
        e.after("spad")
        e.eng.wait_ge(sem("y_done"), ffn.ys.n)
        for _ in EARLY:
            mod_chunk_pe(e, s)
        e.eng.wait_ge(sem("out_done"), e.outs.n)
        loaded(e, f"bias{l}")
        if l:
            e.after("res_f1:h")
        mod_columns_pe(e, mr, f"mod{l}:cols")

    def late_pe(e, s, l, st):
        def turn_():
            e.eng.wait_ge(sem("out_done"), e.outs.n - 1)
            loaded(e, f"late{l}", 3)
            mod_columns_pe(e, late_rows, f"late{l}:cols")
        return late(l, st, lambda c: mod_chunk_pe(e, s), turn_)

    def mod_chunk_act(e, s, c):
        bank = (G, U, O)[e.outs.n % 3][0]
        part, c0 = c // 2, c * N % D
        to = {0: mr[0:4, c0:c0 + N], 1: mr[0:4, D + c0:D + c0 + N], 2: gates[0:4, 0, c0:c0 + N],
              3: late_rows[0:4, c0:c0 + N], 4: late_rows[0:4, D + c0:D + c0 + N],
              5: gates[0:4, 1, c0:c0 + N]}[part]

        def take():
            nc.scalar.activation(to, bank[0:4, :], ACT.Copy).then_inc(sem("out_done"), 1)
        s.step()
        s.step(take)
        e.outs.n += 1

    def mod_act(e, s, l):
        if l:
            e.after("res_f1:gate")
        for c in EARLY:
            mod_chunk_act(e, s, c)

    def mod_chunk_dve(e, s):
        s.step()
        s.step()
        e.outs.n += 1

    def mod_columns_dve(e, i, gain, cols_, name):
        e.after(cols_)
        e.link(nc.vector.tensor_copy(mod[:, 2 * i:2 * i + 2, :, :].rearrange("p a k s -> p (a k s)"),
                                     psum[7][:, 0:32]))
        for st in range(2):
            e.link(nc.vector.scalar_tensor_tensor(out=scal[:, i, :, st], in0=mod[:, 2 * i + 1, :, st],
                                                  scalar=1.0, in1=gain, op0=ALU.add, op1=ALU.mult), name)

    def mod_dve(e, s, l):
        for _ in EARLY:
            mod_chunk_dve(e, s)
        mod_columns_dve(e, 0, gain1(l), f"mod{l}:cols", f"mod{l}")

    def cut_pair(e, name, b):
        flat = lambda ap: ap[:, 2 * b:2 * b + 2, :].rearrange("p k t -> p (k t)")
        e.link(nc.vector.tensor_copy(flat(xhi), flat(xf)))
        e.put(nc.vector.tensor_tensor(flat(xlo), flat(xf), flat(xhi).bitcast(F32), ALU.subtract),
              (f"{name}:x{b}", f"{name}:x"))

    def cut_x(e, name, pairs, dep):
        for b in pairs:
            e.after(dep(b))
            cut_pair(e, name, b)

    prob = [tmp[:, i, 0:N] for i in range(2)]
    probT = [tmp[:, i, N:2 * N] for i in range(2)]
    SC, PT = psum[0:2], psum[2:4]
    ITEM = Count()

    def attn_pe(e, base, items, ready, *deps):
        e.after(*deps)
        last = len(items)

        def scores(i):
            it = items[i]
            if ready:
                ready(e, i)
            if i >= 2:
                e.eng.wait_ge(sem("exp_done"), base + i - 1)
            bank = SC[i % 2]
            n = it["n"]
            adds = it["adds"]
            nc_last = nc.tensor.matmul(bank[:, 0:n], it["q"], it["k"], start=True, stop=not adds)
            for j, (l_, r_) in enumerate(adds):
                nc_last = nc.tensor.matmul(bank[:, 0:r_.shape[-1]], l_, r_, start=False, stop=j == len(adds) - 1)
            nc_last.then_inc(sem("scores"), 1)

        def outputs(i):
            it = items[i]
            e.eng.wait_ge(sem("probT_done"), base + i + 1)
            if it.get("o_free"):
                it["o_free"](e)
            kt = it["n"] // P
            for k in range(kt):
                ins = nc.tensor.matmul(it["o"], probT[i % 2][:, k * P:k * P + P], it["v"][k],
                                       start=k == 0, stop=k == kt - 1)
            ins.then_inc(sem("out_ready"), 1)

        scores(0)
        for i in range(last):
            if i + 1 < last:
                scores(i + 1)
            e.eng.wait_ge(sem("exp_done"), base + i + 1)
            if i >= 2:
                e.eng.wait_ge(sem("probT_done"), base + i - 1)
            for k in range(items[i]["n"] // P):
                ins = nc.tensor.transpose(PT[i % 2][:, k * P:k * P + P], prob[i % 2][:, k * P:k * P + P], ident)
            ins.then_inc(sem("prob_turned"), 1)
            if i >= 1:
                outputs(i - 1)
        outputs(last - 1)

    def attn_dve(e, base, items, floor, *deps, every=None):
        e.after(*deps)

        def take(i):
            e.eng.wait_ge(sem("prob_turned"), base + i + 1)
            if i >= 2:
                e.eng.wait_ge(sem("out_ready"), base + i - 1)
            n = items[i]["n"]
            nc.vector.tensor_copy(probT[i % 2][:, 0:n], PT[i % 2][:, 0:n]).then_inc(sem("probT_done"), 1)

        for i, it in enumerate(items):
            e.eng.wait_ge(sem("scores"), base + i + 1)
            col = negm[:, i:i + 1]
            if floor:
                e.link(nc.vector.tensor_reduce(col, SC[i % 2][:, 0:it["n"]], AX.X, ALU.max, negate=True))
                nc.vector.tensor_tensor(col, col, floor(i), ALU.min).then_inc(sem("max_done"), 1)
            else:
                nc.vector.tensor_reduce(col, SC[i % 2][:, 0:it["n"]], AX.X, ALU.max, negate=True)\
                    .then_inc(sem("max_done"), 1)
            if i >= 1:
                take(i - 1)
            if every:
                every(i)
        take(len(items) - 1)

    def attn_act(e, base, items, *deps):
        e.after(*deps)
        for i, it in enumerate(items):
            e.eng.wait_ge(sem("max_done"), base + i + 1)
            if i >= 2:
                e.eng.wait_ge(sem("prob_turned"), base + i - 1)
            nc.scalar.activation(prob[i % 2][:, 0:it["n"]], SC[i % 2][:, 0:it["n"]], ACT.Exp,
                                 bias=negm[:, i:i + 1], accum_out=den[:, i:i + 1]).then_inc(sem("exp_done"), 1)

    def over(col_ap, heads, width):
        return col_ap.rearrange("p (h o) -> p h o", o=1).broadcast_to([P, heads, width])

    p_e, qT, kT, cT = R_E["p"], R_E["qT"], R_E["kT"], R_E["cT"]
    NA_H = 8

    def even_items(st):
        items = []
        for hd in range(NA_H):
            for t in range(NT):
                half = slice((hd % 2) * HD, (hd % 2) * HD + HD)
                q0 = st * TOK + t * P
                keys = slice(0, 2 * TOK) if st == 0 else slice(TOK, 2 * TOK)
                vs = [p_e[:, s_, t_, 2560 + hd * HD:2560 + hd * HD + HD]
                      for s_ in ((0, 1) if st == 0 else (1,)) for t_ in range(NT)]
                items.append(dict(
                    n=2 * TOK if st == 0 else TOK, q=qT[half, hd // 2, q0:q0 + P], k=kT[half, hd // 2, keys],
                    adds=[(ident, R_E["bias"][:, hd % 2, t, :])] if st == 0 else [], v=vs,
                    o=psum[4 + t][:, hd * HD:hd * HD + HD]))
        return items

    def even_pool(e):
        e.after("in_e1:x")
        near = xf[:, 4:6, :].rearrange("p t k -> p (t k)")
        side_load(e, near, a["k_near"], "near")
        for i, name in enumerate(("ev_q_g", "ev_k_g")):
            side_load(e, R_E["gqk"][:, i * HD:i * HD + HD], a[name].broadcast_to([P, HD]), "gqk")
        loaded(e, "gqk", 2)
        e.link(nc.gpsimd.tensor_scalar(R_E["gqk"][:, 0:HD], R_E["gqk"][:, 0:HD], HD ** -0.5, None, ALU.mult), "gqk")
        root_pool(e, "qk_e0", 0, 32, HD, "qk_e:ss0")
        root_pool(e, "qk_e1", 32, 64, HD, "qk_e:ss1")
        loaded(e, "near")
        for hd in range(NA_H):
            if hd >= 2:
                e.eng.wait_ge(sem("scores"), 2 * (hd - 1))
            b = R_E["bias"][:, hd % 2, :, :].rearrange("p t k -> p (t k)")
            e.eng.dma_start(b, a["k_rpb"][hd]).then_inc(sem(f"in_rpb{hd % 2}"), 16)
            e.eng.wait_ge(sem(f"in_rpb{hd % 2}"), 16 * (hd // 2 + 1))
            e.link(nc.gpsimd.tensor_tensor(b, b, near, ALU.add),
                   f"bias{hd}")

    esq = (tmp, qT[:, :, :].rearrange("p k t -> p (k t)").rearrange("p (t d) -> p t d", t=NT))

    def even_squares_act(e, st, t):
        e.put(nc.scalar.activation(esq[st][:, t, :], p_e[:, st, t, 1536:2560], ACT.Square), f"qk_e:sq{st}{t}")

    def even_lat_act(e, i):
        if i < NT:
            if i == 0:
                e.after("in_e1:x")
            even_squares_act(e, 0, i)

    def even_qk_act(e):
        for t in range(NT):
            even_squares_act(e, 1, t)

    def even_sums_dve(e, st, t):
        e.after(f"qk_e:sq{st}{t}")
        c = st * 32 + t * 16
        e.link(nc.vector.tensor_reduce(ss[:, c:c + 16], esq[st][:, t, :].rearrange("p (h d) -> p h d", d=HD),
                                       AX.X, ALU.add), f"qk_e:ss{st}")

    def even_root_dve(e, st, t):
        c = st * 32 + t * 16
        qk = p_e[:, st, t, 1536:2560].rearrange("p (h d) -> p h d", d=HD)
        e.link(nc.vector.tensor_tensor(qk, qk, over(ss[:, c:c + 16], 16, HD), ALU.mult))

    def even_gain_dve(e, st, t):
        both = p_e[:, st, t, 1536:2560].rearrange("p (a h d) -> p a h d", a=2, d=HD)
        g = R_E["gqk"][:, :].rearrange("p (a o d) -> p a o d", a=2, o=1).broadcast_to([P, 2, 8, HD])
        e.link(nc.vector.tensor_tensor(both, both, g, ALU.mult), f"qk_e:{st}")

    def even_lat_dve(e, i):
        if 1 <= i <= NT:
            even_sums_dve(e, 0, i - 1)
        if i == 4:
            e.after("qk_e0:root", "gqk")
        if 4 <= i < 4 + 2 * NT:
            t, stage = (i - 4) // 2, (i - 4) % 2
            (even_root_dve, even_gain_dve)[stage](e, 0, t)
        if 9 <= i < 9 + NT:
            gated_dve(e, 0, i - 9)

    def even_qk_dve(e):
        e.put(nc.vector.memset(cT[:, :, 0:1], 0.0))
        e.link(nc.vector.memset(cT[:, :, TOK + 1:TOK + 2], 0.0), "pads")
        for t in range(NT):
            even_sums_dve(e, 1, t)
        e.after("qk_e1:root")
        for t in range(NT):
            even_root_dve(e, 1, t)
            even_gain_dve(e, 1, t)

    def even_qk_pe(e):
        for st in range(2):
            e.after(f"qk_e:{st}")
            if st:
                e.after("qkT0")
            for b in range(8):
                for t in range(NT):
                    c = (b % 2) * TOK + t * P
                    ins = nc.tensor.transpose(psum[b // 2][:, c:c + P],
                                              p_e[:, st, t, 1536 + b * P:1536 + b * P + P], ident)
            e.put(ins, f"qkT_ps{st}")

    def even_qk_out(e):
        e.after("qk_e:ss1")
        for st in range(2):
            e.after(f"qkT_ps{st}")
            for b in range(4):
                to = (qT, kT)[b // 2][:, (b % 2) * 2:(b % 2) * 2 + 2, st * TOK:st * TOK + TOK]
                e.link(nc.scalar.activation(to, psum[b][:, :].rearrange("p (k t) -> p k t", k=2), ACT.Copy),
                       f"qkT{st}")

    def conv_pe(e, st, *deps):
        e.after(f"gcu{st}", *deps)
        for b in range(4):
            for t in range(NT):
                c = (b % 2) * TOK + t * P
                nc.tensor.transpose(psum[4 + b // 2][:, c:c + P], tmp[:, t, b * P:b * P + P], ident)
                ins = nc.tensor.transpose(psum[6 + b // 2][:, c:c + P], p_e[:, st, t, b * P:b * P + P], ident)
        e.put(ins, f"conv_ps{st}")

    def conv_act(e, st):
        e.after(f"conv_ps{st}", "pads")
        for b in range(2):
            two = lambda x: x.rearrange("p (k t) -> p k t", k=2)
            e.put(nc.scalar.activation(cT[:, 2 * b:2 * b + 2, 1:TOK + 1], two(psum[4 + b][:, :]), ACT.Copy))
            e.link(nc.scalar.activation(tmp[:, b, N:2 * N], psum[6 + b][:, :], ACT.Copy), f"convT{st}")

    def gated_dve(e, st, t):
        e.link(nc.vector.tensor_tensor(tmp[:, t, 0:N], p_e[:, st, t, N:2 * N], p_e[:, st, t, 2 * N:3 * N],
                                       ALU.mult), f"gcu{st}")

    def conv_dve(e, st):
        if st:
            for t in range(NT):
                gated_dve(e, st, t)
        e.after(f"convT{st}")
        for b in range(4):
            for j in range(3):
                tap = cols[:, 1, j * 4 + b:j * 4 + b + 1]
                if j == 0:
                    ins = nc.vector.tensor_scalar(xf[:, b, :], cT[:, b, 0:TOK], tap, None, ALU.mult)
                else:
                    ins = nc.vector.scalar_tensor_tensor(out=xf[:, b, :], in0=cT[:, b, j:j + TOK], scalar=tap,
                                                         in1=xf[:, b, :], op0=ALU.mult, op1=ALU.add)
                e.link(ins)
            e.link(nc.vector.tensor_tensor(xf[:, b, :], xf[:, b, :],
                                           tmp[:, b // 2, N + (b % 2) * TOK:N + (b % 2) * TOK + TOK], ALU.mult),
                   f"conv{st}")

    def heads_out_dve(e, tag, n_items, base, width=HD, heads=8):
        e.eng.wait_ge(sem("out_ready"), base + n_items)
        e.eng.wait_ge(sem("exp_done"), base + n_items)
        e.link(nc.vector.reciprocal(den[:, 0:n_items], den[:, 0:n_items]))
        for t in range(NT):
            r = den[:, 0:n_items].rearrange("p (h t) -> p h t", t=NT)[:, :, t:t + 1].broadcast_to([P, heads, width])
            e.link(nc.vector.tensor_tensor(tmp[:, t, 0:N].rearrange("p (h d) -> p h d", d=width),
                                           psum[4 + t][:, :].rearrange("p (h d) -> p h d", d=width), r, ALU.mult),
                   tag + ":o")

    def heads_out_pe(e, tag):
        e.after(tag + ":o")
        for b in range(4):
            for t in range(NT):
                c = (b % 2) * TOK + t * P
                ins = nc.tensor.transpose(psum[6 + b // 2][:, c:c + P], tmp[:, t, b * P:b * P + P], ident)
        e.put(ins, tag + ":oT_ps")

    def heads_out_act(e, tag, first=4, scale=1.0):
        e.after(tag + ":oT_ps")
        for b in range(2):
            e.link(nc.scalar.activation(xf[:, first + 2 * b:first + 2 * b + 2, :].rearrange("p k t -> p (k t)"),
                                        psum[6 + b][:, :], ACT.Identity, scale=scale),
                   (f"{tag}:oT{first // 2 + b}", tag + ":oT"))

    pl, pc, sq, gain, qTo, kTo, band, rope = (R_O[n] for n in
                                              ("pl", "pc", "sq", "gain", "qT", "kT", "band", "rope"))
    lamv, lame, sink, nsink, sinke, sublng, router, vtop = small.values()
    NORMED = [(pl, 0, 18), (pl, 20, 8), (pc, 0, 2), (pc, 4, 8)]
    root_at = lambda src, t, hd: (t * 28 if src is pl else 56 + t * 12) + hd

    def gain_at(src, hd):
        return (hd if src is pl else hd + 16) * HD

    def window_items():
        items = []
        for hd in range(8):
            for t in range(NT):
                half = slice((hd % 2) * HD, (hd % 2) * HD + HD)
                kv = hd // 4
                v = [pl[:, t_, 1152 + kv * HD:1152 + kv * HD + HD] for t_ in range(NT)] + \
                    [pc[:, t_, 128 + kv * HD:128 + kv * HD + HD] for t_ in range(NT)]
                items.append(dict(n=2 * TOK, q=qTo[half, hd // 2, t * P:t * P + P], k=kTo[half, kv, :],
                                  adds=[(ident, band[:, t, :])], v=v, o=psum[4 + t][:, hd * HD:hd * HD + HD]))
        return items

    def diff_items():
        items = []
        for hd in range(4):
            for i in range(2):
                for t in range(NT):
                    half = slice(i * HD, i * HD + HD)
                    v = [pl[:, t_, 1792 + hd * P:1792 + hd * P + P] for t_ in range(NT)] + \
                        [pc[:, t_, 768 + hd * P:768 + hd * P + P] for t_ in range(NT)]
                    items.append(dict(n=2 * TOK, q=qTo[half, 4 + hd, t * P:t * P + P], k=kTo[half, 2 + hd, :],
                                      adds=[], v=v, o=psum[4 + 2 * i + t][:, hd * P:hd * P + P]))
        return items

    def odd_pool(e):
        e.after("in_o0:x")
        side_load(e, band[:, :, :].rearrange("p t k -> p (t k)"), a["k_band"], "odd")
        side_load(e, rope[:, :, :, :].rearrange("p a t d -> p (a t d)"), a["k_rope"], "odd")
        for name, hd, n in (("od_cq_g", 0, 8), ("od_dq_g", 8, 8), ("od_ck_g", 16, 2), ("od_dk_g", 20, 8)):
            side_load(e, gain[:, hd * HD:(hd + n) * HD].rearrange("p (h d) -> p h d", h=n),
                      a[name].rearrange("o (h d) -> o h d", h=1).broadcast_to([P, n, HD]), "odd")
        for i, name in enumerate(("od_lam_q1", "od_lam_k1", "od_lam_q2", "od_lam_k2")):
            side_load(e, lamv[:, i * HD:i * HD + HD], a[name].broadcast_to([P, HD]), "odd")
        side_load(e, sink[:, :], a["od_sink"].broadcast_to([P, 8]), "odd")
        side_load(e, router[:, :].rearrange("p (k e) -> p k e", e=EXPERTS),
                  a["moe_router"][0].rearrange("(k p) e -> p k e", p=P), "odd")
        loaded(e, "odd", 12)
        e.link(nc.gpsimd.tensor_scalar(gain[:, 0:OQ], gain[:, 0:OQ], HD ** -0.5, None, ALU.mult))
        e.link(nc.gpsimd.tensor_scalar(nsink[:, :], sink[:, :], -1.0, None, ALU.mult), "odd loads")

    def odd_roots_pool(e):
        root_pool(e, "qk_o0", 0, 56, HD, "qk_o:ss0")
        root_pool(e, "qk_o1", 56, 80, HD, "qk_o:ss1")

    def odd_lat_act(e, i):
        if i < NT:
            if i == 0:
                e.after("in_o1:x")
            e.put(nc.scalar.activation(sq[:, i, :], pl[:, i, 0:QK], ACT.Square), f"qk_o:sq0{i}")

    def odd_qk_act(e):
        e.eng.wait_ge(sem("out_done"), e.outs.n)
        e.after("qk_o")
        for t in range(NT):
            e.put(nc.scalar.activation(sq[:, t, 0:768], pc[:, t, 0:768], ACT.Square), f"qk_o:sq1{t}")

    by_head = lambda ap: ap.rearrange("p (h d) -> p h d", d=HD)

    def odd_sums_dve(e, st, t):
        n, c0 = ((28, 0), (12, 56))[st]
        e.after(f"qk_o:sq{st}{t}")
        c = c0 + t * n
        e.link(nc.vector.tensor_reduce(ss[:, c:c + n], by_head(sq[:, t, 0:n * HD]), AX.X, ALU.add), f"qk_o:ss{st}")

    def odd_root_dve(e, src, hd, n, t):
        part, c = src[:, t, hd * HD:(hd + n) * HD], root_at(src, t, hd)
        e.link(nc.vector.tensor_tensor(by_head(part), by_head(part), over(ss[:, c:c + n], n, HD), ALU.mult))

    def odd_gain_dve(e, src, hd, n, t, name=None):
        part, g0 = src[:, t, hd * HD:(hd + n) * HD], gain_at(src, hd)
        e.link(nc.vector.tensor_tensor(part, part, gain[:, g0:g0 + n * HD], ALU.mult), name)

    rot = y[:, :, :].rearrange("p t d -> p (t d)")

    def odd_cos_dve(e, src, hd, n, t):
        part = src[:, t, hd * HD:(hd + n) * HD]
        cos = rope[:, 0, t, :].rearrange("p (o d) -> p o d", o=1).broadcast_to([P, n, HD])
        e.link(nc.vector.tensor_tensor(by_head(sq[:, t, hd * HD:(hd + n) * HD]), by_head(part), cos, ALU.mult))

    def odd_sin_dve(e, src, hd, n, t):
        part = src[:, t, hd * HD:(hd + n) * HD]
        quad = lambda ap: ap.rearrange("p (h a b c) -> p h a b c", a=2, b=2, c=16)
        sin = rope[:, 1, t, :].rearrange("p (o a b c) -> p o a b c", o=1, a=2, b=2, c=16)
        for b in range(2):
            e.put(nc.vector.tensor_tensor(quad(rot[:, 0:n * HD])[:, :, :, b, :], quad(part)[:, :, :, 1 - b, :],
                                          sin[:, :, :, b, :].broadcast_to([P, n, 2, 16]), ALU.mult))
        e.eng.wait_ge(e.chain.sem, e.chain.n)
        e.link(nc.vector.tensor_tensor(part, sq[:, t, hd * HD:(hd + n) * HD], rot[:, 0:n * HD], ALU.add), "qk_o")

    def odd_lat_dve(e, i):
        if 1 <= i <= NT:
            odd_sums_dve(e, 0, i - 1)
        if i == 3:
            e.after("qk_o0:root", "odd loads")
        if 3 <= i < 3 + 4 * NT:
            t, stage = (i - 3) // 4, (i - 3) % 4
            for src, hd, n in NORMED[0:2]:
                (odd_root_dve, odd_gain_dve, odd_cos_dve, odd_sin_dve)[stage](e, src, hd, n, t)

    def odd_qk_dve(e):
        for t in range(NT):
            odd_sums_dve(e, 1, t)
        for i in range(2):
            pr = lamv[:, 2 * i * HD:2 * i * HD + HD]
            e.link(nc.vector.tensor_tensor(pr, pr, lamv[:, (2 * i + 1) * HD:(2 * i + 2) * HD], ALU.mult))
            e.link(nc.vector.tensor_reduce(lame[:, i:i + 1], pr, AX.X, ALU.add), "lam dots")
        e.link(nc.vector.tensor_scalar(sublng[:, :], cols[:, 1, 104:105], 1.0 - LAM_INIT, None, ALU.mult), "sublng")
        e.after("qk_o1:root")
        for src, hd, n in NORMED[2:4]:
            for t in range(NT):
                odd_root_dve(e, src, hd, n, t)
                odd_gain_dve(e, src, hd, n, t, "k_ctx")

    def odd_qk_pe(e):
        e.after("qk_o")
        for b in range(8):
            for t in range(NT):
                c = (b % 2) * TOK + t * P
                ins = nc.tensor.transpose(psum[b // 2][:, c:c + P], pl[:, t, b * P:b * P + P], ident)
        e.put(ins, "qoT_ps")
        e.after("k_ctx")
        for b in range(4):
            for t in range(2 * NT):
                src, c = (pl, 1280) if t < NT else (pc, 256)
                ins = nc.tensor.transpose(psum[4 + b][:, t * P:t * P + P],
                                          src[:, t % NT, c + b * P:c + b * P + P], ident)
        e.put(ins, "dkT_ps")
        e.after("qoT")
        for b in range(2):
            for t in range(2 * NT):
                src, c = (pl, 1024) if t < NT else (pc, 0)
                for half in range(2):
                    ins = nc.tensor.transpose(psum[b][half * 0:HD, t * P:t * P + P] if half == 0 else
                                              psum[2 + b][0:HD, t * P:t * P + P],
                                              src[:, t % NT, c + b * HD:c + b * HD + HD], ident)
        e.put(ins, "ckT_ps")

    def odd_qk_out(e):
        e.after("qoT_ps")
        for b in range(4):
            e.link(nc.scalar.activation(qTo[:, 2 * b:2 * b + 2, :].rearrange("p k t -> p (k t)"), psum[b][:, :],
                                        ACT.Copy), "qoT")
        e.after("dkT_ps")
        for b in range(4):
            e.link(nc.scalar.activation(kTo[:, 2 + b, :], psum[4 + b][:, :], ACT.Copy), "dkT")
        e.after("ckT_ps")
        for b in range(2):
            for half in range(2):
                e.link(nc.scalar.activation(kTo[half * HD:half * HD + HD, b, :], psum[2 * half + b][0:HD, :],
                                            ACT.Copy), "ckT")
        e.after("lam dots")
        e.link(nc.scalar.activation(lame[:, 2:4], lame[:, 0:2], ACT.Exp), "lam exp")

    def window_sinks_dve(e, base):
        e.eng.wait_ge(sem("exp_done"), base + 16)
        e.eng.wait_ge(sem("max_done"), base + 16)
        two = lambda ap: ap.rearrange("p (h t) -> p h t", t=NT)
        e.link(nc.vector.tensor_tensor(two(sinke[:, :]), two(negm[:, 0:16]), over(sink[:, :], 8, NT), ALU.add),
               "sink args")
        e.after("sink exps")
        e.link(nc.vector.tensor_tensor(den[:, 0:16], den[:, 0:16], sinke[:, :], ALU.add))

    def window_sinks_act(e):
        e.after("sink args")
        e.link(nc.scalar.activation(sinke[:, :], sinke[:, :], ACT.Exp), "sink exps")

    def diff_out_dve(e, base):
        e.eng.wait_ge(sem("out_ready"), base + 16)
        e.eng.wait_ge(sem("exp_done"), base + 16)
        e.after("lam exp")
        e.link(nc.vector.tensor_tensor(lame[:, 0:1], lame[:, 2:3], lame[:, 3:4], ALU.subtract))
        e.link(nc.vector.tensor_scalar(lame[:, 0:1], lame[:, 0:1], -1.0, -LAM_INIT, ALU.mult, ALU.add))
        e.link(nc.vector.reciprocal(den[:, 0:16], den[:, 0:16]))
        r = den[:, 0:16].rearrange("p (h i t) -> p h i t", i=2, t=NT)
        e.link(nc.vector.tensor_scalar(r[:, :, 1, :], r[:, :, 1, :], lame[:, 0:1], None, ALU.mult))
        heads = lambda ap: ap.rearrange("p (h d) -> p h d", d=P)
        for t in range(NT):
            for i in range(2):
                e.link(nc.vector.tensor_tensor(heads(tmp[:, t, i * N:i * N + N]), heads(psum[4 + 2 * i + t][:, :]),
                                               r[:, :, i, t:t + 1].broadcast_to([P, 4, P]), ALU.mult))
            e.link(nc.vector.tensor_tensor(tmp[:, t, 0:N], tmp[:, t, 0:N], tmp[:, t, N:2 * N], ALU.add), "diff")
        for t in range(NT):
            e.link(nc.vector.tensor_tensor(tmp[:, t, N:2 * N], tmp[:, t, 0:N], tmp[:, t, 0:N], ALU.mult))
            e.link(nc.vector.tensor_reduce(ss[:, t * 4:t * 4 + 4], heads(tmp[:, t, N:2 * N]), AX.X, ALU.add),
                   "subln:ss")
        e.after("subln:root")
        for t in range(NT):
            e.link(nc.vector.tensor_tensor(heads(tmp[:, t, 0:N]), heads(tmp[:, t, 0:N]),
                                           over(ss[:, t * 4:t * 4 + 4], 4, P), ALU.mult), "att_d:o")

    def router_pe(e):
        for t in range(NT):
            for k in range(KD):
                ins = nc.tensor.matmul(psum[4 + t][:, 0:EXPERTS], xf[:, k, t * P:t * P + P],
                                       router[:, k * EXPERTS:(k + 1) * EXPERTS], start=k == 0, stop=k == KD - 1)
        e.put(ins, "logits")

    def router_dve(e):
        e.after("logits")
        for t in range(NT):
            e.link(nc.vector.tensor_copy(logits[:, t, :], psum[4 + t][:, 0:EXPERTS]))
        e.link(nc.vector.memset(y[:, :, :], 0.0))
        pairs = lambda ap: ap.rearrange("p (e j) -> p e j", j=EXPERTS)
        for t in range(NT):
            e.link(nc.vector.max(top[:, t, :], logits[:, t, :]))
            e.link(nc.vector.tensor_tensor(vtop[:, t:t + 1], top[:, t, 1:2], top[:, t, 0:1], ALU.subtract), "gap")
            lj = logits[:, t:t + 1, :].broadcast_to([P, EXPERTS, EXPERTS])
            le = over(logits[:, t, :], EXPERTS, EXPERTS)
            e.link(nc.vector.tensor_tensor(pairs(cmp[:, :]), lj, le, ALU.is_gt))
            e.link(nc.vector.tensor_tensor(pairs(cmp2[:, :]), lj, le, ALU.is_equal))
            e.link(nc.vector.tensor_tensor(cmp2[:, :], cmp2[:, :], before, ALU.mult))
            e.link(nc.vector.tensor_tensor(cmp[:, :], cmp[:, :], cmp2[:, :], ALU.add))
            e.link(nc.vector.tensor_reduce(rank[:, t, :], pairs(cmp[:, :]), AX.X, ALU.add))
        e.after("gap exp")
        e.link(nc.vector.tensor_scalar(vtop[:, 4:6], vtop[:, 2:4], 1.0, None, ALU.add))
        e.link(nc.vector.reciprocal(vtop[:, 4:6], vtop[:, 4:6]))
        e.link(nc.vector.tensor_tensor(vtop[:, 6:8], vtop[:, 4:6], vtop[:, 2:4], ALU.mult))
        for t in range(NT):
            e.link(nc.vector.tensor_scalar(gate[:, t, :], rank[:, t, :], 0.0, vtop[:, 4 + t:5 + t], ALU.is_equal,
                                           ALU.mult))
            e.link(nc.vector.tensor_scalar(cmp[:, 0:EXPERTS], rank[:, t, :], 1.0, vtop[:, 6 + t:7 + t],
                                           ALU.is_equal, ALU.mult))
            e.link(nc.vector.tensor_tensor(gate[:, t, :], gate[:, t, :], cmp[:, 0:EXPERTS], ALU.add))

    def router_act(e):
        e.after("gap")
        e.link(nc.scalar.activation(vtop[:, 2:4], vtop[:, 0:2], ACT.Exp), "gap exp")

    def resid2_pool(e, tag, i, l, s_, dep):
        if dep:
            e.after(dep)
        side_load(e, gates[:, i % 2, :], a["norm_g_2"][l, s_:s_ + 1, :].broadcast_to([P, D]), f"post{i % 2}")
        roots_pool(e, tag)

    def resid2_dve(e, tag, i, factor):
        loaded(e, f"post{i % 2}", i // 2 + 1)
        for t in range(NT):
            e.after(f"{tag}:root{t}")
            e.link(nc.vector.scalar_tensor_tensor(out=y[:, t, :], in0=y[:, t, :], scalar=ss[:, t:t + 1],
                                                  in1=gates[:, i % 2, :], op0=ALU.mult, op1=ALU.mult))
            e.link(nc.vector.scalar_tensor_tensor(out=h[:, t, :], in0=y[:, t, :], scalar=factor, in1=h[:, t, :],
                                                  op0=ALU.mult, op1=ALU.add), (f"{tag}:h{t}", tag + ":h"))

    def ffn2_weights(l, f):
        w = a["ffn_w1_2"][l, f]
        return w[:, 0:FF], w[:, FF:2 * FF], a["ffn_w2_2"][l, f]

    p_h, hpad, hid, xhead, mu, rstd = (R_H[n] for n in ("p", "pad", "hid", "xhead", "mu", "rstd"))
    flat3 = lambda ap: ap.rearrange("p k t -> p (k t)")

    def conf_pool(e, dep):
        e.after(dep)
        side_load(e, xhead[:, :, :], a["hyb_w_in_2"][0, :, HYB - SSM_H:HYB].rearrange("(k p) e -> p k e", p=P), "xhead")
        e.link(nc.gpsimd.memset(hpad[:, :, 0:TAPS - 1], 0.0), "hpad zero")
        e.link(nc.gpsimd.memset(ones[:, :], 1.0), "ones")

    DVE_TILES, PE_TILES = range(0, KD // 2), range(KD // 2, KD)
    diagonals = [t_[:, :, :].rearrange("p t d -> p (t d)").rearrange("p (j c) -> p j c", c=P) for t_ in (y, tmp)]
    HALF_TAPS = (16, TAPS - 16)

    def diagonals_pool(e):
        e.after("head", "in_h:x", "in_h:xT3")
        for k in PE_TILES:
            for half, n in enumerate(HALF_TAPS):
                if k > PE_TILES[0]:
                    e.after(f"conv{k - 1}_{half}")
                taps = cols[:, 2 + half, k:k + (n - 1) * KD + 1:KD].rearrange("p (j o) -> p j o", o=1)
                e.put(nc.gpsimd.tensor_tensor(diagonals[half][:, 0:n, :],
                                              ident.rearrange("p (o c) -> p o c", o=1).broadcast_to([P, n, P]),
                                              taps.broadcast_to([P, n, P]), ALU.mult), f"taps{k}_{half}")

    def diagonals_pe(e):
        for k in PE_TILES:
            i = k - PE_TILES[0]
            if i % 2 == 0:
                e.after(f"hpad{k // 2}")
            to = psum[6 + i // 2][:, (i % 2) * TOK:(i % 2) * TOK + TOK]
            for half, n in enumerate(HALF_TAPS):
                e.after(f"taps{k}_{half}")
                for j in range(n):
                    at = 16 * half + j
                    ins = nc.tensor.matmul(to, diagonals[half][:, j, :], hpad[:, k, at:at + TOK],
                                           start=at == 0, stop=at == TAPS - 1)
                e.put(ins, f"conv{k}_{half}")

    def head_pe(e):
        loaded(e, "xhead")
        for t in range(NT):
            for k in range(KD):
                ins = nc.tensor.matmul(psum[6 + t][:, 0:SSM_H], xf[:, k, t * P:t * P + P], xhead[:, k, :],
                                       start=k == 0, stop=k == KD - 1)
        e.put(ins, "head")

    def conf_act(e):
        e.after("head taken")
        for t in range(NT):
            e.link(nc.scalar.activation(p_h[:, t, D:2 * D], p_h[:, t, D:2 * D], ACT.Sigmoid), f"sigmoid{t}")
        e.after("hpad zero")
        for b in range(4):
            e.after(f"gluT{b}")
            e.link(nc.scalar.activation(hpad[:, 2 * b:2 * b + 2, TAPS - 1:TAPS - 1 + TOK],
                                        psum[b][:, :].rearrange("p (k t) -> p k t", k=2), ACT.Copy), f"hpad{b}")
        for k in PE_TILES:
            i = k - PE_TILES[0]
            if i % 2 == 0:
                e.after(f"conv{k + 1}_1")
            e.put(nc.scalar.activation(hid[:, k, :], psum[6 + i // 2][:, (i % 2) * TOK:(i % 2) * TOK + TOK],
                                       ACT.Identity, bias=cols[:, 1, 12 + k:13 + k]), "hid_act")
        for half in range(2):
            e.after(f"centred{half}")
            e.put(nc.scalar.activation(hpad[:, 4 * half:4 * half + 4, 0:TOK], hid[:, 4 * half:4 * half + 4, :],
                                       ACT.Square), f"squares{half}")
        e.after("var_ps")
        e.link(nc.scalar.activation(rstd[:, :], psum[5][:, 0:TOK], ACT.Sqrt, scale=1.0 / D, bias=epsc[:, 0:1]), "std")
        for k in range(KD):
            if k % 2 == 0:
                e.after(f"hid normed{k // 2}")
            e.put(nc.scalar.activation(xf[:, k, :], hid[:, k, :], ACT.Silu, scale=cols[:, 1, 20 + k:21 + k],
                                       bias=cols[:, 1, 28 + k:29 + k]), f"conformer{k // 2}")

    def conf_pe(e):
        e.after("glu")
        for b in range(4):
            for k in range(2):
                for t in range(NT):
                    c, kk = k * TOK + t * P, 2 * b + k
                    ins = nc.tensor.transpose(psum[b][:, c:c + P], p_h[:, t, kk * P:kk * P + P], ident)
            e.put(ins, f"gluT{b}")
        diagonals_pe(e)
        e.after("hid", "hid_act", "ones")
        for k in range(KD):
            ins = nc.tensor.matmul(psum[4][:, 0:TOK], ones[:, :], hid[:, k, :], start=k == 0, stop=k == KD - 1)
        e.put(ins, "mean_ps")
        for k in range(KD):
            if k % 4 == 0:
                e.after(f"squares{k // 4}")
            ins = nc.tensor.matmul(psum[5][:, 0:TOK], ones[:, :], hpad[:, k, 0:TOK], start=k == 0, stop=k == KD - 1)
        e.put(ins, "var_ps")

    def conf_dve(e):
        for t in range(NT):
            e.after(f"sigmoid{t}")
            e.link(nc.vector.tensor_tensor(p_h[:, t, 0:D], p_h[:, t, 0:D], p_h[:, t, D:2 * D], ALU.mult), "glu")
        for pair in (DVE_TILES,):
            e.after(f"hpad{pair[-1] // 2}")
            for j in range(TAPS):
                for k in pair:
                    tile, c = (2, j * KD + k) if j < 16 else (3, (j - 16) * KD + k)
                    tap = cols[:, tile, c:c + 1]
                    if j == 0:
                        ins = nc.vector.tensor_scalar(hid[:, k, :], hpad[:, k, 0:TOK], tap,
                                                      cols[:, 1, 12 + k:13 + k], ALU.mult, ALU.add)
                    else:
                        e.eng.wait_ge(e.chain.sem, e.chain.n - len(pair) + 1)
                        ins = nc.vector.scalar_tensor_tensor(out=hid[:, k, :], in0=hpad[:, k, j:j + TOK], scalar=tap,
                                                             in1=hid[:, k, :], op0=ALU.mult, op1=ALU.add)
                    e.put(ins, "hid")
        e.after("mean_ps")
        e.link(nc.vector.tensor_scalar(mu[:, :], psum[4][:, 0:TOK], 1.0 / D, None, ALU.mult))
        rows_ = lambda ap: ap.rearrange("p (o t) -> p o t", o=1).broadcast_to([P, KD, TOK])
        for half in range(2):
            part = hid[:, 4 * half:4 * half + 4, :]
            e.link(nc.vector.tensor_tensor(part, part, rows_(mu[:, :])[:, 0:4, :], ALU.subtract), f"centred{half}")
        e.after("std")
        e.link(nc.vector.reciprocal(rstd[:, :], rstd[:, :]))
        for b in range(4):
            part = hid[:, 2 * b:2 * b + 2, :]
            e.put(nc.vector.tensor_tensor(part, part, rows_(rstd[:, :])[:, 0:2, :], ALU.mult), f"hid normed{b}")
        cut_x(e, "cat_h1", range(4), lambda b: f"conformer{b}")

    gpad, xc, a1, dts, srow2, dec = (R_G[n] for n in ("pad", "xc", "a1", "dt", "row", "dec"))
    gflat = flat3(gpad[:, :, :])
    cbm = gflat[:, 0:4 * P].rearrange("p (i l) -> p i l", i=4)
    bmt = gflat[:, 4 * P:6 * P]
    xw = gflat[:, 6 * P:6 * P + D]
    s0 = gflat[:, 6 * P + D:6 * P + 2 * D].rearrange("p (g c) -> p g c", g=2)
    xs = [p_h[:, t, 0:D] for t in range(NT)]
    xdt = [p_h[:, t, D:2 * D] for t in range(NT)]
    ex = [tmp[:, i, 0:N] for i in range(2)]
    mt = [tmp[:, i, N:2 * N].rearrange("p (i l) -> p i l", i=4) for i in range(2)]
    DT, ADT, NEG, ABS = dts[:, 0], dts[:, 1], dts[:, 2], dts[:, 3]
    heads = lambda ap: ap.rearrange("p (h d) -> p h d", d=HD)

    DVE_ROWS, PE_ROWS = range(0, 6), range(6, 12)
    ssm_diagonals = lambda i: diagonals[1 - i // 4][:, (i % 4) * 4:(i % 4) * 4 + 4, :]
    ssm_conv_ps = lambda i: psum[(6, 7, 0)[i // 2]][:, (i % 2) * TOK:(i % 2) * TOK + TOK]

    def ssm_pool(e):
        e.after("cat_h1:x")
        for i, name in enumerate(("ssm_dt_bias_2", "ssm_a_log_2", "ssm_d_2")):
            side_load(e, srow2[:, i, :], a[name].broadcast_to([P, SSM_H]), "ssm_rows")
        e.link(nc.gpsimd.memset(gpad[:, :, 0:3], 0.0), "gpad zero")
        for i, b in enumerate(PE_ROWS):
            taps = cols[:, 1, 36 + b:36 + b + 37:12].rearrange("p (j o) -> p j o", o=1)
            e.put(nc.gpsimd.tensor_tensor(ssm_diagonals(i),
                                          ident.rearrange("p (o c) -> p o c", o=1).broadcast_to([P, 4, P]),
                                          taps.broadcast_to([P, 4, P]), ALU.mult), f"ssm taps{b}")

    def ssm_act(e):
        e.after("gpad zero")
        for b in range(6):
            e.after(f"xbcT{b}")
            e.link(nc.scalar.activation(gpad[:, 2 * b:2 * b + 2, 3:3 + TOK],
                                        psum[b][:, :].rearrange("p (k t) -> p k t", k=2), ACT.Copy),
                   (f"gpad{b}", "gpad"))
        e.after("dt abs")
        e.link(nc.scalar.activation(ABS, ABS, ACT.Exp, scale=-1.0))
        e.link(nc.scalar.activation(ABS, ABS, ACT.Ln, bias=onec[:, 0:1]))
        e.link(nc.scalar.activation(srow2[:, 1, :], srow2[:, 1, :], ACT.Exp), "a exp")
        for i, b in enumerate(PE_ROWS):
            if i % 2 == 0:
                e.after(f"conv4 ps{i // 2}")
            e.put(nc.scalar.activation(xc[:, b, :], ssm_conv_ps(i), ACT.Silu, bias=cols[:, 1, 84 + b:85 + b]))
        e.after("conv4")
        e.link(nc.scalar.activation(flat3(xc[:, 0:6, :]), flat3(xc[:, 0:6, :]), ACT.Silu), "xc")
        e.after("xsT")
        for t in range(NT):
            for half in range(2):
                e.link(nc.scalar.activation(xs[t][:, half * N:half * N + N], psum[2 * t + half][:, :], ACT.Copy), "xs")
        e.after("bmT")
        e.link(nc.scalar.activation(bmt, psum[4][:, 0:2 * P], ACT.Copy), "bmt")
        e.after("decays_ps")
        e.link(nc.scalar.activation(dec[:, :, :].rearrange("p a h -> p (a h)"), psum[6][:, 0:2 * SSM_H], ACT.Exp),
               "decays")
        for i in range(8):
            e.after(f"seg{i}")
            if i >= 2:
                e.after(f"mt{i - 2}")
            e.link(nc.scalar.activation(ex[i % 2], psum[i % 2][:, :], ACT.Exp), f"ex{i}")
        for g in range(2):
            e.after("s0_ps")
            e.link(nc.scalar.activation(s0[:, g, :], psum[g][:, :], ACT.Copy), "s0")
        e.after("gated z")
        for t in range(NT):
            e.link(nc.scalar.activation(p_h[:, t, 2 * D:3 * D], p_h[:, t, 2 * D:3 * D], ACT.Silu), "z")

    def ssm_pe(e):
        e.after("cat_h1:x")
        for b in range(6):
            for k in range(2):
                for t in range(NT):
                    c, kk = k * TOK + t * P, 3 * D + (2 * b + k) * P
                    ins = nc.tensor.transpose(psum[b][:, c:c + P], p_h[:, t, kk:kk + P], ident)
            e.put(ins, f"xbcT{b}")
        for i, b in enumerate(PE_ROWS):
            e.after(f"gpad{b // 2}", f"ssm taps{b}")
            for j in range(4):
                ins = nc.tensor.matmul(ssm_conv_ps(i), ssm_diagonals(i)[:, j, :], gpad[:, b, j:j + TOK],
                                       start=j == 0, stop=j == 3)
            if i % 2 == 1:
                e.put(ins, f"conv4 ps{i // 2}")
        e.after("xc", "gpad")
        for t in range(NT):
            for b in range(8):
                ins = nc.tensor.transpose(psum[2 * t + b // 4][:, (b % 4) * P:(b % 4) * P + P],
                                          xc[:, b, t * P:t * P + P], ident)
        e.put(ins, "xsT")
        for g in range(2):
            ins = nc.tensor.transpose(psum[4][:, g * P:g * P + P], xc[:, 8 + g, 0:P], ident)
        e.put(ins, "bmT")
        for c in range(NT):
            for g in range(2):
                tok = slice(c * P, c * P + P)
                i = c * 2 + g
                ins = nc.tensor.matmul(psum[5][:, i * P:i * P + P], xc[:, 8 + g, tok], xc[:, 10 + g, tok],
                                       start=True, stop=True)
        e.put(ins, "cb_ps")
        e.after("adt")
        nc.tensor.matmul(psum[6][:, 0:SSM_H], after, ADT[:, 0, :], start=True, stop=True)
        e.put(nc.tensor.matmul(psum[6][:, SSM_H:2 * SSM_H], upto, ADT[:, 1, :], start=True, stop=True), "decays_ps")

        def diagonal(i):
            c, quad_ = i // 4, i % 4
            bank = psum[4 + 2 * c + quad_ // 2]
            for j in range(4):
                hd = quad_ * 4 + j
                ins = nc.tensor.matmul(bank[:, (hd % 8) * HD:(hd % 8) * HD + HD], mt[i % 2][:, j, :],
                                       xdt[c][:, hd * HD:hd * HD + HD], start=True, stop=True)
            e.put(ins, f"diag{i}")

        for i in range(8):
            e.after(f"a1_{i}")
            if i == 0:
                e.after("xdt", "xs")
            if i >= 2:
                e.after(f"ex{i - 2}")
            for j in range(4):
                ins = nc.tensor.matmul(psum[i % 2][:, j * P:j * P + P], a1[:, i % 2, j, :], upto, start=True, stop=True)
            e.put(ins, f"seg{i}")
            if i >= 1:
                if i == 1:
                    e.after("cbm", "decays", "bmt")
                e.after(f"mt{i - 1}")
                diagonal(i - 1)
        e.after("mt7", "ex7")
        diagonal(7)
        e.after("xw", "bmt")
        for g in range(2):
            ins = nc.tensor.matmul(psum[g][:, :], bmt[:, g * P:g * P + P], xw[:, g * N:g * N + N],
                                   start=True, stop=True)
        e.put(ins, "s0_ps")
        e.after("s0")
        for g in range(2):
            ins = nc.tensor.matmul(psum[2 + g][:, :], xc[:, 10 + g, P:2 * P], s0[:, g, :], start=True, stop=True)
        e.put(ins, "yoff_ps")

    def dt_dve(e):
        e.after("head")
        for t in range(NT):
            e.link(nc.vector.tensor_copy(dtraw[:, t, :], psum[6 + t][:, 0:SSM_H]), "head taken")

    def ssm_dve(e):
        loaded(e, "ssm_rows", 3)
        step = lambda ap: ap.rearrange("p (o h) -> p o h", o=1).broadcast_to([P, NT, SSM_H])
        e.link(nc.vector.tensor_tensor(DT, dtraw[:, :, :], step(srow2[:, 0, :]), ALU.add))
        e.link(nc.vector.tensor_scalar(NEG, DT, -1.0, None, ALU.mult))
        e.link(nc.vector.tensor_tensor(ABS, DT, NEG, ALU.max), "dt abs")
        e.after("a exp")
        e.link(nc.vector.scalar_tensor_tensor(out=DT.rearrange("p t h -> p (t h)"), in0=DT.rearrange("p t h -> p (t h)"),
                                              scalar=0.0, in1=ABS.rearrange("p t h -> p (t h)"),
                                              op0=ALU.max, op1=ALU.add))
        e.link(nc.vector.tensor_scalar(srow2[:, 1, :], srow2[:, 1, :], -1.0, None, ALU.mult))
        e.link(nc.vector.tensor_tensor(ADT, DT, step(srow2[:, 1, :]), ALU.mult), "adt")
        for rows_ in (DVE_ROWS[0:2], DVE_ROWS[2:6]):
            e.after(f"gpad{rows_[-1] // 2}")
            for j in range(4):
                for b in rows_:
                    tap = cols[:, 1, 36 + j * 12 + b:37 + j * 12 + b]
                    if j == 0:
                        ins = nc.vector.tensor_scalar(xc[:, b, :], gpad[:, b, 0:TOK], tap, cols[:, 1, 84 + b:85 + b],
                                                      ALU.mult, ALU.add)
                    else:
                        e.eng.wait_ge(e.chain.sem, e.chain.n - len(rows_) + 1)
                        ins = nc.vector.scalar_tensor_tensor(out=xc[:, b, :], in0=gpad[:, b, j:j + TOK], scalar=tap,
                                                             in1=xc[:, b, :], op0=ALU.mult, op1=ALU.add)
                    e.put(ins, "conv4")
        e.after("xs")
        for t in range(NT):
            e.link(nc.vector.tensor_tensor(heads(xdt[t]), heads(xs[t]), over(DT[:, t, :], SSM_H, HD), ALU.mult), "xdt")
        e.after("cb_ps")
        e.link(nc.vector.tensor_tensor(cbm, psum[5][:, :].rearrange("p (i l) -> p i l", i=4),
                                       upto.rearrange("p (o l) -> p o l", o=1).broadcast_to([P, 4, P]), ALU.mult),
               "cbm")

        def masked_steps(i):
            c, q4 = i // 4, (i % 4) * 4
            if i >= 2:
                e.after(f"seg{i - 2}")
            e.link(nc.vector.tensor_tensor(a1[:, i % 2, :, :],
                                           after.rearrange("p (o l) -> p o l", o=1).broadcast_to([P, 4, P]),
                                           over(ADT[:, c, q4:q4 + 4], 4, P), ALU.mult), f"a1_{i}")

        masked_steps(0)
        e.after("decays")
        e.link(nc.vector.tensor_tensor(heads(xw), heads(xdt[0]), over(dec[:, 0, :], SSM_H, HD), ALU.mult), "xw")
        for i in range(8):
            c, g = i // 4, (i % 4) // 2
            if i < 7:
                masked_steps(i + 1)
            e.after(f"ex{i}")
            if i >= 2:
                e.after(f"diag{i - 2}")
            e.link(nc.vector.tensor_tensor(mt[i % 2], ex[i % 2].rearrange("p (i l) -> p i l", i=4),
                                           cbm[:, c * 2 + g:c * 2 + g + 1, :].broadcast_to([P, 4, P]), ALU.mult),
                   f"mt{i}")
        e.after("yoff_ps")
        e.link(nc.vector.tensor_copy(y[:, 0, 0:1], seed[:, 0:1]), "gated z")
        for t in range(NT):
            for half in range(2):
                part = y[:, t, half * N:half * N + N]
                rng = slice(half * N, half * N + N)
                hh = slice(half * 8, half * 8 + 8)
                e.link(nc.vector.tensor_tensor(heads(part), heads(xs[t][:, rng]), over(srow2[:, 2, hh], 8, HD), ALU.mult))
                e.link(nc.vector.tensor_tensor(part, part, psum[4 + 2 * t + half][:, :], ALU.add))
                if t == 1:
                    e.link(nc.vector.tensor_tensor(heads(xw[:, rng]), heads(psum[2 + half][:, :]),
                                                   over(dec[:, 1, hh], 8, HD), ALU.mult))
                    e.link(nc.vector.tensor_tensor(part, part, xw[:, rng], ALU.add))
        e.after("z")
        for t in range(NT):
            e.link(nc.vector.tensor_tensor(y[:, t, :], y[:, t, :], p_h[:, t, 2 * D:3 * D], ALU.mult), "ssm y")

    p_a, qTa, kTa, dist, dil, slope, one = (R_A[n] for n in ("p", "qT", "kT", "dist", "dil", "slope", "one"))
    stage_d = flat3(y[:, :, :])

    def dilated_items():
        items = []
        for t in range(NT):
            for g in range(3):
                for hd in range(8):
                    half = slice((hd % 2) * HD, (hd % 2) * HD + HD)
                    n = (t + 1) * P
                    b = g * 4 + hd // 2
                    items.append(dict(
                        n=n, q=qTa[half, b, t * P:t * P + P], k=kTa[half, b, 0:n],
                        adds=[(slope[:, hd, :], dist[:, t, 0:n]), (one[:, :], dil[:, g, t, 0:n])],
                        v=[p_a[:, t_, 3072 + g * N + hd * HD:3072 + g * N + hd * HD + HD] for t_ in range(t + 1)],
                        o=psum[4 + (t * 3 + g) % 2][:, hd * HD:hd * HD + HD]))
        return items

    def raw_out(gi):
        return (y if gi < 4 else hc)[:, (gi % 4) // 2, (gi % 2) * N:(gi % 2) * N + N]

    def dil_pool(e):
        e.after("in_at:x")
        side_load(e, stage_d[:, 0:N], a["k_dist"], "dil0")
        side_load(e, stage_d[:, N:4 * N], a["k_dil"], "dil0")

    def dil_act(e):
        loaded(e, "dil0", 2)
        e.put(nc.scalar.activation(flat3(dist[:, :, :]), stage_d[:, 0:N], ACT.Copy))
        e.put(nc.scalar.activation(dil[:, :, :, :].rearrange("p g t k -> p (g t k)"), stage_d[:, N:4 * N], ACT.Copy))
        e.put(nc.scalar.activation(one[:, :], ident, ACT.Copy))
        for hd in range(8):
            e.put(nc.scalar.activation(slope[:, hd, :], ident, ACT.Copy, scale=2.0 ** -(hd + 1)), "masks")
        for r in range(3):
            e.after(f"dilT{r}")
            for b in range(4):
                to = (qTa, kTa)[(4 * r + b) // 6]
                at = 2 * ((4 * r + b) % 6)
                e.link(nc.scalar.activation(flat3(to[:, at:at + 2, :]), psum[(4 * r + b) % 8][:, :], ACT.Copy,
                                            scale=HD ** -0.5 if to is qTa else 1.0), f"dilqk{r}")

    def dil_pe(e):
        e.eng.wait_ge(sem("out_done"), e.outs.n)
        for r in range(3):
            if r == 2:
                e.after("dilqk0")
            for b in range(4):
                for k in range(2):
                    for t in range(NT):
                        blk = 2 * (4 * r + b) + k
                        c = k * TOK + t * P
                        ins = nc.tensor.transpose(psum[(4 * r + b) % 8][:, c:c + P],
                                                  p_a[:, t, blk * P:blk * P + P], ident)
            e.put(ins, f"dilT{r}")

    def dil_every(e, base):
        def every(i):
            if i >= 9 and (i - 9) % 8 == 0:
                raw_take((i - 9) // 8)

        def raw_take(gi):
            e.eng.wait_ge(sem("out_ready"), base + 8 * gi + 8)
            e.link(nc.vector.tensor_copy(raw_out(gi), psum[4 + gi % 2][:, :]), f"raw{gi}")
        return every, raw_take

    def merge_dve(e, base):
        e.eng.wait_ge(sem("exp_done"), base + 48)
        e.eng.wait_ge(sem("max_done"), base + 48)
        grp = lambda ap, t, g: ap[:, (t * 3 + g) * 8:(t * 3 + g) * 8 + 8]
        for t in range(NT):
            low = ss[:, t * 8:t * 8 + 8]
            e.link(nc.vector.tensor_tensor(low, grp(negm, t, 0), grp(negm, t, 1), ALU.min))
            e.link(nc.vector.tensor_tensor(low, low, grp(negm, t, 2), ALU.min))
            for g in range(3):
                e.link(nc.vector.tensor_tensor(grp(negm, t, g), low, grp(negm, t, g), ALU.subtract), "weights")
        e.after("weight exps")
        for t in range(NT):
            z = ss[:, t * 8:t * 8 + 8]
            for g in range(3):
                e.link(nc.vector.tensor_tensor(grp(den, t, g), grp(den, t, g), grp(negm, t, g), ALU.mult))
            e.link(nc.vector.tensor_tensor(z, grp(den, t, 0), grp(den, t, 1), ALU.add))
            e.link(nc.vector.tensor_tensor(z, z, grp(den, t, 2), ALU.add))
            e.link(nc.vector.reciprocal(z, z))
            for g in range(3):
                e.link(nc.vector.tensor_tensor(grp(negm, t, g), grp(negm, t, g), z, ALU.mult))
                part = raw_out(t * 3 + g)
                e.link(nc.vector.tensor_tensor(heads(part), heads(part), over(grp(negm, t, g), 8, HD), ALU.mult))
            e.link(nc.vector.tensor_tensor(tmp[:, t, 0:N], raw_out(t * 3), raw_out(t * 3 + 1), ALU.add))
            e.link(nc.vector.tensor_tensor(tmp[:, t, 0:N], tmp[:, t, 0:N], raw_out(t * 3 + 2), ALU.add), "att_a:o")

    def merge_act(e):
        e.after("weights")
        e.link(nc.scalar.activation(negm[:, 0:48], negm[:, 0:48], ACT.Exp), "weight exps")

    E_ITEMS = [even_items(0), even_items(1)]
    W_ITEMS, D_ITEMS, A_ITEMS = window_items(), diff_items(), dilated_items()
    ATT0 = [0, 16, 32, 48, 64]

    STAGES = plan["stop"]

    def on(n):
        return STAGES >= n

    with ctx:
        block = ctx.enter_context(nc.Block())

        @block.sync
        def _(sp):
            ld = Load(sp)
            mod_load(ld, 0, EARLY)
            for st in range(2):
                project_load(ld, a["ev_w_in"][0], D, 6 * N, extra=late(0, st, lambda c: mod_load(ld, 0, (c,))))
            for _ in range(2):
                project_load(ld, a["ev_w_out"][0], D, D)
            if on(2):
                for _ in range(2):
                    load_ffn(ld, a["ffn_w1"][0], a["ffn_w3"][0], a["ffn_w2"][0], FF)
            if on(3):
                mod_load(ld, 1, EARLY)
                for st, (n, first) in enumerate(((OW, 0), (OW - OQ, OQ))):
                    project_load(ld, a["od_w_in"][0], D, n, first, late(1, st, lambda c: mod_load(ld, 1, (c,))))
                project_load(ld, a["od_w_out"][0], D, D)
            if on(4):
                with sp.Fori(0, EXPERTS) as x:
                    turns = Turns(x, EXPERTS, [(ld.r, PER_EXPERT)])
                    load_ffn(ld, a["moe_w1"][0, bass.ds(x, 1)].rearrange("o k n -> (o k) n"),
                             a["moe_w3"][0, bass.ds(x, 1)].rearrange("o k n -> (o k) n"),
                             a["moe_w2"][0, bass.ds(x, 1)].rearrange("o k n -> (o k) n"), FE)
                    turns.end()
            if on(5):
                load_ffn(ld, *ffn2_weights(0, 0), FF)
                project_load(ld, a["hyb_w_in_2"][0], D, HYB - SSM_H)
                project_load(ld, a["hyb_w_out_2"][0], 2 * D, D)
            if on(6):
                load_ffn(ld, *ffn2_weights(0, 1), FF)
                load_ffn(ld, *ffn2_weights(1, 0), FF)
                project_load(ld, a["attn_w_qkv_2"][0], D, QKV)
                project_load(ld, a["attn_w_o_2"][0], D // 2, D)
                load_ffn(ld, *ffn2_weights(1, 1), FF)
            if STAGES == 4:
                for _ in range(2):
                    ld.unit(tiles(a["ada_w"][0], 0, 4, 0, N), 4, N)
            plan["new"]["units"] = ("units", ld.r.n)
            if not plan["dry"]:
                key, n = old["final"]
                sp.wait_ge(sem("dve_done"), n)
            sp.dma_start(out[0].rearrange("(t p) d -> p t d", p=P), h[:, :, :]).then_inc(sem("stored"), 16)
            sp.wait_ge(sem("stored"), 16)

        @block.gpsimd
        def _(g):
            e = Engine(g, "pool")
            setup_pool(e)
            mod_pool(e, 0)
            norm_pool(e, "in_e0")
            late_pool(e, 0, "in_e0")
            norm_pool(e, "in_e1")
            even_pool(e)
            if on(2):
                norm_pool(e, "ff0")
                norm_pool(e, "ff1")
            if on(3):
                mod_pool(e, 1, "res_f1:h")
                norm_pool(e, "in_o0")
                late_pool(e, 1, "in_o0")
                odd_pool(e)
                norm_pool(e, "in_o1")
                odd_roots_pool(e)
                root_pool(e, "subln", 0, 8, P, "subln:ss")
            if on(4):
                norm_pool(e, "moe")
            if on(5):
                norm_pool(e, "a0")
                resid2_pool(e, "ra0", 0, 0, 1, "res_m:h")
                conf_pool(e, "ra0:h")
                norm_pool(e, "in_h")
                diagonals_pool(e)
                ssm_pool(e)
                norm_pool(e, "ssm")
                resid2_pool(e, "rh", 1, 0, 3, "ra0:h")
            if on(6):
                for i, (tag, l, g_) in enumerate((("a1", 0, 5), ("b0", 1, 1))):
                    norm_pool(e, tag)
                    resid2_pool(e, "r" + tag, 2 + i, l, g_, ("ra0:h", "rh:h")[i])
                norm_pool(e, "in_at")
                dil_pool(e)
                resid2_pool(e, "rat", 4, 1, 3, "ra1:h")
                norm_pool(e, "b1")
                resid2_pool(e, "rb1", 5, 1, 5, "rb0:h")

        @block.scalar
        def _(act):
            e = Engine(act, "act")
            s = Split(act, True)
            f = FfnAct(act, s)
            setup_act(e)
            for name in ("silu_done", "turned_hi"):
                act.sem_inc(sem(name), 1)
            s.first()
            mod_act(e, s, 0)
            for st, src in enumerate((h, hc)):
                loaded(e, ("x", "ctx")[st])
                norm_act(e, src, f"in_e{st}", lambda k: scal[:, 0, k, st:st + 1],
                         lambda k: mod[:, 0, k, st:st + 1], ("mod0", "late0:cols")[st])
                if st:
                    s.with_(lambda i: even_lat_act(e, i))
                project_act(e, s, D, 6 * N, lambda t, c, n: p_e[:, st, t, c:c + n],
                            late(0, st, lambda c: mod_chunk_act(e, s, c)))
            s.with_(None)
            even_qk_act(e)
            conv_act(e, 0)
            even_qk_out(e)
            for st in range(2):
                if st:
                    conv_act(e, 1)
                attn_act(e, ATT0[st], E_ITEMS[st])
                heads_out_act(e, f"att_e{st}")
                project_act(e, s, D, D, lambda t, c, n: y[:, t, c:c + n])
            if on(2):
                for st, src in enumerate((h, hc)):
                    norm_act(e, src, f"ff{st}", lambda k: scal[:, 1, k, st:st + 1],
                             lambda k: mod[:, 2, k, st:st + 1], f"res_e{st}:h")
                    dense(f)
            if on(3):
                mod_act(e, s, 1)
                for st, (src, dst, n) in enumerate(((h, pl, OW), (hc, pc, OW - OQ))):
                    norm_act(e, src, f"in_o{st}", lambda k: scal[:, 0, k, st:st + 1],
                             lambda k: mod[:, 0, k, st:st + 1], ("mod1", "late1:cols")[st])
                    if st:
                        s.with_(lambda i: odd_lat_act(e, i))
                    project_act(e, s, D, n, lambda t, c, w: dst[:, t, c:c + w],
                                late(1, st, lambda c: mod_chunk_act(e, s, c)))
                s.with_(None)
                odd_qk_act(e)
                odd_qk_out(e)
                attn_act(e, ATT0[2], W_ITEMS)
                window_sinks_act(e)
                heads_out_act(e, "att_w", 0)
                attn_act(e, ATT0[3], D_ITEMS)
                e.after("sublng")
                heads_out_act(e, "att_d", 4, sublng[:, 0:1])
                project_act(e, s, D, D, lambda t, c, n: y[:, t, c:c + n])
            if on(4):
                norm_act(e, h, "moe", lambda k: scal[:, 1, k, 0:1], lambda k: mod[:, 2, k, 0:1], "res_o:h")
                router_act(e)
                experts(f)
            if on(5):
                norm_act(e, h, "a0", lambda k: gain_b2(0, 0)[:, k:k + 1], None, "res_m:h")
                dense(f)
                e.eng.wait_ge(sem("y_done"), f.ys.n)
                rms_act(e, y, "ra0")
                norm_act(e, h, "in_h", lambda k: gain_b2(0, 2)[:, k:k + 1], None, "ra0:h")
                project_act(e, s, D, HYB - SSM_H, lambda t, c, n: p_h[:, t, c:c + n])
                conf_act(e)
                ssm_act(e)
                norm_act(e, y, "ssm", lambda k: cols[:, 1, 96 + k:97 + k], None, "ssm y")
                project_act(e, s, 2 * D, D, lambda t, c, n: y[:, t, c:c + n])
                e.eng.wait_ge(sem("out_done"), e.outs.n)
                rms_act(e, y, "rh")
            if on(6):
                for tag, l, g_, dep in (("a1", 0, 4, "rh:h"), ("b0", 1, 0, "ra1:h")):
                    norm_act(e, h, tag, lambda k: gain_b2(l, g_)[:, k:k + 1], None, dep)
                    dense(f)
                    e.eng.wait_ge(sem("y_done"), f.ys.n)
                    rms_act(e, y, "r" + tag)
                norm_act(e, h, "in_at", lambda k: gain_b2(1, 2)[:, k:k + 1], None, "rb0:h")
                project_act(e, s, D, QKV, lambda t, c, n: p_a[:, t, c:c + n])
                dil_act(e)
                attn_act(e, ATT0[4], A_ITEMS)
                merge_act(e)
                heads_out_act(e, "att_a", 0)
                project_act(e, s, D // 2, D, lambda t, c, n: y[:, t, c:c + n])
                e.eng.wait_ge(sem("out_done"), e.outs.n)
                rms_act(e, y, "rat")
                norm_act(e, h, "b1", lambda k: gain_b2(1, 4)[:, k:k + 1], None, "rat:h")
                dense(f)
                e.eng.wait_ge(sem("y_done"), f.ys.n)
                rms_act(e, y, "rb1")

        @block.vector
        def _(dve):
            e = Engine(dve, "dve")
            s = Split(dve, False)
            f = FfnDve(dve, s)
            setup_dve(e)
            for name in ("product_ready", "turned_lo", "y_done"):
                dve.sem_inc(sem(name), 1)
            s.first()
            mod_dve(e, s, 0)
            for st, src in enumerate((h, hc)):
                norm_dve(e, src, f"in_e{st}")
                if st:
                    s.with_(lambda i: even_lat_dve(e, i))
                project_dve(e, s, D, 6 * N, late(0, st, lambda c: mod_chunk_dve(e, s)))
                if st == 0:
                    mod_columns_dve(e, 1, gain2(0), "late0:cols", "late0")
            e.eng.wait_ge(sem("out_done"), e.outs.n)
            s.with_(None)
            even_qk_dve(e)
            conv_dve(e, 0)
            for st, src in enumerate((h, hc)):
                if st:
                    conv_dve(e, 1, )
                attn_dve(e, ATT0[st], E_ITEMS[st], None,
                         every=lambda i: cut_pair(e, f"cat_e{st}", (i - 4) // 2) if i in (4, 6) else None)
                heads_out_dve(e, f"att_e{st}", 16, ATT0[st])
                cut_x(e, f"cat_e{st}", range(2, 4), lambda b: f"att_e{st}:oT{b}")
                project_dve(e, s, D, D)
                resid_dve(e, src, f"res_e{st}", e.outs.n)
            if on(2):
                for st, src in enumerate((h, hc)):
                    norm_dve(e, src, f"ff{st}")
                    dense(f)
                    resid_dve(e, src, f"res_f{st}")
            if on(3):
                mod_dve(e, s, 1)
                for st, (src, n) in enumerate(((h, OW), (hc, OW - OQ))):
                    norm_dve(e, src, f"in_o{st}")
                    if st:
                        s.with_(lambda i: odd_lat_dve(e, i))
                    project_dve(e, s, D, n, late(1, st, lambda c: mod_chunk_dve(e, s)))
                    if st == 0:
                        mod_columns_dve(e, 1, gain2(1), "late1:cols", "late1")
                s.with_(None)
                e.eng.wait_ge(sem("out_done"), e.outs.n)
                odd_qk_dve(e)
                attn_dve(e, ATT0[2], W_ITEMS, lambda i: nsink[:, i // NT:i // NT + 1])
                window_sinks_dve(e, ATT0[2])
                heads_out_dve(e, "att_w", 16, ATT0[2])

                def window_half(i):
                    if i in (4, 6):
                        cut_x(e, "cat_o", ((i - 4) // 2,), lambda b: f"att_w:oT{b}")
                attn_dve(e, ATT0[3], D_ITEMS, None, every=window_half)
                diff_out_dve(e, ATT0[3])
                cut_x(e, "cat_o", range(2, 4), lambda b: f"att_d:oT{b}")
                project_dve(e, s, D, D)
                resid_dve(e, h, "res_o", e.outs.n)
            if on(4):
                norm_dve(e, h, "moe")
                router_dve(e)
                experts(f)
                resid_dve(e, h, "res_m")
            if on(5):
                norm_dve(e, h, "a0")
                dense(f)
                resid2_dve(e, "ra0", 0, 0.5)
                norm_dve(e, h, "in_h")
                dt_dve(e)
                project_dve(e, s, D, HYB - SSM_H)
                e.eng.wait_ge(sem("out_done"), e.outs.n)
                conf_dve(e)
                ssm_dve(e)
                norm_dve(e, y, "ssm", (R_G2["x2hi"], R_G2["x2lo"]))
                project_dve(e, s, 2 * D, D)
                resid2_dve(e, "rh", 1, 1.0)
            if on(6):
                for i, tag in enumerate(("a1", "b0")):
                    norm_dve(e, h, tag)
                    dense(f)
                    resid2_dve(e, "r" + tag, 2 + i, 0.5)
                norm_dve(e, h, "in_at")
                project_dve(e, s, D, QKV)
                every, raw_take = dil_every(e, ATT0[4])
                attn_dve(e, ATT0[4], A_ITEMS, None, every=every)
                raw_take(5)
                merge_dve(e, ATT0[4])
                cut_x(e, "cat_a", range(2), lambda b: f"att_a:oT{b}")
                project_dve(e, s, D // 2, D)
                resid2_dve(e, "rat", 4, 1.0)
                norm_dve(e, h, "b1")
                dense(f)
                resid2_dve(e, "rb1", 5, 0.5)
            e.link(nc.vector.tensor_copy(seed[:, 1:2], seed[:, 0:1]), "final")

        @block.tensor
        def _(pe):
            e = Engine(pe, "pe")
            s = Use(pe)
            f = FfnPe(pe, s)
            pe.sem_inc(sem("turned"), 1)
            setup_pe(e)
            mod_pe(e, s, 0, f)
            for st in range(2):
                norm_pe(e, f"in_e{st}")
                follow(e, s, f"in_e{st}")
                project_pe(e, s, [(xhi, xlo, KD)], 6 * N, f"in_e{st}", late_pe(e, s, 0, st))
            e.eng.wait_ge(sem("out_done"), e.outs.n)
            conv_pe(e, 0)
            even_qk_pe(e)
            for st in range(2):
                if st:
                    conv_pe(e, 1)

                def ready(e, i):
                    if st == 0 and i % NT == 0:
                        e.after(f"bias{i // NT}")
                attn_pe(e, ATT0[st], E_ITEMS[st], ready, "qkT1", f"convT{st}")
                heads_out_pe(e, f"att_e{st}")
                follow(e, s, f"cat_e{st}")
                project_pe(e, s, [(xhi, xlo, KD)], D, f"out_e{st}")
                resid_pe(e, f"res_e{st}", (pick_lat, pick_ctx)[st], 0)
            if on(2):
                for st in range(2):
                    norm_pe(e, f"ff{st}")
                    follow(e, s, f"ff{st}")
                    dense(f)
                    resid_pe(e, f"res_f{st}", (pick_lat, pick_ctx)[st], 1)
            if on(3):
                mod_pe(e, s, 1, f)
                for st, n in enumerate((OW, OW - OQ)):
                    norm_pe(e, f"in_o{st}")
                    follow(e, s, f"in_o{st}")
                    project_pe(e, s, [(xhi, xlo, KD)], n, f"in_o{st}", late_pe(e, s, 1, st))
                odd_qk_pe(e)
                attn_pe(e, ATT0[2], W_ITEMS, None, "ckT", "dkT")
                heads_out_pe(e, "att_w")
                attn_pe(e, ATT0[3], D_ITEMS, None, "att_w:oT")
                heads_out_pe(e, "att_d")
                follow(e, s, "cat_o")
                project_pe(e, s, [(xhi, xlo, KD)], D, "out_o")
                resid_pe(e, "res_o", pick_lat, 0)
            if on(4):
                norm_pe(e, "moe")
                e.after("moe:x")
                router_pe(e)
                experts(f)
                resid_pe(e, "res_m", pick_lat, 1)
            if on(5):
                norm_pe(e, "a0", "res_m:h")
                follow(e, s, "a0")
                dense(f)
                norm_pe(e, "in_h")
                e.after("in_h:x")
                head_pe(e)
                project_pe(e, s, [(xhi, xlo, KD)], HYB - SSM_H, "in_h")
                e.eng.wait_ge(sem("out_done"), e.outs.n)
                conf_pe(e)
                ssm_pe(e)
                norm_pe(e, "ssm")
                e.after("ssm:x")
                project_pe(e, s, [(xhi, xlo, KD), (R_G2["x2hi"], R_G2["x2lo"], KD)], D, "out_h")
            if on(6):
                for tag in ("a1", "b0"):
                    norm_pe(e, tag)
                    follow(e, s, tag)
                    dense(f)
                norm_pe(e, "in_at")
                follow(e, s, "in_at")
                project_pe(e, s, [(xhi, xlo, KD)], QKV, "in_at")
                dil_pe(e)
                attn_pe(e, ATT0[4], A_ITEMS, lambda e, i: e.after(f"raw{i // 8 - 2}") if i % 8 == 0 and i >= 16
                        else None, "dilqk2", "masks")
                heads_out_pe(e, "att_a")
                follow(e, s, "cat_a", 2)
                project_pe(e, s, [(xhi, xlo, KD // 2)], D, "out_a")
                norm_pe(e, "b1")
                follow(e, s, "b1")
                dense(f)


def kernel(**inputs):
    import concourse.bacc as bacc
    from concourse.bass_utils import run_bass_kernel_spmd as run

    arrays = {k: np.ascontiguousarray(v) for k, v in inputs.items()}
    arrays.update(constants())
    rows, width = TOK // 64, 64
    r, c = np.arange(rows), np.arange(width)
    dr = np.clip(np.arange(rows)[None, :] - r[:, None] + 7, 0, 14)
    dc = np.clip(c[None, :] - c[:, None] + 15, 0, 30)
    laid = arrays["ev_rpb"][0][:, dr[:, None, :, None], dc[None, :, None, :]]
    laid = laid.reshape(8, NT, P, TOK).transpose(0, 2, 1, 3)
    arrays["k_rpb"] = np.ascontiguousarray(laid.reshape(8, P, NT * TOK))

    def build(plan):
        nc = bacc.Bacc("TRN2", target_bir_lowering=False, num_devices=1)
        aps = {k: nc.dram_tensor(f"in_{k}", v.shape, mybir.dt.from_np(v.dtype), kind="ExternalInput").ap()
               for k, v in arrays.items()}
        o = nc.dram_tensor("out_0", (1, TOK, D), F32, kind="ExternalOutput").ap()
        program(nc, aps, o, plan)
        return nc

    plan = {"old": {}, "dry": True, "stop": STOP}
    build(plan)
    plan = {"old": plan["new"], "dry": False, "stop": STOP}
    nc = build(plan)
    res = run(nc, [{f"in_{k}": v for k, v in arrays.items()}], core_ids=[0])
    return res.results[0]["out_0"]
```
